# Optimizing a Trainium2 kernel written in Bass

```python
import math
import jax
import jax.numpy as jnp
from jax import lax
import numpy as np
import jax, jax.numpy as jnp

D_MODEL = 1024
BATCH = 1
SEQ = 512
DEPTH = 1

GRID_W = 64
CTX_LEN = 256
RMS_EPS = 1e-6

D_MIX = 2 * D_MODEL
HEAD_DIM = 64
SSD_WIDTH = D_MIX // 2
SSD_HEADS = SSD_WIDTH // HEAD_DIM
SSD_GROUPS = 4
SSD_HPG = SSD_HEADS // SSD_GROUPS
SSD_STATE = 128
SSD_CONV = 5
SSD_CHUNK = 128
SSD_CONV_DIM = SSD_WIDTH + 2 * SSD_GROUPS * SSD_STATE
HY_WIDTH = D_MIX - SSD_WIDTH
HY_HEADS = HY_WIDTH // HEAD_DIM
HY_ORDER = 2
HY_SHORT = 3
HY_EMB = 33
HY_BANDS = (HY_EMB - 1) // 2
HY_HIDDEN = 64
HY_TARGET = 1e-2
HY_FAST_DECAY = 0.3
HY_SLOW_DECAY = 1.5
HY_MAX_DECAY = math.log(HY_TARGET) / HY_FAST_DECAY
HY_MIN_DECAY = math.log(HY_TARGET) / HY_SLOW_DECAY
PEER_HEADS = 8
PEER_KEYS = 128
PEER_EXPERTS = PEER_KEYS * PEER_KEYS
PEER_TOPK = 16
PEER_DKEY = 256
PEER_BLOCK = 128
OFF_XBC = SSD_WIDTH
OFF_DT = OFF_XBC + SSD_CONV_DIM
OFF_HY = OFF_DT + 2 * SSD_HEADS
D_IN_PROJ = OFF_HY + (HY_ORDER + 1) * HY_WIDTH


def rmsnorm(x, g):
    xf = x.astype(jnp.float32)
    y = xf * lax.rsqrt(jnp.mean(xf * xf, axis=-1, keepdims=True) + RMS_EPS)
    return (y * g.astype(jnp.float32)).astype(x.dtype)

def group_rmsnorm(x, g, groups):
    shp = x.shape
    xg = x.reshape(shp[:-1] + (groups, shp[-1] // groups))
    return rmsnorm(xg, g.reshape(groups, shp[-1] // groups)).reshape(shp)

def modulate(x, shift, scale):
    return x * (1.0 + scale) + shift

def dwconv_centred(u, w, b):
    k = w.shape[0]
    y = lax.conv_general_dilated(u, w[:, None, :].astype(u.dtype), window_strides=(1,),
                                 padding=[(k // 2, k // 2)],
                                 dimension_numbers=('NWC', 'WIO', 'NWC'),
                                 feature_group_count=u.shape[-1])
    return y + b

def segsum(a):
    t = a.shape[-1]
    cs = jnp.cumsum(a, axis=-1)
    diff = cs[..., :, None] - cs[..., None, :]
    mask = jnp.tril(jnp.ones((t, t), dtype=bool))
    return jnp.where(mask, diff, -jnp.inf)

def ssd_scan(x, dt, a_head, b_mat, c_mat, h0):
    bsz, seqlen, g, r, p = x.shape
    n = b_mat.shape[-1]
    q = SSD_CHUNK
    nc = seqlen // q
    xdt = (x * dt[..., None]).reshape(bsz, nc, q, g, r, p)
    bc = b_mat.reshape(bsz, nc, q, g, n)
    cc = c_mat.reshape(bsz, nc, q, g, n)
    a = jnp.moveaxis((dt * a_head).reshape(bsz, nc, q, g, r), (3, 4), (1, 2))
    a_cum = jnp.cumsum(a, axis=-1)
    l_intra = jnp.exp(segsum(a))
    y_diag = jnp.einsum('bclgn,bcsgn,bgrcls,bcsgrp->bclgrp', cc, bc, l_intra, xdt)
    decay_to_end = jnp.exp(a_cum[..., -1:] - a_cum)
    states = jnp.einsum('bclgn,bgrcl,bclgrp->bcgrpn', bc, decay_to_end, xdt)
    states = jnp.concatenate([h0[:, None].astype(states.dtype), states], axis=1)
    chunk_a = jnp.pad(a_cum[..., -1], ((0, 0), (0, 0), (0, 0), (1, 0)))
    decay_chunk = jnp.exp(segsum(chunk_a))
    states = jnp.einsum('bgrzc,bcgrpn->bzgrpn', decay_chunk, states)
    prev_states, final_state = states[:, :-1], states[:, -1]
    y_off = jnp.einsum('bclgn,bcgrpn,bgrcl->bclgrp', cc, prev_states, jnp.exp(a_cum))
    y = (y_diag + y_off).reshape(bsz, seqlen, g, r, p)
    return y, final_state

def ssd_inputs(proj, conv_w, conv_b, dt_bias):
    bsz, l, _ = proj.shape
    z = proj[..., :OFF_XBC]
    xbc = jax.nn.silu(dwconv_centred(proj[..., OFF_XBC:OFF_DT], conv_w, conv_b))
    dt_raw = proj[..., OFF_DT:OFF_HY]
    xs = xbc[..., :SSD_WIDTH].reshape(bsz, l, SSD_GROUPS, SSD_HPG, HEAD_DIM)
    gn = SSD_GROUPS * SSD_STATE
    bm = xbc[..., SSD_WIDTH:SSD_WIDTH + gn].reshape(bsz, l, SSD_GROUPS, SSD_STATE)
    cm = xbc[..., SSD_WIDTH + gn:].reshape(bsz, l, SSD_GROUPS, SSD_STATE)
    dt_f = jax.nn.softplus(dt_raw[..., :SSD_HEADS] + dt_bias[0]).reshape(bsz, l, SSD_GROUPS, SSD_HPG)
    dt_b = jax.nn.softplus(dt_raw[..., SSD_HEADS:] + dt_bias[1]).reshape(bsz, l, SSD_GROUPS, SSD_HPG)
    return z, xs, bm, cm, dt_f, dt_b

def ssd_bidir(xs, bm, cm, dt_f, dt_b, a_f, a_b, h0_f, h0_b):
    y_f, s_f = ssd_scan(xs, dt_f, a_f, bm, cm, h0_f)
    fl = lambda t: jnp.flip(t, axis=1)
    y_b, s_b = ssd_scan(fl(xs), fl(dt_b), a_b, fl(bm), fl(cm), h0_b)
    return y_f + fl(y_b), s_f, s_b

def ssd_output(y, xs, z, d_skip, norm_g):
    bsz, l = y.shape[:2]
    y = (y + xs * d_skip.reshape(SSD_GROUPS, SSD_HPG)[:, :, None]).reshape(bsz, l, SSD_WIDTH)
    return group_rmsnorm(y * jax.nn.silu(z), norm_g, SSD_GROUPS)

def hyena_filters(seqlen, w1, b1, w2, b2, w3, sin_freq):
    f32 = jnp.float32
    t = jnp.linspace(0.0, 1.0, seqlen, dtype=f32)[:, None]
    w_ang = 2.0 * math.pi * jnp.arange(seqlen, dtype=f32) / seqlen
    bands = jnp.linspace(1e-4, HY_BANDS - 1, HY_BANDS, dtype=f32)
    ang = w_ang[:, None] * bands[None, :]
    zpos = jnp.concatenate([t, jnp.cos(ang), -jnp.sin(ang)], axis=-1)
    h = jnp.sin(sin_freq[0] * (zpos @ w1 + b1))
    h = jnp.sin(sin_freq[1] * (h @ w2 + b2))
    h = (h @ w3).astype(f32).reshape(seqlen, HY_ORDER, 2, HY_WIDTH)
    deltas = jnp.abs(jnp.linspace(HY_MIN_DECAY, HY_MAX_DECAY, HY_WIDTH, dtype=f32))
    h = h * jnp.exp(-t * deltas)[:, None, None, :]
    return jnp.moveaxis(h, 0, 2)

def long_conv_bidir(u, h_fwd, h_bwd, bias):
    seqlen = u.shape[1]
    k = jnp.concatenate([h_fwd, jnp.zeros_like(h_fwd[:1]), h_bwd[:0:-1]], axis=0)
    k_f = jnp.fft.rfft(k, axis=0)
    u_f = jnp.fft.rfft(u.astype(jnp.float32), n=2 * seqlen, axis=1)
    y = jnp.fft.irfft(u_f * k_f, n=2 * seqlen, axis=1)[:, :seqlen]
    return (y + u.astype(jnp.float32) * bias.astype(jnp.float32)).astype(u.dtype)

def raster_to_colmajor(u, rows):
    bsz, l, ch = u.shape
    return u.reshape(bsz, rows, GRID_W, ch).transpose(0, 2, 1, 3).reshape(bsz, l, ch)

def colmajor_to_raster(u, rows):
    bsz, l, ch = u.shape
    return u.reshape(bsz, GRID_W, rows, ch).transpose(0, 2, 1, 3).reshape(bsz, l, ch)

def hyena(proj_hy, short_w, short_b, filters, filt_bias, norm_g, rows):
    u = dwconv_centred(proj_hy, short_w, short_b)
    v, x1, x2 = jnp.split(u, 3, axis=-1)
    z = x1 * long_conv_bidir(v, filters[0, 0], filters[0, 1], filt_bias[0])
    if rows is None:
        z = long_conv_bidir(z, filters[1, 0], filters[1, 1], filt_bias[1])
    else:
        z = colmajor_to_raster(
            long_conv_bidir(raster_to_colmajor(z, rows), filters[1, 0], filters[1, 1], filt_bias[1]), rows)
    return group_rmsnorm(x2 * z, norm_g, HY_HEADS)

def peer(h, wq, subkeys, u_tab, v_tab):
    bsz, l, d = h.shape
    blocks = h.reshape(-1, PEER_BLOCK, d)

    def block(hb):
        q = (hb @ wq).reshape(PEER_BLOCK, PEER_HEADS, 2, PEER_DKEY // 2)
        s = jnp.einsum('thsd,snd->thsn', q, subkeys).astype(jnp.float32)
        s1, i1 = lax.top_k(s[:, :, 0], PEER_TOPK)
        s2, i2 = lax.top_k(s[:, :, 1], PEER_TOPK)
        cand = (s1[..., :, None] + s2[..., None, :]).reshape(PEER_BLOCK, PEER_HEADS, PEER_TOPK * PEER_TOPK)
        sc, ci = lax.top_k(cand, PEER_TOPK)
        e1 = jnp.take_along_axis(i1, ci // PEER_TOPK, axis=-1)
        e2 = jnp.take_along_axis(i2, ci % PEER_TOPK, axis=-1)
        idx = e1 * PEER_KEYS + e2
        gate = jax.nn.softmax(sc, axis=-1).astype(hb.dtype)
        u_sel = u_tab[idx]
        v_sel = v_tab[idx]
        act = jax.nn.gelu(jnp.einsum('td,thkd->thk', hb, u_sel), approximate=False) * gate
        return jnp.einsum('thk,thkd->td', act, v_sel)

    return lax.map(block, blocks).reshape(bsz, l, d)

def first_inputs(seed: int = 0) -> dict:
    key = jax.random.key(seed)
    ks = jax.random.split(key, 32)
    f32 = jnp.float32

    def nrm(k, shape, scale):
        return jax.random.normal(k, shape, f32) * scale

    def gain(k, shape):
        return 1.0 + 0.02 * jax.random.normal(k, shape, f32)

    dt0 = jnp.exp(jax.random.uniform(ks[9], (DEPTH, 2, SSD_HEADS), f32, math.log(1e-3), math.log(1e-1)))
    dt_bias = dt0 + jnp.log(-jnp.expm1(-dt0))
    a_log = jnp.log(jax.random.uniform(ks[8], (DEPTH, 2, SSD_HEADS), f32, 1.0, 16.0))
    return {
        'x': nrm(ks[0], (BATCH, SEQ, D_MODEL), 1.0),
        'c': nrm(ks[1], (BATCH, D_MODEL), 1.0),
        'ctx': nrm(ks[2], (BATCH, CTX_LEN, D_MODEL), 1.0),
        'c_ctx': nrm(ks[3], (D_MODEL,), 1.0),
        'w_mod': nrm(ks[4], (DEPTH, D_MODEL, 6 * D_MODEL), 0.5 * D_MODEL ** -0.5),
        'b_mod': nrm(ks[5], (DEPTH, 6 * D_MODEL), 0.02),
        'norm1': gain(ks[6], (DEPTH, D_MODEL)),
        'w_in': nrm(ks[7], (DEPTH, D_MODEL, D_IN_PROJ), D_MODEL ** -0.5),
        'ssd_conv_w': nrm(ks[10], (DEPTH, SSD_CONV, SSD_CONV_DIM), SSD_CONV ** -0.5),
        'ssd_conv_b': nrm(ks[11], (DEPTH, SSD_CONV_DIM), 0.02),
        'ssd_a_log': a_log,
        'ssd_dt_bias': dt_bias,
        'ssd_d': gain(ks[12], (DEPTH, SSD_HEADS)),
        'ssd_norm': gain(ks[13], (DEPTH, SSD_WIDTH)),
        'hy_short_w': nrm(ks[14], (DEPTH, HY_SHORT, (HY_ORDER + 1) * HY_WIDTH), HY_SHORT ** -0.5),
        'hy_short_b': nrm(ks[15], (DEPTH, (HY_ORDER + 1) * HY_WIDTH), 0.02),
        'hy_w1': nrm(ks[16], (DEPTH, HY_EMB, HY_HIDDEN), HY_EMB ** -0.5),
        'hy_b1': nrm(ks[17], (DEPTH, HY_HIDDEN), 0.02),
        'hy_w2': nrm(ks[18], (DEPTH, HY_HIDDEN, HY_HIDDEN), HY_HIDDEN ** -0.5),
        'hy_b2': nrm(ks[19], (DEPTH, HY_HIDDEN), 0.02),
        'hy_w3': nrm(ks[20], (DEPTH, HY_HIDDEN, HY_ORDER * 2 * HY_WIDTH), 0.05 * HY_HIDDEN ** -0.5),
        'hy_sin_freq': 1.0 + 0.1 * jax.random.normal(ks[21], (DEPTH, 2, HY_HIDDEN), f32),
        'hy_filt_bias': nrm(ks[22], (DEPTH, HY_ORDER, HY_WIDTH), 0.5),
        'hy_norm': gain(ks[23], (DEPTH, HY_WIDTH)),
        'w_out': nrm(ks[24], (DEPTH, D_MIX, D_MODEL), D_MIX ** -0.5),
        'norm2': gain(ks[25], (DEPTH, D_MODEL)),
        'peer_wq': nrm(ks[26], (DEPTH, D_MODEL, PEER_HEADS * PEER_DKEY), D_MODEL ** -0.5),
        'peer_subkeys': nrm(ks[27], (DEPTH, 2, PEER_KEYS, PEER_DKEY // 2), (PEER_DKEY // 2) ** -0.5),
        'peer_u': nrm(ks[28], (DEPTH, PEER_EXPERTS, D_MODEL), D_MODEL ** -0.5),
        'peer_v': nrm(ks[29], (DEPTH, PEER_EXPERTS, D_MODEL), 1.0),
        'final_norm': gain(ks[30], (D_MODEL,)),
    }

def first_block(x, c, ctx, c_ctx, w_mod, b_mod, norm1, w_in, ssd_conv_w, ssd_conv_b, ssd_a_log,
              ssd_dt_bias, ssd_d, ssd_norm, hy_short_w, hy_short_b, hy_w1, hy_b1, hy_w2, hy_b2,
              hy_w3, hy_sin_freq, hy_filt_bias, hy_norm, w_out, norm2, peer_wq, peer_subkeys,
              peer_u, peer_v, final_norm):
    rows = x.shape[1] // GRID_W
    h_lat = x
    h_ctx = ctx
    bsz = x.shape[0]
    for i in range(DEPTH):
        last = i == DEPTH - 1
        mod_l = (jax.nn.silu(c) @ w_mod[i] + b_mod[i])[:, None, :]
        mod_c = (jax.nn.silu(c_ctx) @ w_mod[i] + b_mod[i])[None, None, :]
        sh1_l, sc1_l, g1_l, sh2_l, sc2_l, g2_l = jnp.split(mod_l, 6, axis=-1)
        sh1_c, sc1_c, g1_c, sh2_c, sc2_c, g2_c = jnp.split(mod_c, 6, axis=-1)

        p_l = modulate(rmsnorm(h_lat, norm1[i]), sh1_l, sc1_l) @ w_in[i]
        p_c = modulate(rmsnorm(h_ctx, norm1[i]), sh1_c, sc1_c) @ w_in[i]

        a_f = -jnp.exp(ssd_a_log[i, 0]).reshape(SSD_GROUPS, SSD_HPG)
        a_b = -jnp.exp(ssd_a_log[i, 1]).reshape(SSD_GROUPS, SSD_HPG)
        z_c, xs_c, b_c, c_c, dtf_c, dtb_c = ssd_inputs(p_c, ssd_conv_w[i], ssd_conv_b[i], ssd_dt_bias[i])
        z_l, xs_l, b_l, c_l, dtf_l, dtb_l = ssd_inputs(p_l, ssd_conv_w[i], ssd_conv_b[i], ssd_dt_bias[i])
        h0 = jnp.zeros((bsz, SSD_GROUPS, SSD_HPG, HEAD_DIM, SSD_STATE), dtype=xs_c.dtype)
        y_c, s_f, s_b = ssd_bidir(xs_c, b_c, c_c, dtf_c, dtb_c, a_f, a_b, h0, h0)
        y_l, _, _ = ssd_bidir(xs_l, b_l, c_l, dtf_l, dtb_l, a_f, a_b, s_f, s_b)
        o_ssd_l = ssd_output(y_l, xs_l, z_l, ssd_d[i], ssd_norm[i])

        filt_l = hyena_filters(h_lat.shape[1], hy_w1[i], hy_b1[i], hy_w2[i], hy_b2[i], hy_w3[i], hy_sin_freq[i])
        o_hy_l = hyena(p_l[..., OFF_HY:], hy_short_w[i], hy_short_b[i], filt_l, hy_filt_bias[i], hy_norm[i], rows)

        mix_l = jnp.concatenate([o_ssd_l, o_hy_l], axis=-1) @ w_out[i]
        h_lat = h_lat + g1_l * mix_l

        f_l = modulate(rmsnorm(h_lat, norm2[i]), sh2_l, sc2_l)
        h_lat = h_lat + g2_l * peer(f_l, peer_wq[i], peer_subkeys[i], peer_u[i], peer_v[i])

        if not last:
            o_ssd_c = ssd_output(y_c, xs_c, z_c, ssd_d[i], ssd_norm[i])
            filt_c = hyena_filters(h_ctx.shape[1], hy_w1[i], hy_b1[i], hy_w2[i], hy_b2[i], hy_w3[i], hy_sin_freq[i])
            o_hy_c = hyena(p_c[..., OFF_HY:], hy_short_w[i], hy_short_b[i], filt_c, hy_filt_bias[i], hy_norm[i], None)
            h_ctx = h_ctx + g1_c * (jnp.concatenate([o_ssd_c, o_hy_c], axis=-1) @ w_out[i])
            f_c = modulate(rmsnorm(h_ctx, norm2[i]), sh2_c, sc2_c)
            h_ctx = h_ctx + g2_c * peer(f_c, peer_wq[i], peer_subkeys[i], peer_u[i], peer_v[i])
    return rmsnorm(h_lat, final_norm)


DEPTH_2 = 2

ROPE_THETA = 10000.0
Q_BLOCK = 128

MLA_HEADS = 8
MLA_Q_RANK = 256
MLA_KV_RANK = 128
MLA_NOPE = 64
MLA_ROPE = 32
MLA_V = 64
SWA_HEADS = 8
SWA_KV_HEADS = 2
SWA_GROUP = SWA_HEADS // SWA_KV_HEADS
WINDOW = 128
DIFF_HEADS = D_MODEL // (2 * HEAD_DIM)
D_FF = 2816

ALPHA = (2 * DEPTH_2) ** 0.25
BETA = (8 * DEPTH_2) ** -0.25
LN_EPS = 1e-5
NEG_INF = -1e30
N_EVEN = (DEPTH_2 + 1) // 2
N_ODD = DEPTH_2 // 2

EVEN_Q_SIZES = (MLA_Q_RANK, SWA_HEADS * HEAD_DIM)
EVEN_KV_SIZES = (MLA_KV_RANK, MLA_ROPE, SWA_KV_HEADS * HEAD_DIM, SWA_KV_HEADS * HEAD_DIM)
EVEN_Q_COLS = sum(EVEN_Q_SIZES)
EVEN_IN = EVEN_Q_COLS + sum(EVEN_KV_SIZES)
EVEN_OUT = MLA_HEADS * MLA_V + SWA_HEADS * HEAD_DIM
DIFF_QK_COLS = DIFF_HEADS * 2 * HEAD_DIM
ODD_IN = 3 * DIFF_QK_COLS
ODD_OUT = DIFF_HEADS * 2 * HEAD_DIM


def layer_norm(x, g, b):
    xf = x.astype(jnp.float32)
    mu = jnp.mean(xf, -1, keepdims=True)
    var = jnp.mean(jnp.square(xf - mu), -1, keepdims=True)
    return ((xf - mu) * lax.rsqrt(var + LN_EPS) * g + b).astype(x.dtype)

def rms_norm(x, g):
    xf = x.astype(jnp.float32)
    return (xf * lax.rsqrt(jnp.mean(jnp.square(xf), -1, keepdims=True) + RMS_EPS) * g).astype(x.dtype)

def split_cols(t, sizes):
    idx = np.cumsum(np.array(sizes))[:-1].tolist()
    return jnp.split(t, idx, axis=-1)

def axial_rope_tables(rows, dim):
    row = jnp.repeat(jnp.arange(rows), GRID_W).astype(jnp.float32)
    col = jnp.tile(jnp.arange(GRID_W), rows).astype(jnp.float32)
    quarter = dim // 4
    freqs = ROPE_THETA ** (-jnp.arange(quarter, dtype=jnp.float32) / quarter)
    ar = row[:, None] * freqs
    ac = col[:, None] * freqs
    cos = jnp.concatenate([jnp.cos(ar), jnp.cos(ar), jnp.cos(ac), jnp.cos(ac)], -1)
    sin = jnp.concatenate([jnp.sin(ar), jnp.sin(ar), jnp.sin(ac), jnp.sin(ac)], -1)
    return cos, sin

def apply_rope(x, cos, sin):
    shape = (cos.shape[0],) + (1,) * (x.ndim - 3) + (cos.shape[1],)
    cos = cos.reshape(shape)
    sin = sin.reshape(shape)
    a, b, c_, d = jnp.split(x, 4, axis=-1)
    rot = jnp.concatenate([-b, a, -d, c_], -1)
    return (x * cos + rot * sin).astype(x.dtype)

def sweep_query_blocks(fn, q):
    B, S = q.shape[:2]
    nb = S // Q_BLOCK
    blocks = jnp.moveaxis(q.reshape((B, nb, Q_BLOCK) + q.shape[2:]), 1, 0)
    out = jnp.moveaxis(lax.map(fn, blocks), 0, 1)
    return out.reshape((B, S) + out.shape[3:])

def softmax_attend(q, k, v, scale):
    s = jnp.einsum('bqhd,bkhd->bhqk', q, k).astype(jnp.float32) * scale
    p = jax.nn.softmax(s, axis=-1).astype(v.dtype)
    return jnp.einsum('bhqk,bkhd->bqhd', p, v)

def mla_queries(q_a, q_norm, w_qb, cos, sin):
    B, T = q_a.shape[:2]
    q = (rms_norm(q_a, q_norm) @ w_qb).reshape(B, T, MLA_HEADS, MLA_NOPE + MLA_ROPE)
    if cos is None:
        return q
    return jnp.concatenate([q[..., :MLA_NOPE], apply_rope(q[..., MLA_NOPE:], cos, sin)], -1)

def mla_keys_values(kv_a, k_rope, kv_norm, w_kvb, cos, sin):
    B, T = kv_a.shape[:2]
    kv = (rms_norm(kv_a, kv_norm) @ w_kvb).reshape(B, T, MLA_HEADS, MLA_NOPE + MLA_V)
    if cos is not None:
        k_rope = apply_rope(k_rope, cos, sin)
    k_rope = jnp.broadcast_to(k_rope[:, :, None, :], (B, T, MLA_HEADS, MLA_ROPE))
    return jnp.concatenate([kv[..., :MLA_NOPE], k_rope], -1), kv[..., MLA_NOPE:]

def window_attend(q, k, v, k_ctx, v_ctx, sink):
    B, S = q.shape[:2]
    L = k_ctx.shape[1]
    nb = S // WINDOW
    qb = q.reshape(B, nb, WINDOW, SWA_KV_HEADS, SWA_GROUP, HEAD_DIM)

    def band(t):
        tb = t.reshape(B, nb, WINDOW, SWA_KV_HEADS, HEAD_DIM)
        tp = jnp.pad(tb, ((0, 0), (1, 1), (0, 0), (0, 0), (0, 0)))
        return jnp.concatenate([tp[:, :-2], tp[:, 1:-1], tp[:, 2:]], axis=2)

    kb, vb = band(k), band(v)
    qpos = jnp.arange(nb)[:, None] * WINDOW + jnp.arange(WINDOW)[None, :]
    kpos = (jnp.arange(nb)[:, None] - 1) * WINDOW + jnp.arange(3 * WINDOW)[None, :]
    valid = ((jnp.abs(qpos[:, :, None] - kpos[:, None, :]) <= WINDOW)
             & (kpos[:, None, :] >= 0) & (kpos[:, None, :] < S))
    scale = HEAD_DIM ** -0.5
    s_band = jnp.einsum('bnqhgd,bnkhd->bnhgqk', qb, kb).astype(jnp.float32) * scale
    s_band = jnp.where(valid[None, :, None, None], s_band, NEG_INF)
    s_ctx = jnp.einsum('bnqhgd,bchd->bnhgqc', qb, k_ctx).astype(jnp.float32) * scale
    sink_col = jnp.broadcast_to(sink.reshape(SWA_KV_HEADS, SWA_GROUP, 1, 1).astype(jnp.float32),
                                s_ctx.shape[:-1] + (1,))
    p = jax.nn.softmax(jnp.concatenate([s_ctx, s_band, sink_col], -1), axis=-1)
    p_ctx = p[..., :L].astype(v.dtype)
    p_band = p[..., L:L + 3 * WINDOW].astype(v.dtype)
    o = (jnp.einsum('bnhgqc,bchd->bnqhgd', p_ctx, v_ctx)
         + jnp.einsum('bnhgqk,bnkhd->bnqhgd', p_band, vb))
    return o.reshape(B, S, SWA_HEADS * HEAD_DIM)

def sink_attend(q, k, v, sink):
    B, T = q.shape[:2]
    qg = q.reshape(B, T, SWA_KV_HEADS, SWA_GROUP, HEAD_DIM)
    s = jnp.einsum('bqhgd,bkhd->bhgqk', qg, k).astype(jnp.float32) * HEAD_DIM ** -0.5
    sink_col = jnp.broadcast_to(sink.reshape(SWA_KV_HEADS, SWA_GROUP, 1, 1).astype(jnp.float32),
                                s.shape[:-1] + (1,))
    p = jax.nn.softmax(jnp.concatenate([s, sink_col], -1), axis=-1)[..., :-1].astype(v.dtype)
    return jnp.einsum('bhgqk,bkhd->bqhgd', p, v).reshape(B, T, SWA_HEADS * HEAD_DIM)

def even_mixer(h_lat, h_ctx, w_in, q_norm, w_qb, kv_norm, w_kvb, sink, w_out, rope32, rope64, need_ctx):
    B, S = h_lat.shape[:2]
    L = h_ctx.shape[1]
    cos32, sin32 = rope32
    cos64, sin64 = rope64
    qa_l, qs_l, kva_l, kr_l, ks_l, vs_l = split_cols(h_lat @ w_in, EVEN_Q_SIZES + EVEN_KV_SIZES)
    kva_c, kr_c, ks_c, vs_c = split_cols(h_ctx @ w_in[:, EVEN_Q_COLS:], EVEN_KV_SIZES)
    mla_scale = (MLA_NOPE + MLA_ROPE) ** -0.5
    q_mla = mla_queries(qa_l, q_norm, w_qb, cos32, sin32)
    k_mla_l, v_mla_l = mla_keys_values(kva_l, kr_l, kv_norm, w_kvb, cos32, sin32)
    k_mla_c, v_mla_c = mla_keys_values(kva_c, kr_c, kv_norm, w_kvb, None, None)
    k_all = jnp.concatenate([k_mla_c, k_mla_l], axis=1)
    v_all = jnp.concatenate([v_mla_c, v_mla_l], axis=1)
    o_mla = sweep_query_blocks(lambda qb: softmax_attend(qb, k_all, v_all, mla_scale), q_mla)
    o_mla = o_mla.reshape(B, S, MLA_HEADS * MLA_V)
    q_swa = apply_rope(qs_l.reshape(B, S, SWA_HEADS, HEAD_DIM), cos64, sin64)
    k_swa = apply_rope(ks_l.reshape(B, S, SWA_KV_HEADS, HEAD_DIM), cos64, sin64)
    v_swa = vs_l.reshape(B, S, SWA_KV_HEADS, HEAD_DIM)
    k_swa_c = ks_c.reshape(B, L, SWA_KV_HEADS, HEAD_DIM)
    v_swa_c = vs_c.reshape(B, L, SWA_KV_HEADS, HEAD_DIM)
    o_swa = window_attend(q_swa, k_swa, v_swa, k_swa_c, v_swa_c, sink)
    out_l = jnp.concatenate([o_mla, o_swa], -1) @ w_out
    if not need_ctx:
        return out_l, None
    qa_c, qs_c = split_cols(h_ctx @ w_in[:, :EVEN_Q_COLS], EVEN_Q_SIZES)
    q_mla_c = mla_queries(qa_c, q_norm, w_qb, None, None)
    o_mla_c = softmax_attend(q_mla_c, k_mla_c, v_mla_c, mla_scale).reshape(B, L, MLA_HEADS * MLA_V)
    o_swa_c = sink_attend(qs_c.reshape(B, L, SWA_HEADS, HEAD_DIM), k_swa_c, v_swa_c, sink)
    out_c = jnp.concatenate([o_mla_c, o_swa_c], -1) @ w_out
    return out_l, out_c

def diff_attend(q, k, v, lam, lambda_init, subln_g):
    s = jnp.einsum('bqhtd,bkhtd->bthqk', q, k).astype(jnp.float32) * HEAD_DIM ** -0.5
    p = jax.nn.softmax(s, axis=-1)
    a = (p[:, 0] - lam * p[:, 1]).astype(v.dtype)
    o = jnp.einsum('bhqk,bkhe->bqhe', a, v)
    o = rms_norm(o, subln_g) * (1.0 - lambda_init)
    return o.reshape(o.shape[0], o.shape[1], DIFF_HEADS * 2 * HEAD_DIM)

def odd_mixer(h_lat, h_ctx, w_in, lam_q1, lam_k1, lam_q2, lam_k2, subln_g, w_out, rope64,
              lambda_init, need_ctx):
    B, S = h_lat.shape[:2]
    L = h_ctx.shape[1]
    cos, sin = rope64
    q_l, k_l, v_l = jnp.split(h_lat @ w_in, 3, axis=-1)
    q_l = apply_rope(q_l.reshape(B, S, DIFF_HEADS, 2, HEAD_DIM), cos, sin)
    k_l = apply_rope(k_l.reshape(B, S, DIFF_HEADS, 2, HEAD_DIM), cos, sin)
    v_l = v_l.reshape(B, S, DIFF_HEADS, 2 * HEAD_DIM)
    k_c, v_c = jnp.split(h_ctx @ w_in[:, DIFF_QK_COLS:], 2, axis=-1)
    k_c = k_c.reshape(B, L, DIFF_HEADS, 2, HEAD_DIM)
    v_c = v_c.reshape(B, L, DIFF_HEADS, 2 * HEAD_DIM)
    lam = (jnp.exp(jnp.sum(lam_q1 * lam_k1).astype(jnp.float32))
           - jnp.exp(jnp.sum(lam_q2 * lam_k2).astype(jnp.float32)) + lambda_init)
    k_all = jnp.concatenate([k_c, k_l], axis=1)
    v_all = jnp.concatenate([v_c, v_l], axis=1)
    o_l = sweep_query_blocks(lambda qb: diff_attend(qb, k_all, v_all, lam, lambda_init, subln_g), q_l)
    out_l = o_l @ w_out
    if not need_ctx:
        return out_l, None
    q_c = (h_ctx @ w_in[:, :DIFF_QK_COLS]).reshape(B, L, DIFF_HEADS, 2, HEAD_DIM)
    out_c = diff_attend(q_c, k_c, v_c, lam, lambda_init, subln_g) @ w_out
    return out_l, out_c

def conv_ffn(h, w_gate, w_up, conv_w, conv_b, w_down):
    g = h @ w_gate
    gp = jnp.pad(g, ((0, 0), (1, 1), (0, 0)))
    g = gp[:, :-2] * conv_w[0] + gp[:, 1:-1] * conv_w[1] + gp[:, 2:] * conv_w[2] + conv_b
    return (jax.nn.silu(g) * (h @ w_up)) @ w_down

def modulation(cond, w_mod, b_mod):
    return jnp.split(jax.nn.silu(cond) @ w_mod + b_mod, 6, axis=-1)

def second_inputs(seed: int = 0) -> dict:
    key = jax.random.key(seed)
    ks = iter(jax.random.split(key, 40))

    def nrm(shape, scale):
        return jax.random.normal(next(ks), shape, jnp.float32) * scale

    def gain(shape):
        return 1.0 + nrm(shape, 0.01)

    D, F = D_MODEL, D_FF
    return {
        "x": nrm((BATCH, SEQ, D), 1.0),
        "c": nrm((BATCH, D), 1.0),
        "ctx": nrm((BATCH, CTX_LEN, D), 1.0),
        "c_ctx": nrm((D,), 1.0),
        "w_mod": nrm((DEPTH_2, D, 6 * D), 0.5 * D ** -0.5),
        "b_mod": nrm((DEPTH_2, 6 * D), 0.01),
        "ln1_g": gain((DEPTH_2, D)),
        "ln1_b": nrm((DEPTH_2, D), 0.01),
        "ln2_g": gain((DEPTH_2, D)),
        "ln2_b": nrm((DEPTH_2, D), 0.01),
        "ffn_w_gate": nrm((DEPTH_2, D, F), D ** -0.5),
        "ffn_w_up": nrm((DEPTH_2, D, F), D ** -0.5),
        "ffn_conv_w": nrm((DEPTH_2, 3, F), 3 ** -0.5),
        "ffn_conv_b": nrm((DEPTH_2, F), 0.01),
        "ffn_w_down": nrm((DEPTH_2, F, D), BETA * F ** -0.5),
        "ab_w_in": nrm((N_EVEN, D, EVEN_IN), D ** -0.5),
        "mla_q_norm": gain((N_EVEN, MLA_Q_RANK)),
        "mla_w_qb": nrm((N_EVEN, MLA_Q_RANK, MLA_HEADS * (MLA_NOPE + MLA_ROPE)), MLA_Q_RANK ** -0.5),
        "mla_kv_norm": gain((N_EVEN, MLA_KV_RANK)),
        "mla_w_kvb": nrm((N_EVEN, MLA_KV_RANK, MLA_HEADS * (MLA_NOPE + MLA_V)), MLA_KV_RANK ** -0.5),
        "swa_sink": nrm((N_EVEN, SWA_HEADS), 0.5),
        "ab_w_out": nrm((N_EVEN, EVEN_OUT, D), BETA * EVEN_OUT ** -0.5),
        "diff_w_in": nrm((N_ODD, D, ODD_IN), D ** -0.5),
        "diff_lam_q1": nrm((N_ODD, HEAD_DIM), 0.1),
        "diff_lam_k1": nrm((N_ODD, HEAD_DIM), 0.1),
        "diff_lam_q2": nrm((N_ODD, HEAD_DIM), 0.1),
        "diff_lam_k2": nrm((N_ODD, HEAD_DIM), 0.1),
        "diff_subln_g": gain((N_ODD, 2 * HEAD_DIM)),
        "diff_w_out": nrm((N_ODD, ODD_OUT, D), BETA * ODD_OUT ** -0.5),
    }

def second_block(x, c, ctx, c_ctx, w_mod, b_mod, ln1_g, ln1_b, ln2_g, ln2_b,
              ffn_w_gate, ffn_w_up, ffn_conv_w, ffn_conv_b, ffn_w_down,
              ab_w_in, mla_q_norm, mla_w_qb, mla_kv_norm, mla_w_kvb, swa_sink, ab_w_out,
              diff_w_in, diff_lam_q1, diff_lam_k1, diff_lam_q2, diff_lam_k2, diff_subln_g, diff_w_out):
    S = x.shape[1]
    ROWS = S // GRID_W
    rope32 = axial_rope_tables(ROWS, MLA_ROPE)
    rope64 = axial_rope_tables(ROWS, HEAD_DIM)
    xl, xc = x, ctx
    for i in range(DEPTH_2):
        need_ctx = i < DEPTH_2 - 1
        j = i // 2
        sh1_l, sc1_l, gt1_l, sh2_l, sc2_l, gt2_l = [t[:, None, :] for t in modulation(c, w_mod[i], b_mod[i])]
        sh1_c, sc1_c, gt1_c, sh2_c, sc2_c, gt2_c = modulation(c_ctx, w_mod[i], b_mod[i])
        h_l = xl * (1.0 + sc1_l) + sh1_l
        h_c = xc * (1.0 + sc1_c) + sh1_c
        if i % 2 == 0:
            o_l, o_c = even_mixer(h_l, h_c, ab_w_in[j], mla_q_norm[j], mla_w_qb[j], mla_kv_norm[j],
                                  mla_w_kvb[j], swa_sink[j], ab_w_out[j], rope32, rope64, need_ctx)
        else:
            lambda_init = 0.8 - 0.6 * math.exp(-0.3 * i)
            o_l, o_c = odd_mixer(h_l, h_c, diff_w_in[j], diff_lam_q1[j], diff_lam_k1[j], diff_lam_q2[j],
                                 diff_lam_k2[j], diff_subln_g[j], diff_w_out[j], rope64, lambda_init, need_ctx)
        xl = layer_norm(ALPHA * xl + gt1_l * o_l, ln1_g[i], ln1_b[i])
        h_l = xl * (1.0 + sc2_l) + sh2_l
        f_l = conv_ffn(h_l, ffn_w_gate[i], ffn_w_up[i], ffn_conv_w[i], ffn_conv_b[i], ffn_w_down[i])
        xl = layer_norm(ALPHA * xl + gt2_l * f_l, ln2_g[i], ln2_b[i])
        if need_ctx:
            xc = layer_norm(ALPHA * xc + gt1_c * o_c, ln1_g[i], ln1_b[i])
            h_c = xc * (1.0 + sc2_c) + sh2_c
            f_c = conv_ffn(h_c, ffn_w_gate[i], ffn_w_up[i], ffn_conv_w[i], ffn_conv_b[i], ffn_w_down[i])
            xc = layer_norm(ALPHA * xc + gt2_c * f_c, ln2_g[i], ln2_b[i])
    return xl


def setup_inputs(seed=0):
    out = dict(first_inputs(seed))
    for name, value in second_inputs(seed + 1).items():
        if name != "x":
            out[name + "_2"] = value
    return out


def reference(
    x, c, ctx, c_ctx, w_mod, b_mod, norm1, w_in, ssd_conv_w, ssd_conv_b, ssd_a_log, ssd_dt_bias,
    ssd_d, ssd_norm, hy_short_w, hy_short_b, hy_w1, hy_b1, hy_w2, hy_b2, hy_w3, hy_sin_freq,
    hy_filt_bias, hy_norm, w_out, norm2, peer_wq, peer_subkeys, peer_u, peer_v, final_norm, c_2,
    ctx_2, c_ctx_2, w_mod_2, b_mod_2, ln1_g_2, ln1_b_2, ln2_g_2, ln2_b_2, ffn_w_gate_2,
    ffn_w_up_2, ffn_conv_w_2, ffn_conv_b_2, ffn_w_down_2, ab_w_in_2, mla_q_norm_2, mla_w_qb_2,
    mla_kv_norm_2, mla_w_kvb_2, swa_sink_2, ab_w_out_2, diff_w_in_2, diff_lam_q1_2,
    diff_lam_k1_2, diff_lam_q2_2, diff_lam_k2_2, diff_subln_g_2, diff_w_out_2,
):
    x = first_block(
        x, c, ctx, c_ctx, w_mod, b_mod, norm1, w_in, ssd_conv_w, ssd_conv_b, ssd_a_log,
        ssd_dt_bias, ssd_d, ssd_norm, hy_short_w, hy_short_b, hy_w1, hy_b1, hy_w2, hy_b2, hy_w3,
        hy_sin_freq, hy_filt_bias, hy_norm, w_out, norm2, peer_wq, peer_subkeys, peer_u, peer_v,
        final_norm,
    )
    return second_block(
        x, c_2, ctx_2, c_ctx_2, w_mod_2, b_mod_2, ln1_g_2, ln1_b_2, ln2_g_2, ln2_b_2,
        ffn_w_gate_2, ffn_w_up_2, ffn_conv_w_2, ffn_conv_b_2, ffn_w_down_2, ab_w_in_2,
        mla_q_norm_2, mla_w_qb_2, mla_kv_norm_2, mla_w_kvb_2, swa_sink_2, ab_w_out_2,
        diff_w_in_2, diff_lam_q1_2, diff_lam_k1_2, diff_lam_q2_2, diff_lam_k2_2, diff_subln_g_2,
        diff_w_out_2,
    )


_drawn_inputs = setup_inputs


def setup_inputs(seed=0):
    import zlib

    import numpy as np

    out = dict(_drawn_inputs(seed))
    spreads = {}
    factors = {'ctx': 3.095,
     'norm1': 2.821,
     'ssd_conv_b': 3.69,
     'ssd_d': 8.0,
     'ssd_norm': 4.584,
     'hy_b1': 3.011,
     'hy_norm': 4.807,
     'final_norm': 2.749,
     'ctx_2': 3.59,
     'b_mod_2': 8.0,
     'ln1_g_2': 11.782,
     'ln1_b_2': 12.63,
     'ln2_g_2': 11.363,
     'ln2_b_2': 13.233,
     'ffn_conv_b_2': 38.386,
     'mla_q_norm_2': 8.0,
     'mla_w_qb_2': 7.876,
     'mla_kv_norm_2': 8.0,
     'mla_w_kvb_2': 2.805,
     'swa_sink_2': 64.0,
     'diff_lam_q1_2': 2.905,
     'diff_lam_k1_2': 5.572,
     'diff_lam_q2_2': 8.0,
     'diff_lam_k2_2': 8.0,
     'diff_subln_g_2': 64.0}
    for name, (base, spread) in spreads.items():
        noise = np.random.default_rng([zlib.crc32(name.encode()), seed]).standard_normal(out[name].shape)
        drawn = base * np.exp(spread * noise) if base else spread * noise
        out[name] = jnp.asarray(drawn.astype(out[name].dtype))
    for name, factor in factors.items():
        out[name] = (out[name] * factor).astype(out[name].dtype)
    return out
```

```python
import math
from contextlib import ExitStack

import numpy as np

import concourse.bass as bass
from concourse import mybir

F = mybir.dt.float32
U32 = mybir.dt.uint32
ALU = mybir.AluOpType
AF = mybir.ActivationFunctionType
AX = mybir.AxisListType.X

L, C, T = 512, 256, 768
EPS = 1e-6
LN_EPS = 1e-5
ALPHA = 4.0 ** 0.25
NEG = -1e30
LOW = -3e38
LAMBDA_INIT = 0.8 - 0.6 * math.exp(-0.3)

SQ = ["ident", "ones", "le", "ge", "gt", "lt", "m256", "m1024", "m64", "m128", "iota", "r96", "r128",
      "bandlo", "bandhi"]
VECS = [("norm1", 8), ("convw", 80), ("convb", 16), ("ssd_norm", 8), ("hyw", 72), ("hyb", 24), ("hbias", 16),
        ("hy_norm", 8), ("norm2", 8), ("final_norm", 8), ("bmod", 48), ("dtb", 1), ("hyb1", 1), ("hyb2", 1),
        ("fr0", 1), ("fr1", 1), ("ln1g", 16), ("ln1b", 16), ("ln2g", 16), ("ln2b", 16), ("fcw", 132),
        ("fcb", 44), ("bmod2", 96), ("qn", 2), ("kvn", 1), ("subln", 1), ("c1", 16), ("c2", 16)]
ROWS = [("alog", 32), ("dskip", 16), ("sink", 8), ("lq1", 64), ("lk1", 64), ("lq2", 64), ("lk2", 64), ("i16", 16)]


class Queue:

    def __init__(self, sem):
        self.sem, self.n, self.ops, self.seen = sem, 0, [], {}

    def wait(self, *toks):
        for t in toks:
            if t is None:
                continue
            if isinstance(t, list):
                self.wait(*t)
                continue
            sem, v = t
            if self.seen.get(id(sem), 0) < v:
                self.seen[id(sem)] = v
                self.ops.append((None, sem, v))

    def do(self, fn, *toks):
        self.wait(*toks)
        self.n += 1
        self.ops.append((fn, self.sem, 1))
        return (self.sem, self.n)

    def quiet(self, fn, *toks):
        self.wait(*toks)
        self.ops.append((fn, None, 0))

    def dma(self, out, in_, sem, *toks):
        self.wait(*toks)
        sem[1] += 16
        self.ops.append((lambda e: e.dma_start(out, in_), sem[0], 16))
        return (sem[0], sem[1])

    def last(self):
        return (self.sem, self.n) if self.n else None

    def run(self, e):
        for fn, sem, v in self.ops:
            if fn is None:
                e.wait_ge(sem, v)
            else:
                i = fn(e)
                if sem is not None:
                    i.then_inc(sem, v)


class Arena:

    def __init__(self, ap, size):
        self.ap, self.size, self.at, self.top = ap, size, 0, 0

    def take(self, n):
        a = self.at
        self.at += n
        self.top = max(self.top, self.at)
        assert self.at <= self.size, (self.at, self.size)
        return self.ap[:, a:a + n]


class Banks:

    def __init__(self, ap):
        self.ap, self.at, self.rel = ap, 0, [[] for _ in range(8)]

    def take(self, n=1):
        for i in range(8):
            b = (self.at + i) % 8
            if b % n == 0 and all(self.rel[j] is not None for j in range(b, b + n)):
                break
        else:
            assert False, "no bank is free"
        self.at = b + n
        toks = []
        for i in range(b, b + n):
            toks += self.rel[i]
            self.rel[i] = None
        return self.ap[:, 512 * b:512 * (b + n)], range(b, b + n), toks

    def free(self, banks, *toks):
        for i in banks:
            self.rel[i] = list(toks)


class Ring:

    def __init__(self, ap, n, sems, sp):
        self.ap, self.n, self.sems, self.sp, self.at = ap, n, sems, sp, 0
        self.rel = [[] for _ in range(n)]

    def take(self, src, cols=1024, *toks, parts=128):
        s = self.at % self.n
        self.at += 1
        assert self.rel[s] is not None, "slot not given back"
        out = self.ap[0:parts, 1024 * s:1024 * s + cols]
        t = self.sp.dma(out, src, self.sems[s], self.rel[s], *toks)
        self.rel[s] = None
        return out, t, s

    def free(self, s, *toks):
        self.rel[s] = list(toks)


def v3(ap, b):
    return ap.rearrange("p (a b) -> p a b", b=b)


def v4(ap, b, c):
    return ap.rearrange("p (a b c) -> p a b c", b=b, c=c)


def bc(ap, axis, shape):
    return ap.unsqueeze(axis).to_broadcast(shape)


class Core:
    def __init__(self, nc, d, ctx):
        self.nc, self.d = nc, d
        sem = lambda n: ctx.enter_context(nc.semaphore(n))
        self.sem = sem
        self.pe, self.dve, self.act = Queue(sem("s_pe")), Queue(sem("s_dve")), Queue(sem("s_act"))
        self.pool, self.sp = Queue(sem("s_pool")), Queue(sem("s_sp"))
        sb = ctx.enter_context(nc.sbuf_tensor("arena", [128, 39296], F))
        rg = ctx.enter_context(nc.sbuf_tensor("ring", [128, 13312], F))
        self.ar = Arena(sb, 39296)
        ps = ctx.enter_context(nc.psum_tensor("psum", [128, 4096], F))
        self.ps = Banks(ps)
        self.ring = Ring(rg, 13, [[sem(f"s_r{i}"), 0] for i in range(13)], self.sp)
        self.nsem = 0
        self.floor = []

    def dsem(self):
        self.nsem += 1
        return [self.sem(f"s_d{self.nsem}"), 0]

    def fence(self):
        toks = [q.last() for q in (self.pe, self.dve, self.act, self.pool)]
        for q in (self.pe, self.dve, self.act, self.pool):
            q.wait(toks)
        self.floor = toks

    def load(self, out, src, *toks):
        return self.pool.dma(out, src, self.dsem(), self.floor, *toks)

    def mm(self, out, pairs, *toks, start=True, stop=True, mark=True):
        self.pe.wait(*toks)
        n = len(pairs)
        for i, (l, r) in enumerate(pairs):
            s0, s1 = start and i == 0, stop and i == n - 1
            f = lambda e, l=l, r=r, s0=s0, s1=s1: e.matmul(out, l, r, start=s0, stop=s1, skip_group_check=True)
            if mark and i == n - 1:
                return self.pe.do(f)
            self.pe.quiet(f)

    def tr(self, out, in_, *toks, mark=True):
        k = in_.shape[0]
        p0 = in_.start_partition if not callable(in_.start_partition) else in_.start_partition()
        ident = self.sq["ident"][p0:p0 + k, p0:p0 + k]
        f = lambda e: e.transpose(out, in_, ident)
        return self.pe.do(f, *toks) if mark else self.pe.quiet(f, *toks)

    def tt(self, out, a, b, op, *toks, q=None):
        return (q or self.dve).do(lambda e: e.tensor_tensor(out, a, b, op), *toks)

    def ts(self, out, a, s1, s2, op0, op1, *toks, q=None):
        if op1 is None:
            return (q or self.dve).do(lambda e: e.tensor_scalar(out, a, s1, None, op0), *toks)
        return (q or self.dve).do(lambda e: e.tensor_scalar(out, a, s1, s2, op0, op1), *toks)

    def stt(self, out, a, s, b, op0, op1, *toks):
        return self.dve.do(lambda e: e.scalar_tensor_tensor(out=out, in0=a, scalar=s, in1=b, op0=op0, op1=op1), *toks)

    def cp(self, out, a, *toks, q=None):
        return (q or self.dve).do(lambda e: e.tensor_copy(out, a), *toks)

    def red(self, out, a, op, *toks):
        return self.dve.do(lambda e: e.tensor_reduce(out, a, AX, op), *toks)

    def rec(self, out, a, *toks):
        return self.dve.do(lambda e: e.reciprocal(out, a), *toks)

    def zero(self, out, *toks, q=None):
        return (q or self.pool).do(lambda e: e.memset(out, 0.0), *toks)

    def ac(self, out, a, func, *toks, scale=1.0, bias=None, accum=None):
        def f(e):
            kw = {}
            if bias is not None:
                kw["bias"] = bias
            if accum is not None:
                kw["accum_out"] = accum
            return e.activation(out, a, func, scale=scale, **kw)
        return self.act.do(f, *toks)

    def acp(self, out, a, *toks):
        return self.act.do(lambda e: e.copy(out, a), *toks)

    def proj(self, units, rhs, segs, M=128, toks=(), p0=0):
        got = [self.ring.take(u, w) for u, w in units]
        out = []
        for a, b in segs:
            bank, ids, rel = self.ps.take()
            pairs = []
            for ui, (w, _, _) in enumerate(got):
                m = M
                nk = units[ui][1] // m
                pairs += [(w[:, k * m:(k + 1) * m], rhs(8 * ui + k, a, b)) for k in range(nk)]
            t = self.mm(bank[p0:p0 + M, 0:b - a], pairs, [g[1] for g in got], rel, *toks)
            out.append((bank, ids, t))
        for g in got:
            self.ring.free(g[2], out[-1][2])
        return out

    def rms(self, src, n, out, tmp, mean, eps, segs, *toks):
        banks = [self.ps.take() for _ in segs]
        t = None
        free = [self.pe.last()] * 2
        for k in range(n):
            s = tmp[k % 2]
            t = self.act.do(lambda e, s=s, x=src(k): e.square(s, x), free[k % 2], *toks)
            for i, (a, b) in enumerate(segs):
                f = lambda e, i=i, a=a, b=b, s=s, k=k: e.matmul(banks[i][0][:, 0:b - a], mean, s[:, a:b],
                                                               start=(k == 0), stop=(k == n - 1), skip_group_check=True)
                free[k % 2] = self.pe.do(f, t, banks[i][2])
        r = []
        for i, (a, b) in enumerate(segs):
            o = out[:, a:b]
            u = self.ts(o, banks[i][0][:, 0:b - a], eps, None, ALU.add, None, free[(n - 1) % 2])
            self.ps.free(banks[i][1], u)
            u = self.ac(o, o, AF.Sqrt, u)
            u = self.rec(o, o, u)
            r.append(u)
        return r

    def setup(self):
        d, ar = self.d, self.ar
        nsq, nv, nr = len(SQ), sum(n for _, n in VECS), sum(n for _, n in ROWS)
        a = ar.take(nsq * 128)
        b = ar.take(nv)
        c = ar.take(nr)
        self.t_const = [self.load(a, d["squares"]), self.load(b, d["vecs"]), self.load(c, d["rows"])]
        for q in (self.pe, self.dve, self.act, self.pool):
            q.wait(self.t_const)
        self.sq = {n: a[:, 128 * i:128 * i + 128] for i, n in enumerate(SQ)}
        self.vec, self.row = {}, {}
        at = 0
        for n, w in VECS:
            self.vec[n] = b[:, at:at + w]
            at += w
        at = 0
        for n, w in ROWS:
            self.row[n] = c[:, at:at + w]
            at += w
        self.mods = [(ar.take(16), ar.take(96)) for _ in range(3)]
        self.gain_l, self.gain_c = ar.take(8), ar.take(8)
        self.base = ar.at

    def modulation(self, cname, wname, i0, bias, n=0):
        cs, mod = self.mods[n]
        t = self.ac(cs, self.vec[cname], AF.Silu)
        bank, ids, rel = self.ps.take()
        for j in range(48):
            w, tw, s = self.ring.take(self.d[wname][i0 + j])
            tm = self.mm(bank[:, 2 * j:2 * j + 2], [(w[:, 128 * k:128 * k + 128], cs[:, 2 * k:2 * k + 2])
                                                    for k in range(8)], tw, t, rel)
            self.ring.free(s, tm)
        m3 = v3(mod, 2)
        t = self.tt(m3, v3(bank[:, 0:96], 2), bc(bias, 2, [128, 48, 2]), ALU.add, tm)
        self.ps.free(ids, t)
        return m3, t

    def gains(self, out, mod, t, j0, g, s):
        return self.stt(out, mod[:, j0:j0 + 8, s], 1.0, g, ALU.add, ALU.mult, t)

    def in_projection(self):
        d, ar, V, S = self.d, self.ar, self.vec, self.sq
        m, tm = self.modulation("c1", "wmod", 0, V["bmod"])
        self.mod1 = m
        gl, gc = self.gain_l, self.gain_c
        tg = [self.gains(gl, m, tm, 8, V["norm1"], 0), self.gains(gc, m, tm, 8, V["norm1"], 1)]
        ar.at = self.base
        fT = ar.take(4096)
        zT = ar.take(4096)
        xl = ar.take(4096)
        BT, CT = ar.take(2048), ar.take(2048)
        self.small = ar.take(1600)
        self.Sprev = ar.take(8192)
        self.rest = ar.at
        xc, Btok = ar.take(2048), ar.take(3072)
        fc = self.Sprev[:, 0:2048]
        sqt = [self.Sprev[:, 2048 + 768 * i:2816 + 768 * i] for i in range(2)]
        rstd = self.Sprev[:, 3584:4352]
        raws = [self.Sprev[:, 4352 + 776 * i:5128 + 776 * i] for i in range(2)]
        accs = [self.Sprev[:, 5904 + 768 * i:6672 + 768 * i] for i in range(2)]
        sil = [ar.take(768) for i in range(2)]
        f3, c3 = v3(fT, 512), v3(fc, 256)
        th = [self.load(f3, d["xT"]), self.load(c3, d["ctxT"])]
        tz = [self.zero(r) for r in raws]

        for lo, hi, src, g, s in ((0, 512, f3, gl, 0), (512, 768, c3, gc, 1)):
            r = self.rms(lambda k: src[:, k, :], 8, rstd[:, lo:hi], [q[:, 0:hi - lo] for q in sqt], S["m1024"], EPS,
                         [(0, hi - lo)], th)
            for k in range(8):
                t = self.tt(src[:, k, :], src[:, k, :], rstd[:, lo:hi], ALU.mult, r, th)
                t = self.ac(src[:, k, :], src[:, k, :], AF.Identity, t, tg, scale=g[:, k:k + 1], bias=m[:, k, s:s + 1])
        tf = self.act.last()
        self.fT, self.tf = f3, tf
        seg2, seg1 = [(0, 512), (512, 768)], [(0, 512)]
        rhs = lambda k, a, b: f3[:, k, :] if a == 0 else c3[:, k, :]

        z3 = v3(zT, 512)
        for j in range(8):
            (bank, ids, t), = self.proj([(d["win"][j], 1024)], rhs, seg1, toks=(tf,))
            t = self.ac(z3[:, j, :], bank, AF.Silu, t)
            self.ps.free(ids, t)

        xl3, xc3, B3, C3, Bt3 = v3(xl, 1024), v3(xc, 1024), v3(BT, 512), v3(CT, 512), v3(Btok, 512)
        tr_free = [None, None]
        raw_free, acc_free = [[tz], [tz]], [[], []]
        for j in range(16):
            i = j % 2
            raw, acc, si = raws[i], accs[i], sil[i]
            segs = seg2 if j < 12 else seg1
            got = self.proj([(d["win"][8 + j], 1024)], rhs, segs, toks=(tf,))
            tc = []
            for (bank, ids, t), off, n in zip(got, (2, 518), (512, 256)):
                t = self.acp(raw[:, off:off + n], bank[:, 0:n], t, raw_free[i])
                self.ps.free(ids, t)
                tc.append(t)
            w = V["convw"][:, 5 * j:5 * j + 5]
            last = []
            for lo, n, base in ((0, 512, 0), (512, 256, 516))[:len(segs)]:
                a = acc[:, lo:lo + n]
                t = self.ts(a, raw[:, base:base + n], w[:, 0:1], V["convb"][:, j:j + 1], ALU.mult, ALU.add,
                            tc, acc_free[i])
                for k in range(1, 5):
                    t = self.stt(a, raw[:, base + k:base + k + n], w[:, k:k + 1], a, ALU.mult, ALU.add, t)
                last.append(t)
            raw_free[i] = last
            if j >= 12:
                acc_free[i] = [self.ac(C3[:, j - 12, :], acc[:, 0:512], AF.Silu, last)]
                continue
            if j < 8:
                t = self.ac(si, acc, AF.Silu, last, tr_free[i])
                acc_free[i], lat = [t], si[:, 0:512]
            else:
                t = self.ac(B3[:, j - 8, :], acc[:, 0:512], AF.Silu, last)
                t = self.ac(si[:, 512:768], acc[:, 512:768], AF.Silu, t, tr_free[i])
                acc_free[i], lat = [t], B3[:, j - 8, :]
            bank, ids, rel = self.ps.take(2)
            for q in range(6):
                src = lat[:, 128 * q:128 * q + 128] if q < 4 else si[:, 128 * q:128 * q + 128]
                t2 = self.tr(bank[:, 128 * q:128 * q + 128], src, t, rel, mark=(q == 5))
            tr_free[i] = [t2]
            if j < 8:
                c0 = slice(128 * j, 128 * j + 128)
                u = [self.cp(xl3[:, :, c0], v3(bank[:, 0:512], 128), t2), self.cp(xc3[:, :, c0], v3(bank[:, 512:768], 128), t2)]
            else:
                c0 = slice(128 * (j - 8), 128 * (j - 8) + 128)
                u = [self.cp(Bt3[:, :, c0], v3(bank[:, 0:768], 128), t2)]
            self.ps.free(ids, u)

        sm = self.small
        dtT = sil[0][0:32, :]
        got = self.proj([(d["wdt"], 256)], rhs, seg2, M=32, toks=(tf,))
        t2 = []
        for (bank, ids, t), (a, b) in zip(got, seg2):
            u = self.ts(dtT[:, a:b], bank[0:32, 0:b - a], V["dtb"][0:32, :], None, ALU.add, None, t, tr_free[0])
            self.ps.free(ids, u)
            t2.append(u)
        bank, ids, rel = self.ps.take()
        for q in range(6):
            t = self.tr(bank[:, 32 * q:32 * q + 32], dtT[:, 128 * q:128 * q + 128], t2, rel)
        x, e, s, q, p, dt, a, A = (sm[:, 192 * i:192 * i + 192] for i in range(8))
        t = self.cp(x, bank[:, 0:192], t)
        self.ps.free(ids, t)
        t = self.stt(e, x, -1.0, x, ALU.mult, ALU.max, t)
        t = self.ac(e, e, AF.Exp, t, scale=-1.0)
        t = self.ts(s, e, 2.0, None, ALU.add, None, t)
        t = self.rec(s, s, t)
        t = self.tt(s, s, e, ALU.mult, t)
        t = self.tt(q, s, s, ALU.mult, t)
        t = self.ts(p, q, 1.0 / 17, None, ALU.mult, None, t)
        for n in (15, 13, 11, 9, 7, 5, 3):
            t = self.stt(p, p, 1.0 / n, q, ALU.add, ALU.mult, t)
        t = self.stt(p, p, 1.0, s, ALU.add, ALU.mult, t)
        t = self.ts(x, x, 0.0, None, ALU.max, None, t)
        t = self.stt(dt, p, 2.0, x, ALU.mult, ALU.add, t)
        A = A[:, 0:32]
        u = self.ac(A, self.row["alog"], AF.Exp)
        u = self.ts(A, A, -1.0, None, ALU.mult, None, u)
        t = self.tt(v3(a, 32), v3(dt, 32), bc(A, 1, [128, 6, 32]), ALU.mult, t, u)
        self.dt, self.a = v3(dt, 32), v3(a, 32)
        self.zT, self.xl, self.xc, self.BT, self.CT, self.Btok = z3, xl3, xc3, B3, C3, Bt3
        return t

    def ssd(self):
        V, S, ar, sm = self.vec, self.sq, self.ar, self.small
        self.fence()
        dt, a = self.dt, self.a
        E = sm[:, 0:576]
        wd = sm[:, 576:768]
        b0, i0, r0 = self.ps.take()
        b1, i1, r1 = self.ps.take()
        masks = ["le", "ge", "gt", "lt", "ones", "ones"]
        for n, mk in enumerate(masks):
            o = b0[:, 96 * n:96 * n + 96] if n < 5 else b1[:, 0:96]
            t = self.mm(o, [(S[mk], a[:, :, 16 * (n % 2):16 * (n % 2) + 16])], r0, r1)
        u = [self.ac(E[:, 0:480], b0[:, 0:480], AF.Exp, t), self.ac(E[:, 480:576], b1[:, 0:96], AF.Exp, t)]
        self.ps.free(i0, u)
        self.ps.free(i1, u)
        E5 = E.rearrange("p (k d c h) -> p k d c h", k=3, d=2, c=6)
        wd4 = wd.rearrange("p (d c h) -> p d c h", d=2, c=6)
        tw = []
        for k in range(2):
            tw.append(self.tt(wd4[:, k], dt[:, :, 16 * k:16 * k + 16], E5[:, 1, k], ALU.mult, u))
        ar.at = self.rest + 5120
        xws = [ar.take(1024) for _ in range(2)]
        Sp = self.Sprev.rearrange("p (d c n) -> p d c n", d=2, c=4)
        xw_free = [None, None]
        n = 0
        t_s = []
        for k, order in ((0, (4, 5, 0, 1, 2)), (1, (5, 4, 3, 2, 1))):
            prev, cur, tp = None, (0 if k == 0 else 3), None
            for step, c in enumerate(order):
                xw = xws[n % 2]
                xs = self.xl[:, c, :] if c < 4 else self.xc[:, c - 4, :]
                t = self.tt(v3(xw, 64), v3(xs, 64), bc(wd4[:, k, c], 2, [128, 16, 64]), ALU.mult, tw, xw_free[n % 2],
                            q=self.pool)
                bank, ids, rel = self.ps.take(2)
                for g in range(4):
                    t2 = self.mm(bank[:, 256 * g:256 * g + 256],
                                 [(self.Btok[:, c, 128 * g:128 * g + 128], xw[:, 256 * g:256 * g + 256])], t, rel,
                                 mark=(g == 3))
                xw_free[n % 2] = t2
                n += 1
                if step >= 2:
                    prev, cur = cur, cur + (1 if k == 0 else -1)
                else:
                    prev = cur
                dst = Sp[:, k, cur, :]
                if step == 0:
                    tp = self.cp(dst, bank, t2)
                else:
                    tp = self.tt(v3(dst, 64), v3(Sp[:, k, prev, :], 64), bc(E5[:, 2, k, c], 2, [128, 16, 64]), ALU.mult,
                                 tp, u)
                    tp = self.tt(dst, dst, bank, ALU.add, tp, t2)
                self.ps.free(ids, tp)
            t_s.append(tp)
        self.fence()
        ar.at = self.rest
        CB = [ar.take(512) for _ in range(2)]
        xd = [ar.take(1024) for _ in range(2)]
        aL = [ar.take(512) for _ in range(2)]
        M = [ar.take(512) for _ in range(4)]
        ys = [ar.take(1024) for _ in range(2)]
        tmp = ar.take(1024)
        aL_free, M_free, y_free = [None] * 2, [None] * 4, [None] * 2
        mk = [("le", "gt", "le"), ("ge", "lt", "ge")]
        t_xd, t_y, t_z = None, None, None
        for c in range(4):
            cs = slice(128 * c, 128 * c + 128)
            bank, ids, rel = self.ps.take()
            for g in range(4):
                t = self.mm(bank[:, 128 * g:128 * g + 128], [(self.BT[:, g, cs], self.CT[:, g, cs])], rel, mark=(g == 3))
            tcb = [self.tt(v3(CB[k], 128), v3(bank, 128), bc(S[mk[k][0]], 1, [128, 4, 128]), ALU.mult, t, M_free)
                   for k in range(2)]
            self.ps.free(ids, tcb)
            txd = [self.tt(v3(xd[k], 64), v3(self.xl[:, c, :], 64), bc(dt[:, c, 16 * k:16 * k + 16], 2, [128, 16, 64]),
                           ALU.mult, t_xd, q=self.pool) for k in range(2)]
            y = ys[c % 2]
            offs = []
            for k in range(2):
                bank, ids, rel = self.ps.take(2)
                for g in range(4):
                    t = self.mm(bank[:, 256 * g:256 * g + 256], [(self.CT[:, g, cs], Sp[:, k, c, 256 * g:256 * g + 256])],
                                rel, mark=(g == 3))
                offs.append((bank, ids, t))
            (bf, idf, tf), (bb, idb, tb) = offs
            ty = self.tt(v3(y, 64), v3(bf, 64), bc(E5[:, 0, 0, c], 2, [128, 16, 64]), ALU.mult, tf, y_free[c % 2])
            self.ps.free(idf, ty)
            tt2 = self.tt(v3(tmp, 64), v3(bb, 64), bc(E5[:, 0, 1, c], 2, [128, 16, 64]), ALU.mult, tb, t_y)
            self.ps.free(idb, tt2)
            ty = self.tt(y, y, tmp, ALU.add, ty, tt2)
            tt2 = self.tt(v3(tmp, 64), v3(self.xl[:, c, :], 64), bc(self.row["dskip"], 2, [128, 16, 64]), ALU.mult, ty)
            ty = self.tt(y, y, tmp, ALU.add, tt2)
            t_y = ty
            yb, idy, rely = self.ps.take(2)
            for g in range(4):
                tms = []
                for k in range(2):
                    h0 = 16 * k + 4 * g
                    t = self.tt(v3(aL[k], 128), bc(S[mk[k][1]], 1, [128, 4, 128]), bc(a[:, c, h0:h0 + 4], 2, [128, 4, 128]),
                                ALU.mult, aL_free[k], q=self.pool)
                    bank, ids, rel = self.ps.take()
                    for h in range(4):
                        t2 = self.mm(bank[:, 128 * h:128 * h + 128], [(aL[k][:, 128 * h:128 * h + 128], S[mk[k][2]])], t, rel,
                                     mark=(h == 3))
                    aL_free[k] = t2
                    mi = 2 * (g % 2) + k
                    t = self.ac(M[mi], bank, AF.Exp, t2, M_free[mi])
                    self.ps.free(ids, t)
                    tms.append(self.tt(v3(M[mi], 128), v3(M[mi], 128), bc(CB[k][:, 128 * g:128 * g + 128], 1, [128, 4, 128]),
                                       ALU.mult, t, tcb))
                for h in range(4):
                    o = slice(256 * g + 64 * h, 256 * g + 64 * h + 64)
                    t = self.mm(yb[:, o], [(M[2 * (g % 2) + k][:, 128 * h:128 * h + 128], xd[k][:, o]) for k in range(2)],
                                tms, txd, rely, mark=(h == 3))
                M_free[2 * (g % 2)] = M_free[2 * (g % 2) + 1] = t
            t_xd = t
            ty = self.tt(y, y, yb, ALU.add, t, ty)
            self.ps.free(idy, ty)
            for i in range(2):
                bank, ids, rel = self.ps.take()
                for q in range(4):
                    f = 4 * i + q
                    t = self.tr(bank[:, 128 * q:128 * q + 128], y[:, 128 * f:128 * f + 128], ty, rel, mark=(q == 3))
                z = self.zT[:, 4 * i:4 * i + 4, cs]
                u = self.tt(z, z, v3(bank, 128), ALU.mult, t)
                self.ps.free(ids, u)
            y_free[c % 2] = t
        for g in range(4):
            sq = [tmp[:, 0:512], tmp[:, 512:1024]]
            r = self.rms(lambda k: self.zT[:, 2 * g + k, :], 2, M[g], sq, S["m256"], EPS, [(0, 512)], u, self.dve.last(),
                         self.pe.last())
            for k in range(2):
                z = self.zT[:, 2 * g + k, :]
                u = self.stt(z, z, V["ssd_norm"][:, 2 * g + k:2 * g + k + 1], M[g], ALU.mult, ALU.mult, r)
        return u

    def hyena(self):
        d, ar, V, S = self.d, self.ar, self.vec, self.sq
        self.fence()
        ar.at = self.base + 8192
        vT, x1, x2 = ar.take(4096), ar.take(4096), ar.take(4096)
        Cm, Sm = ar.take(2048), ar.take(2048)
        IS0, NY = ar.take(512), ar.take(512)
        top = ar.at
        raws = [ar.take(516) for _ in range(2)]
        accs = [ar.take(512) for _ in range(2)]
        C3, S3 = v3(Cm, 512), v3(Sm, 512)
        tdft = [self.load(C3, d["dftc"]), self.load(S3, d["dfts"]), self.load(IS0, d["is0"]), self.load(v3(NY, 128), d["nyq"])]
        tz = [self.zero(r, *self.floor) for r in raws]
        dst = [v3(q, 512) for q in (vT, x1, x2)]
        v, x1, x2 = dst
        raw_free = [tz, tz]
        rhs = lambda k, a, b: self.fT[:, k, :]
        for j in range(24):
            i = j % 2
            (bank, ids, t), = self.proj([(d["win"][24 + j], 1024)], rhs, [(0, 512)])
            t = self.acp(raws[i][:, 2:514], bank, t, raw_free[i])
            self.ps.free(ids, t)
            w = V["hyw"][:, 3 * j:3 * j + 3]
            o = dst[j // 8][:, j % 8, :]
            t = self.ts(accs[i], raws[i][:, 1:513], w[:, 0:1], V["hyb"][:, j:j + 1], ALU.mult, ALU.add, t)
            t = self.stt(accs[i], raws[i][:, 2:514], w[:, 1:2], accs[i], ALU.mult, ALU.add, t)
            t = self.stt(o, raws[i][:, 3:515], w[:, 2:3], accs[i], ALU.mult, ALU.add, t)
            raw_free[i] = [t]
        self.fence()
        ar.at = top
        h1, h2 = ar.take(512), ar.take(512)
        e, o = v3(ar.take(2048), 512), v3(ar.take(2048), 512)
        Kr, Ki = v3(ar.take(2048), 512), v3(ar.take(2048), 512)
        at2 = ar.at
        ar.at = self.base
        ut = v3(ar.take(2048), 512)
        P, Q = ar.take(512), ar.take(512)
        W = [ar.take(512) for _ in range(2)]
        ar.at = at2
        W += [ar.take(512) for _ in range(2)]
        zp, tzp, sz = self.ring.take(d["zpos"], 512, parts=33)
        w12, tw, sw = self.ring.take(d["hyw12"], 128, parts=64)

        def sine(out, bank, t, b, fr):
            t = self.ts(h1[0:64, :], bank[0:64, :], b[0:64, :], fr[0:64, :], ALU.add, ALU.mult, t)
            t = self.ts(P[0:64, :], h1[0:64, :], 1.0 / (2 * math.pi), 12582912.0, ALU.mult, ALU.add, t)
            t = self.ts(P[0:64, :], P[0:64, :], 12582912.0, None, ALU.subtract, None, t)
            for cst in (6.28125, 0.0019340515136718750, 2 * math.pi - 6.28125 - 0.0019340515136718750):
                t = self.stt(h1[0:64, :], P[0:64, :], -cst, h1[0:64, :], ALU.mult, ALU.add, t)
            t = self.ts(h1[0:64, :], h1[0:64, :], 3.1415925, -3.1415925, ALU.min, ALU.max, t)
            return self.ac(out[0:64, :], h1[0:64, :], AF.Sin, t)

        bank, ids, rel = self.ps.take()
        t = self.mm(bank[0:64, :], [(w12[0:33, 0:64], zp)], tzp, tw, rel)
        self.ring.free(sz, t)
        t = sine(h2, bank, t, V["hyb1"], V["fr0"])
        self.ps.free(ids, self.dve.last())
        bank, ids, rel = self.ps.take()
        t = self.mm(bank[0:64, :], [(w12[0:64, 64:128], h2[0:64, :])], t, rel)
        self.ring.free(sw, t)
        th2 = sine(h2, bank, t, V["hyb2"], V["fr1"])
        self.ps.free(ids, self.dve.last())
        self.pe.wait(tdft)

        K_free, e_free, u_free = [None], [None], [None]
        for hf in range(2):
            for od in range(2):
                w3, tw3, s3 = self.ring.take(d["hyw3"][od, hf], parts=64)
                decs = [self.ring.take(d["dec"][hf, i]) for i in range(2)]
                tPQ = [self.pool.last()]
                for tt in range(4):
                    dec = decs[tt // 2]
                    dm = dec[0][:, 512 * (tt % 2):512 * (tt % 2) + 512]
                    tp = []
                    for buf, c0 in ((P, 0), (Q, 512)):
                        bank, ids, rel = self.ps.take()
                        t = self.mm(bank, [(h2[0:64, 128 * tt:128 * tt + 128], w3[:, c0:c0 + 512])], tw3, th2, rel)
                        u = self.tt(buf, bank, dm, ALU.mult, t, dec[1], tPQ)
                        self.ps.free(ids, u)
                        tp.append(u)
                    if tt == 0:
                        tp.append(self.zero(Q[0:1, :], tp, q=self.dve))
                    tPQ = [self.tt(e[:, tt, :], P, Q, ALU.add, tp, e_free, q=self.pool),
                           self.tt(o[:, tt, :], P, Q, ALU.subtract, tp, e_free, q=self.pool)]
                self.ring.free(s3, t)
                for i in range(2):
                    self.ring.free(decs[i][2], u)
                tk = []
                for ft in range(4):
                    fs = slice(128 * ft, 128 * ft + 128)
                    for Kx, Mx, x in ((Kr, C3, e), (Ki, S3, o)):
                        bank, ids, rel = self.ps.take()
                        pairs = [(Mx[:, tt, fs], x[:, tt, :]) for tt in range(4)]
                        if Kx is Ki and ft == 0:
                            pairs += [(NY[:, 128 * tt:128 * tt + 128], e[:, tt, :]) for tt in range(4)]
                        t = self.mm(bank, pairs, tPQ, rel)
                        u = self.act.do(lambda q, o_=Kx[:, ft, :], b_=bank: q.mul(o_, b_, 2.0 / 1024), t, K_free)
                        self.ps.free(ids, u)
                        if ft == 0:
                            u = self.ts(Kx[0:1, 0, :], Kx[0:1, 0, :], 0.5, None, ALU.mult, None, u)
                        tk.append(u)
                te = self.pe.last()
                tu = []
                for tt in range(4):
                    bank, ids, rel = self.ps.take()
                    for j in range(4):
                        src = v[:, 4 * hf + j, 128 * tt:128 * tt + 128]
                        t = self.tr(bank[:, 128 * j:128 * j + 128], src, rel, tu_in if od else None, mark=(j == 3))
                    u = self.acp(ut[:, tt, :], bank, t, u_free)
                    self.ps.free(ids, u)
                    tu.append(u)
                ty = []
                for ft in range(4):
                    fs = slice(128 * ft, 128 * ft + 128)
                    br, idr, rr = self.ps.take()
                    t1 = self.mm(br, [(C3[:, tt, fs], ut[:, tt, :]) for tt in range(4)], tu, rr)
                    bi, idi, ri = self.ps.take()
                    pairs = [(S3[:, tt, fs], ut[:, tt, :]) for tt in range(4)]
                    if ft == 0:
                        pairs += [(NY[:, 128 * tt:128 * tt + 128], ut[:, tt, :]) for tt in range(4)]
                    t2 = self.mm(bi, pairs, ri)
                    a1 = self.tt(W[0], br, Kr[:, ft, :], ALU.mult, t1, tk, ty, self.pool.last())
                    a2 = self.tt(W[1], bi, Ki[:, ft, :], ALU.mult, t2)
                    a3 = self.tt(W[2], br, Ki[:, ft, :], ALU.mult)
                    a4 = self.tt(W[3], bi, Kr[:, ft, :], ALU.mult)
                    self.ps.free(idr, a3)
                    self.ps.free(idi, a4)
                    y1 = self.tt(e[:, ft, :], W[0], W[1], ALU.subtract, a4, te, q=self.pool)
                    y2 = self.tt(o[:, ft, :], W[2], W[3], ALU.add, a4, q=self.pool)
                    if ft == 0:
                        y1 = self.cp(e[0:1, 0, :], W[0][0:1, :], y1, y2)
                        y2 = self.cp(o[0:1, 0, :], W[1][0:1, :], y1, y2)
                    ty += [y1, y2]
                K_free = [self.dve.last()]
                u_free = [t2]
                outs = []
                for j in range(4):
                    bank, ids, rel = self.ps.take()
                    js = slice(128 * j, 128 * j + 128)
                    pairs = [(e[:, ft, js], C3[:, ft, :]) for ft in range(4)]
                    pairs += [(o[:, ft, js], S3[:, ft, :] if ft else IS0) for ft in range(4)]
                    t = self.mm(bank, pairs, ty, rel)
                    m = 4 * hf + j
                    hb = V["hbias"][:, 8 * od + m:8 * od + m + 1]
                    turned = v[:, m, :].rearrange("p (c r) -> p r c", r=8)
                    if od == 0:
                        u = self.stt(W[j], v[:, m, :], hb, bank, ALU.mult, ALU.add, t)
                        self.ps.free(ids, u)
                        outs.append(self.tt(turned, v3(W[j], 64), v3(x1[:, m, :], 64), ALU.mult, u))
                    else:
                        u = self.stt(v[:, m, :], v[:, m, :], hb, bank, ALU.mult, ALU.add, t)
                        self.ps.free(ids, u)
                        outs.append(self.tt(v3(x2[:, m, :], 64), v3(x2[:, m, :], 64), turned, ALU.mult, u))
                e_free = [t]
                tu_in = outs
        for m in range(8):
            sq = [W[0], W[1]]
            r = self.rms(lambda k: x2[:, m, :], 1, P if m % 2 else Q, [sq[m % 2]] * 2, S["m64"], EPS, [(0, 512)],
                         self.dve.last(), self.pe.last())
            z = x2[:, m, :]
            u = self.stt(z, z, V["hy_norm"][:, m:m + 1], P if m % 2 else Q, ALU.mult, ALU.mult, r)
        self.x2 = x2
        return u

    def out_projection(self, t):
        d, ar = self.d, self.ar
        self.fence()
        ar.at = self.base
        keep = ar.at
        ar.at = self.base + 8192
        h = v3(ar.take(4096), 512)
        th = self.load(h, d["xT"])
        for j in range(8):
            rhs = lambda k, a, b: self.zT[:, k, :] if k < 8 else self.x2[:, k - 8, :]
            (bank, ids, t), = self.proj([(d["wout"][j, i], 1024) for i in range(2)], rhs, [(0, 512)])
            t = self.stt(h[:, j, :], bank, self.mod1[:, 16 + j, 0:1], h[:, j, :], ALU.mult, ALU.add, t, th)
            self.ps.free(ids, t)
        self.h = h
        return t

    def peer(self, t):
        d, ar, V, S = self.d, self.ar, self.vec, self.sq
        m, h = self.mod1, self.h
        self.fence()
        ar.at = self.base
        f = v3(ar.take(4096), 512)
        sqt = [ar.take(512) for _ in range(2)]
        rstd, g2 = ar.take(512), ar.take(8)
        tg = self.gains(g2, m, None, 32, V["norm2"], 0)
        assert ar.at <= self.base + 8192
        ar.at = self.base + 12288
        low = ar.at
        r = self.rms(lambda k: h[:, k, :], 8, rstd, sqt, S["m1024"], EPS, [(0, 512)], t)
        for k in range(8):
            t = self.tt(f[:, k, :], h[:, k, :], rstd, ALU.mult, r)
            t = self.ac(f[:, k, :], f[:, k, :], AF.Identity, t, tg, scale=g2[:, k:k + 1], bias=m[:, 24 + k, 0:1])
        tf = t
        EG = [ar.take(512) for _ in range(3)]
        sc = v3(ar.take(8192), 2048)
        qs = [ar.take(512) for _ in range(2)]
        at1 = ar.at
        kt = ar.take(256)
        tk = self.load(kt, d["subkeys"])
        q_free = [None, None]
        tsc = []
        for n in range(16):
            (bank, ids, t), = self.proj([(d["wq"][n], 1024)], lambda k, a, b: f[:, k, :], [(0, 512)], toks=(tf,))
            t = self.acp(qs[n % 2], bank, t, q_free[n % 2])
            self.ps.free(ids, t)
            bank, ids, rel = self.ps.take()
            for tt in range(4):
                t2 = self.mm(bank[:, 128 * tt:128 * tt + 128],
                             [(qs[n % 2][:, 128 * tt:128 * tt + 128], kt[:, 128 * (n % 2):128 * (n % 2) + 128])], t, tk, rel,
                             mark=(tt == 3))
            q_free[n % 2] = t2
            u = self.cp(sc[:, :, 128 * n:128 * n + 128], v3(bank, 128), t2)
            self.ps.free(ids, u)
            tsc.append(u)
        val, idx = ar.take(256), ar.take(256).bitcast(U32)
        fidx, cand = ar.take(256), ar.take(2048)
        s2 = ar.take(256)
        best, ci, hi, hf = ar.take(128), ar.take(128).bitcast(U32), ar.take(128).bitcast(U32), ar.take(128)
        mx, oh = ar.take(8), ar.take(2048)
        esel, gate = ar.take(256), ar.take(128)
        D = self.dve.do
        for tt in range(4):
            t = self.dve.last()
            for n in range(16):
                a = sc[:, tt, 128 * n:128 * n + 128]
                v, x = val[:, 16 * n:16 * n + 16], idx[:, 16 * n:16 * n + 16]
                t = self.top16(a, v, x, s2[:, 0:128], t)
            t = self.cp(fidx, idx, t)
            v4_, f4 = val.rearrange("p (h s k) -> p h s k", h=8, s=2), fidx.rearrange("p (h s k) -> p h s k", h=8, s=2)
            for hd in range(8):
                c = cand[:, 256 * hd:256 * hd + 256]
                t = self.tt(v3(c, 16), bc(v4_[:, hd, 0, :], 2, [128, 16, 16]), bc(v4_[:, hd, 1, :], 1, [128, 16, 16]), ALU.add,
                            t)
                t = self.top16(c, best[:, 16 * hd:16 * hd + 16], ci[:, 16 * hd:16 * hd + 16], s2, t)
            o4 = v4(oh, 16, 16)
            for s in range(2):
                if s == 0:
                    t = self.ts(hi, ci, 4, None, ALU.logical_shift_right, None, t)
                else:
                    t = self.ts(hi, ci, 15, None, ALU.bitwise_and, None, t)
                t = self.cp(hf, hi, t)
                h3 = v3(hf, 16)
                t = self.tt(o4, bc(h3, 3, [128, 8, 16, 16]), self.row["i16"].unsqueeze(1).unsqueeze(1).to_broadcast(
                    [128, 8, 16, 16]), ALU.is_equal, t)
                t = self.tt(o4, o4, bc(f4[:, :, s, :], 2, [128, 8, 16, 16]), ALU.mult, t)
                t = self.red(esel[:, 128 * s:128 * s + 128], v3(oh, 16), ALU.add, t, self.pe.last() if s == 0 else None)
            b3, g3 = v3(best, 16), v3(gate, 16)
            t = self.tt(g3, b3, b3[:, :, 0:1].to_broadcast([128, 8, 16]), ALU.subtract, t, self.pe.last())
            t = self.ac(gate, gate, AF.Exp, t)
            t = self.red(mx, g3, ALU.add, t)
            t = self.rec(mx, mx, t)
            t = self.tt(g3, g3, bc(mx, 2, [128, 8, 16]), ALU.mult, t)
            bank, ids, rel = self.ps.take()
            for i, src in enumerate((esel[:, 0:128], esel[:, 128:256], gate)):
                t2 = self.tr(bank[:, 128 * i:128 * i + 128], src, t, rel, mark=(i == 2))
            us = [self.cp(EG[i][:, 128 * tt:128 * tt + 128], bank[:, 128 * i:128 * i + 128], t2) for i in range(3)]
            self.ps.free(ids, us)
        self.fence()
        ar.at = low + 1536
        stage = [ar.take(8192)]
        NO = 8
        o1 = [ar.take(128) for _ in range(NO)]
        o2 = [ar.take(128) for _ in range(NO)]
        f1, f2 = [None] * NO, [None] * NO
        st_free = [None, None]
        gd = d["gates"]
        t_w = []
        half = [[], []]
        for ch in range(8):
            sg = stage[0].rearrange("p (e t) -> p e t", t=64)
            tcp = []
            for q in range(16):
                bank, ids, rel = self.ps.take()
                for i in range(4):
                    tk = 64 * ch + 4 * q + i
                    n = tk % NO
                    ta = self.ts(o1[n], S["iota"], EG[0][:, tk:tk + 1], EG[2][:, tk:tk + 1], ALU.is_equal, ALU.mult, f1[n])
                    tb = self.ts(o2[n], S["iota"], EG[1][:, tk:tk + 1], None, ALU.is_equal, None, f1[n], q=self.pool)
                    tm = self.mm(bank[:, 128 * i:128 * i + 128], [(o2[n], o1[n])], ta, tb, rel)
                    f1[n] = tm
                src = bank.rearrange("p (t e) -> p e t", e=128)
                o = sg[:, :, 4 * q:4 * q + 4]
                if q % 2:
                    u = self.acp(o, src, tm, st_free)
                else:
                    u = self.cp(o, src, tm, st_free)
                self.ps.free(ids, u)
                tcp.append(u)
            w = self.act.dma(gd[:, :, 64 * ch:64 * ch + 64].rearrange("a b t -> b a t"), sg, self.dsem(), tcp)
            st_free = [w]
            t_w.append(w)
        self.fence()
        for q in (self.pe, self.dve, self.act, self.pool):
            q.wait(t_w)
        ar.at = low
        acc = v3(ar.take(4096), 512)
        A = [ar.take(512) for _ in range(8)]
        gl = [ar.take(512) for _ in range(3)]
        A_free, g_free = [None] * 8, [None] * 3
        tz = self.zero(acc, self.floor, q=self.dve)
        tacc = [tz] * 8
        tA = {}

        def up(gi):
            for p in range(2):
                G, tG, sG = self.ring.take(gd[4 * gi + 2 * p:4 * gi + 2 * p + 2].rearrange("a b t -> b a t"), 1024, t_w)
                for i in range(2):
                    n = 4 * gi + 2 * p + i
                    (bank, ids, t), = self.proj([(d["peeru"][n], 1024)], lambda k, a, b: f[:, k, :], [(0, 512)])
                    x = gl[n % 3]
                    t = self.ac(x, bank, AF.Gelu, t, g_free[n % 3])
                    self.ps.free(ids, t)
                    tA[n] = self.tt(A[n % 8], x, G[:, 512 * i:512 * i + 512], ALU.mult, t, tG, A_free[n % 8])
                    g_free[n % 3] = tA[n]
                self.ring.free(sG, tA[n])

        def down(gi):
            ns = range(4 * gi, 4 * gi + 4)
            vs = [self.ring.take(d["peerv"][n]) for n in ns]
            for j in range(8):
                bank, ids, rel = self.ps.take()
                t = self.mm(bank, [(w[0][:, 128 * j:128 * j + 128], A[n % 8]) for w, n in zip(vs, ns)],
                            [w[1] for w in vs], [tA[n] for n in ns], rel)
                tacc[j] = self.tt(acc[:, j, :], acc[:, j, :], bank, ALU.add, t, tacc[j])
                self.ps.free(ids, tacc[j])
            for n, w in zip(ns, vs):
                self.ring.free(w[2], t)
                A_free[n % 8] = t

        up(0)
        for gi in range(32):
            if gi + 1 < 32:
                up(gi + 1)
            down(gi)
        for j in range(8):
            t = self.stt(h[:, j, :], acc[:, j, :], m[:, 40 + j, 0:1], h[:, j, :], ALU.mult, ALU.add, tacc[j])
        r = self.rms(lambda k: h[:, k, :], 8, rstd, sqt, S["m1024"], EPS, [(0, 512)], t)
        for j in range(8):
            t = self.stt(h[:, j, :], h[:, j, :], V["final_norm"][:, j:j + 1], rstd, ALU.mult, ALU.mult, r)
        return t

    def top16(self, a, v, x, tmp, t):
        D = self.dve.do
        t = D(lambda e: e.max(v[:, 0:8], a), t)
        u = D(lambda e: e.max_index(x[:, 0:8], v[:, 0:8], a), t)
        t = D(lambda e: e.match_replace(tmp, v[:, 0:8], a, LOW), t)
        t = D(lambda e: e.max(v[:, 8:16], tmp), t)
        return D(lambda e: e.max_index(x[:, 8:16], v[:, 8:16], tmp), t)

    def affine(self, X, H, m, j0, segs, t, tm):
        one = self.ones16
        t1 = [self.ts(one[:, 8 * s:8 * s + 8], m[:, j0 + 8:j0 + 16, s], 1.0, None, ALU.add, None, tm, self.act.last())
              for s in range(2)]
        for k in range(8):
            for s, (a, b) in enumerate(segs):
                u = self.ac(H[:, k, a:b], X[:, k, a:b], AF.Identity, t, t1, scale=one[:, 8 * s + k:8 * s + k + 1],
                            bias=m[:, j0 + k, s:s + 1])
        return u

    def residual_norm(self, X, units, rhs, m, jg, g, b, segs, rstd, sqt, *toks):
        n = segs[-1][1]
        t = None
        for k in range(8):
            x = X[:, k, 0:n]
            ta = self.act.do(lambda e, x=x: e.mul(x, x, ALPHA), *toks)
            got = self.proj(units(k), rhs, segs, toks=toks)
            for s, ((bank, ids, t), (lo, hi)) in enumerate(zip(got, segs)):
                x = X[:, k, lo:hi]
                t = self.stt(x, bank[:, 0:hi - lo], m[:, jg + k, s:s + 1], x, ALU.mult, ALU.add, t, ta)
                self.ps.free(ids, t)
        means = []
        for lo, hi in segs:
            bank, ids, rel = self.ps.take()
            u = self.mm(bank[:, 0:hi - lo], [(self.sq["m1024"], X[:, k, lo:hi]) for k in range(8)], t, rel)
            means.append((bank, ids, u))
        for k in range(8):
            for (bank, ids, u), (lo, hi) in zip(means, segs):
                t = self.tt(X[:, k, lo:hi], X[:, k, lo:hi], bank[:, 0:hi - lo], ALU.subtract, u)
        for bank, ids, u in means:
            self.ps.free(ids, t)
        r = self.rms(lambda k: X[:, k, 0:n], 8, rstd, [s[:, 0:n] for s in sqt], self.sq["m1024"], LN_EPS, segs, t)
        for k in range(8):
            x = X[:, k, 0:n]
            t = self.tt(x, x, rstd[:, 0:n], ALU.mult, r)
            t = self.ac(x, x, AF.Identity, t, scale=g[:, k:k + 1], bias=b[:, k:k + 1])
        return t

    def turn(self, x, R, cos, sin, tmp, t, p=128):
        bank, ids, rel = self.ps.take()
        u = self.mm(bank[0:p, :], [(R[0:p, 0:p], x)], t, rel)
        w = self.tt(tmp[0:p, :], bank[0:p, :], sin[0:p, :], ALU.mult, u, self.pool.last())
        self.ps.free(ids, w)
        u = self.tt(x, x, cos[0:p, :], ALU.mult, u, q=self.pool)
        return self.tt(x, x, tmp[0:p, :], ALU.add, u, w, q=self.pool)

    def attend(self, units, P, PT, st, P2=()):
        P, nP = [*P, *P2], len(P)
        P_free, PT_free, st_free = [None] * len(P), [None] * len(PT), [None] * len(st)
        pend, cnt, banks = [], [0, 0, 0, 0], {}

        def first(u):
            ps = []
            for which, segs in enumerate(u["segs"]):
                n = sum(x[3] for x in segs)
                bank, ids, rel = self.ps.take(2)
                for i, (q, k, c, w) in enumerate(segs):
                    t = self.mm(bank[:, c:c + w], [(q, k)], rel, u["toks"], mark=True)
                for c, mk in u.get("masks", ()):
                    t = self.tt(bank[:, c:c + 128], bank[:, c:c + 128], self.sq[mk], ALU.add, t)
                pi = nP + cnt[3] % 2 if which else cnt[0] % nP
                cnt[3 if which else 0] += 1
                si = cnt[1] % len(st)
                cnt[1] += 1
                p, s = P[pi], st[si]
                t = self.red(s[:, 0:1], bank[:, 0:n], ALU.max, t, st_free[si])
                sc = u["scale"]
                if u.get("sink") is not None:
                    t = self.ts(s[:, 0:1], s[:, 0:1], sc, u["sink"], ALU.mult, ALU.max, t)
                    t = self.ts(s[:, 0:1], s[:, 0:1], -1.0, None, ALU.mult, None, t)
                else:
                    t = self.ts(s[:, 0:1], s[:, 0:1], -sc, None, ALU.mult, None, t)
                t = self.ac(p[:, 0:n], bank[:, 0:n], AF.Exp, t, P_free[pi], scale=sc, bias=s[:, 0:1], accum=s[:, 1:2])
                self.ps.free(ids, t)
                if u.get("sink") is not None:
                    t = self.ac(s[:, 2:3], u["sink"], AF.Exp, t, bias=s[:, 0:1])
                    t = self.tt(s[:, 1:2], s[:, 1:2], s[:, 2:3], ALU.add, t)
                t = self.rec(s[:, 1:2], s[:, 1:2], t)
                ps.append((p, s, pi, si, n, t))
            p, s, pi, si, n, t = ps[0]
            if len(ps) == 2:
                p2, s2, pi2, si2, _, t2 = ps[1]
                t2 = self.tt(s2[:, 1:2], s2[:, 1:2], self.lam, ALU.mult, t2)
                t2 = self.ts(p2[:, 0:n], p2[:, 0:n], s2[:, 1:2], None, ALU.mult, None, t2)
                t = self.stt(p[:, 0:n], p[:, 0:n], s[:, 1:2], p2[:, 0:n], ALU.mult, ALU.subtract, t, t2)
                P_free[pi2] = st_free[si2] = t
            else:
                t = self.ts(p[:, 0:n], p[:, 0:n], s[:, 1:2], None, ALU.mult, None, t)
            st_free[si] = t
            return p, pi, n, t

        def second(u, p, pi, n, t):
            xi = cnt[2] % len(PT)
            cnt[2] += 1
            pt = PT[xi]
            bank, ids, rel = self.ps.take(2)
            for c in range(n // 128):
                t2 = self.tr(bank[:, 128 * c:128 * c + 128], p[:, 128 * c:128 * c + 128], t, rel, mark=True)
            P_free[pi] = t2
            h = min(n, 512)
            ta = self.acp(pt[:, 0:h], bank[:, 0:h], t2, PT_free[xi])
            tb = self.cp(pt[:, h:n], bank[:, h:n], t2, PT_free[xi]) if n > h else None
            self.ps.free(ids, [ta, tb])
            out, p0, M, col, width, key, lastu = u["out"]
            if key not in banks:
                banks[key] = self.ps.take()
            ob, oid, orel = banks[key]
            t = self.mm(ob[p0:p0 + M, col:col + 128],
                        [(v, pt[:, 128 * c:128 * c + 128]) for c, v in enumerate(u["vals"])], ta, tb, orel)
            PT_free[xi] = t
            if lastu:
                t = self.acp(out, ob[p0:p0 + M, 0:width], t)
                self.ps.free(oid, t)
                del banks[key]
            return t

        t = None
        for u in units:
            pend.append((u, first(u)))
            if len(pend) > 2:
                v, a = pend.pop(0)
                t = second(v, *a)
        for v, a in pend:
            t = second(v, *a)
        return t

    def ffn(self, i, X, H, m, segs, hid, raws, accs, t):
        d, V = self.d, self.vec
        n = segs[-1][1]
        th = self.affine(X, H, m, 24, segs, t, None)
        rhs = lambda k, a, b: H[:, k, a:b]
        tz = [self.zero(r, self.floor) for r in raws]
        raw_free, acc_free = [tz, tz], [None, None]
        for j in range(22):
            r, acc = raws[j % 2], accs[j % 2]
            got = self.proj([(d["wgate"][22 * i + j], 1024)], rhs, segs, toks=(th,))
            tc = []
            for (bank, ids, t), off, (a, b) in zip(got, (2, 518), segs):
                u = self.acp(r[:, off:off + b - a], bank[:, 0:b - a], t, raw_free[j % 2])
                self.ps.free(ids, u)
                tc.append(u)
            w = V["fcw"][:, 66 * i + 3 * j:66 * i + 3 * j + 3]
            last = []
            for base, (a, b) in zip((1, 517), segs):
                o, w0 = acc[:, a:b], b - a
                t = self.ts(o, r[:, base:base + w0], w[:, 0:1], V["fcb"][:, 22 * i + j:22 * i + j + 1], ALU.mult, ALU.add, tc,
                            acc_free[j % 2])
                for k in (1, 2):
                    t = self.stt(o, r[:, base + k:base + k + w0], w[:, k:k + 1], o, ALU.mult, ALU.add, t)
                last.append(t)
            raw_free[j % 2] = last
            ts = self.ac(acc[:, 0:n], acc[:, 0:n], AF.Silu, last)
            got = self.proj([(d["wup"][22 * i + j], 1024)], rhs, segs)
            for (bank, ids, t), (a, b) in zip(got, segs):
                u = self.tt(hid[:, j, a:b], acc[:, a:b], bank[:, 0:b - a], ALU.mult, t, ts)
                self.ps.free(ids, u)
            acc_free[j % 2] = u
        return u

    def second(self, alone):
        d, ar, V, S = self.d, self.ar, self.vec, self.sq
        seg2, seg1 = [(0, 512), (512, 768)], [(0, 512)]
        m, tm = self.modulation("c2", "wmod2", 0, V["bmod2"][:, 0:48], 1)
        m1, tm1 = self.modulation("c2", "wmod2", 48, V["bmod2"][:, 48:96], 2)
        self.fence()
        ar.at = self.base
        X = v3(ar.take(6144), 768)
        assert ar.at <= self.base + 8192
        if alone:
            tx = self.load(X[:, :, 0:512], d["xT"])
        else:
            tx = self.cp(X[:, :, 0:512], self.h, self.floor)
        tc = self.load(X[:, :, 512:768], d["ctxT2"])
        self.fence()
        self.ones16 = ar.take(16)
        lamb = ar.take(8)
        sub = ar.take(1)
        st = [ar.take(4) for _ in range(6)]
        top = ar.at
        H = v3(ar.take(6144), 768)
        O1 = ar.take(6144)
        O = v3(O1, 768)
        qa, kva, kr = v3(ar.take(1536), 768), ar.take(768), ar.take(768)
        Vm, wkv, rope = v3(ar.take(3072), 512), ar.take(1024), ar.take(2048)
        qb, kb = [ar.take(768) for _ in range(2)], [ar.take(768) for _ in range(2)]
        tmp = O1[:, 3072:3584]
        rstd, sqt = O1[:, 3584:4352], [O1[:, 4352 + 768 * i:5120 + 768 * i] for i in range(2)]
        P = [ar.take(768) for _ in range(3)]
        PT = [ar.take(768) for _ in range(2)]
        trp, twk = self.load(rope, d["rope"]), self.load(wkv, d["wkvb"])
        c96, s96, c128, s128 = (rope[:, 512 * i:512 * i + 512] for i in range(4))
        th = self.affine(X, H, m, 0, seg2, [tx, tc], tm)
        rhs = lambda k, a, b: H[:, k, a:b]

        def project(j, out, p=128):
            ts = []
            for (bank, ids, t), (a, b) in zip(self.proj([(d["abin"][j], 1024)], rhs, seg2, toks=(th,)), seg2):
                u = self.acp(out[0:p, a:b], bank[0:p, 0:b - a], t)
                self.ps.free(ids, u)
                ts.append(u)
            return ts

        t0 = [project(j, qa[:, j, :]) for j in range(2)]
        r = self.rms(lambda k: qa[:, k, :], 2, rstd, sqt, S["m256"], EPS, seg2, t0)
        tq = [self.stt(qa[:, k, :], qa[:, k, :], V["qn"][:, k:k + 1], rstd, ALU.mult, ALU.mult, r) for k in range(2)]
        t0 = project(6, kva)
        r = self.rms(lambda k: kva, 1, rstd, sqt, S["m128"], EPS, seg2, t0, tq)
        tk = self.stt(kva, kva, V["kvn"], rstd, ALU.mult, ALU.mult, r)
        t0 = project(8, kr, 96)
        tkr = self.turn(kr[0:96, 0:512], S["r96"], c96, s96, tmp, [t0, trp], 96)
        tv = []
        for c in range(6):
            bank, ids, rel = self.ps.take()
            t = self.mm(bank, [(kva[:, 128 * c:128 * c + 128], wkv[:, 512:1024])], tk, twk, rel)
            u = self.acp(Vm[:, c, :], bank, t)
            self.ps.free(ids, u)
            tv.append(u)
        qk_free = [None, None]
        scale = 96 ** -0.5

        def prepare(h):
            q, k = qb[h % 2], kb[h % 2]
            w, tw, s = self.ring.take(d["wqb"][h], 192)
            ts = []
            for a, b in seg2:
                bank, ids, rel = self.ps.take()
                t = self.mm(bank[0:96, 0:b - a], [(w[:, 96 * i:96 * i + 96], qa[:, i, a:b]) for i in range(2)], tw, tq, rel)
                u = self.acp(q[0:96, a:b], bank[0:96, 0:b - a], t, qk_free[h % 2])
                self.ps.free(ids, u)
                ts.append(u)
            self.ring.free(s, t)
            ts.append(self.turn(q[0:96, 0:512], S["r96"], c96, s96, tmp, ts, 96))
            for a, b in seg2:
                bank, ids, rel = self.ps.take()
                t = self.mm(bank[0:64, 0:b - a], [(wkv[:, 64 * h:64 * h + 64], kva[:, a:b])], rel)
                u = self.acp(k[0:64, a:b], bank[0:64, 0:b - a], t, qk_free[h % 2])
                self.ps.free(ids, u)
                ts.append(u)
            ts.append(self.cp(k[64:96, :], kr[64:96, :], tkr, t0, qk_free[h % 2]))
            return ts

        tp = prepare(0)
        for h in range(8):
            tn = prepare(h + 1) if h < 7 else None
            q, k = qb[h % 2], kb[h % 2]
            p0 = 64 * (h % 2)
            units = []
            vals = [Vm[:, c, 64 * h:64 * h + 64] for c in range(6)]
            for qt in range(6):
                ql = q[0:96, 128 * qt:128 * qt + 128]
                lat = qt < 4
                if lat:
                    segs = [(ql, k[0:96, 0:512], 0, 512), (ql, k[0:96, 512:768], 512, 256)]
                else:
                    segs = [(ql, k[0:96, 512:768], 0, 256)]
                o = O[p0:p0 + 64, h // 2, 0:512] if lat else O[p0:p0 + 64, h // 2, 512:768]
                units.append(dict(segs=[segs], scale=scale, toks=[tp, tv], vals=vals if lat else vals[4:],
                                  out=(o, p0, 64, 128 * (qt % 4), 512 if lat else 256, (h, lat), qt in (3, 5))))
            self.attend(units, P, PT, st)
            qk_free[h % 2] = self.pe.last()
            tp = tn
        self.fence()
        ar.at = top + 12288
        qs, ks, Vs = v3(ar.take(3072), 768), ar.take(768), v3(ar.take(768), 128)
        tmp = ar.take(512)
        assert ar.at <= top + 12288 + 1536 + 768 + 768 + 3072
        ts = []
        for j in range(4):
            t0 = project(2 + j, qs[:, j, :])
            ts.append([t0, self.turn(qs[:, j, 0:512], S["r128"], c128, s128, tmp, t0)])
        t0 = project(7, ks)
        ts.append([t0, self.turn(ks[:, 0:512], S["r128"], c128, s128, tmp, t0)])
        w, tw, s = self.ring.take(d["abin"][9])
        for c in range(6):
            bank, ids, rel = self.ps.take()
            t = self.mm(bank[:, 0:128], [(H[:, k, 128 * c:128 * c + 128], w[:, 128 * k:128 * k + 128]) for k in range(8)], tw, rel)
            u = self.acp(Vs[:, c, :], bank[:, 0:128], t)
            self.ps.free(ids, u)
            ts.append(u)
        self.ring.free(s, t)
        units = []
        for i in range(4):
            for kv in range(2):
                p0 = 64 * kv
                ps = slice(p0, p0 + 64)
                sk = self.row["sink"][:, i + 4 * kv:i + 4 * kv + 1]
                for qt in range(6):
                    ql = qs[ps, i, 128 * qt:128 * qt + 128]
                    segs = [(ql, ks[ps, 512:768], 0, 256)]
                    tiles, masks = [4, 5], []
                    if qt < 4:
                        lo, hi = max(qt - 1, 0), min(qt + 1, 3)
                        segs.append((ql, ks[ps, 128 * lo:128 * lo + 256], 256, 256))
                        if hi - lo == 2:
                            segs.append((ql, ks[ps, 128 * hi:128 * hi + 128], 512, 128))
                        tiles += range(lo, hi + 1)
                        if qt > 0:
                            masks.append((256, "bandlo"))
                        if qt < 3:
                            masks.append((256 + 128 * (hi - lo), "bandhi"))
                    o = O[ps, 4 + i, 0:512] if qt < 4 else O[ps, 4 + i, 512:768]
                    units.append(dict(segs=[segs], scale=0.125, toks=[ts], masks=masks, sink=sk,
                                      vals=[Vs[:, c, p0:p0 + 64] for c in tiles],
                                      out=(o, p0, 64, 128 * (qt % 4), 512 if qt < 4 else 256, (i, kv, qt < 4), qt in (3, 5))))
        self.attend(units, P, PT, st)
        self.fence()
        ar.at = top + 12288
        rstd, sqt = ar.take(768), [ar.take(768) for _ in range(2)]
        t = self.residual_norm(X, lambda k: [(d["about"][k], 1024)], lambda k, a, b: O[:, k, a:b], m, 16, V["ln1g"][:, 0:8],
                               V["ln1b"][:, 0:8], seg2, rstd, sqt)
        t = self.feed(0, X, m, seg2, top, t, V)
        self.fence()
        ar.at = top
        H1 = ar.take(6144)
        H, O = v3(H1, 768), v3(H1[:, 0:4096], 512)
        q, k = v3(ar.take(4096), 512), v3(ar.take(6144), 768)
        Vd = v3(ar.take(6144), 1024)
        rope = ar.take(1024)
        tmp = ar.take(512)
        P, P2 = [ar.take(768) for _ in range(3)], [H1[:, 4096 + 768 * i:4864 + 768 * i] for i in range(2)]
        PT = [ar.take(768) for _ in range(2)]
        trp = self.load(rope, d["rope"][:, 1024:2048])
        c128, s128 = rope[:, 0:512], rope[:, 512:1024]
        self.lam = lamb[:, 0:1]
        pr = tmp[:, 0:64]
        t = self.floor
        for i, (a, b) in enumerate((("lq1", "lk1"), ("lq2", "lk2"))):
            t = self.tt(pr, self.row[a], self.row[b], ALU.mult, t)
            t = self.red(lamb[:, 2 + i:3 + i], pr, ALU.add, t)
            t = self.ac(lamb[:, 2 + i:3 + i], lamb[:, 2 + i:3 + i], AF.Exp, t)
        t = self.tt(lamb[:, 0:1], lamb[:, 2:3], lamb[:, 3:4], ALU.subtract, t)
        t = self.ts(lamb[:, 0:1], lamb[:, 0:1], LAMBDA_INIT, None, ALU.add, None, t)
        t = self.ts(sub, V["subln"], 1.0 - LAMBDA_INIT, None, ALU.mult, None, t)
        th = self.affine(X, H, m1, 0, seg2, t, tm1)
        rhs = lambda k, a, b: H[:, k, a:b]
        ts = []
        for j in range(16):
            dst, segs = (q[:, j, :], seg1) if j < 8 else (k[:, j - 8, :], seg2)
            t0 = []
            for (bank, ids, t), (a, b) in zip(self.proj([(d["dqk"][j], 1024)], rhs, segs, toks=(th,)), segs):
                u = self.acp(dst[:, a:b], bank[:, 0:b - a], t)
                self.ps.free(ids, u)
                t0.append(u)
            ts += [t0, self.turn(dst[:, 0:512], S["r128"], c128, s128, tmp, [t0, trp])]
        ws = [self.ring.take(d["dv"][i]) for i in range(8)]
        for c in range(6):
            for hf in range(2):
                bank, ids, rel = self.ps.take()
                t = self.mm(bank, [(H[:, i, 128 * c:128 * c + 128], ws[i][0][:, 512 * hf:512 * hf + 512]) for i in range(8)],
                            [w[1] for w in ws], rel)
                u = self.acp(Vd[:, c, 512 * hf:512 * hf + 512], bank, t)
                self.ps.free(ids, u)
                ts.append(u)
        for w in ws:
            self.ring.free(w[2], t)
        self.act.wait(t)
        units = []
        for h in range(8):
            for qt in range(4):
                sg = []
                for s in range(2):
                    ps = slice(64 * s, 64 * s + 64)
                    ql = q[ps, h, 128 * qt:128 * qt + 128]
                    sg.append([(ql, k[ps, h, 0:512], 0, 512), (ql, k[ps, h, 512:768], 512, 256)])
                units.append(dict(segs=sg, scale=0.125, toks=[ts], vals=[Vd[:, c, 128 * h:128 * h + 128] for c in range(6)],
                                  out=(O[:, h, :], 0, 128, 128 * qt, 512, h, qt == 3)))
        t = self.attend(units, P, PT, st, P2)
        self.fence()
        for h in range(8):
            r = self.rms(lambda k: O[:, h, :], 1, P[h % 2][:, 0:512], [P2[h % 2][:, 0:512]] * 2, S["m128"], EPS, seg1, t)
            u = self.stt(O[:, h, :], O[:, h, :], sub, P[h % 2][:, 0:512], ALU.mult, ALU.mult, r)
        t = self.residual_norm(X, lambda k: [(d["dout"][k], 1024)], lambda k, a, b: O[:, k, a:b], m1, 16, V["ln1g"][:, 8:16],
                               V["ln1b"][:, 8:16], seg1, P[0], P[1:3], u)
        t = self.feed(1, X, m1, seg1, top, t, V)
        self.h = X[:, :, 0:512]
        return t

    def feed(self, i, X, m, segs, top, t, V):
        d, ar = self.d, self.ar
        self.fence()
        ar.at = top
        H = v3(ar.take(6144), 768)
        hid = v3(ar.take(22 * 768), 768)
        raws = [ar.take(776) for _ in range(2)]
        accs = [ar.take(768) for _ in range(2)]
        rstd, sqt = ar.take(768), [ar.take(768) for _ in range(2)]
        t = self.ffn(i, X, H, m, segs, hid, raws, accs, t)
        units = lambda k: [(d["wdown"][i, k][:, a:b], b - a) for a, b in ((0, 1024), (1024, 2048), (2048, 2816))]
        return self.residual_norm(X, units, lambda k, a, b: hid[:, k, a:b], m, 40, V["ln2g"][:, 8 * i:8 * i + 8],
                                  V["ln2b"][:, 8 * i:8 * i + 8], segs, rstd, sqt, t)


def _tiles(w):
    k, n = w.shape
    return np.ascontiguousarray(w.reshape(k // 128, 128, n // 128, 128).transpose(2, 1, 0, 3).reshape(n // 128, 128, k))


def _cols(v):
    return np.ascontiguousarray(np.asarray(v).reshape(-1, 128).T)


def _fm(x):
    t, f = x.shape
    return np.ascontiguousarray(x.T.reshape(f // 128, 128, t).transpose(1, 0, 2))


def _constants():
    f32 = np.float32
    i = np.arange(128)
    j, l = i[:, None], i[None, :]
    sq = {"ident": j == l, "ones": j >= 0 * l, "le": j <= l, "ge": j >= l, "gt": j > l, "lt": j < l}
    sq = {k: (v + 0 * l).astype(f32) for k, v in sq.items()}
    sq["ones"][:] = 1
    sq["m256"] = np.full((128, 128), 1 / 256, f32)
    sq["m1024"] = np.full((128, 128), 1 / 1024, f32)
    sq["m128"] = np.full((128, 128), 1 / 128, f32)
    sq["m64"] = ((j // 64 == l // 64) / 64).astype(f32)
    sq["iota"] = np.broadcast_to(l, (128, 128)).astype(f32)

    def rot(n, blocks, start):
        r = np.zeros((128, 128), f32)
        q = n // 4
        for b in blocks:
            o = start + b * n
            for k in range(q):
                r[o + q + k, o + k] = -1
                r[o + k, o + q + k] = 1
                r[o + 3 * q + k, o + 2 * q + k] = -1
                r[o + 2 * q + k, o + 3 * q + k] = 1
        return r

    sq["r96"] = rot(32, [0], 64)
    sq["r128"] = rot(64, [0, 1], 0)
    sq["bandlo"] = np.where(l >= j, 0, NEG).astype(f32)
    sq["bandhi"] = np.where(l <= j, 0, NEG).astype(f32)
    out = {"squares": np.concatenate([sq[n] for n in SQ], 1)}
    t = np.arange(512)
    ang = 2 * np.pi * ((t[:, None] * t[None, :]) % 1024) / 1024
    c, s = np.cos(ang), np.sin(ang)
    s[0, :] = 0
    s[:, 0] = 0
    tm = lambda a: np.ascontiguousarray(a.reshape(4, 128, -1).transpose(1, 0, 2)).astype(f32)
    out["dftc"], out["dfts"] = tm(c), tm(s)
    is0 = s[0:128].copy()
    is0[0] = (-1.0) ** t
    out["is0"] = is0.astype(f32)
    ny = np.zeros((512, 128))
    ny[:, 0] = (-1.0) ** t
    out["nyq"] = tm(ny)
    tl = np.linspace(0.0, 1.0, 512).astype(f32)
    wa = (f32(2 * np.pi) * t.astype(f32) / f32(512)).astype(f32)
    bands = np.linspace(1e-4, 15, 16).astype(f32)
    an = (wa[:, None] * bands[None, :]).astype(f32)
    out["zpos"] = np.ascontiguousarray(np.concatenate([tl[:, None], np.cos(an), -np.sin(an)], -1).T).astype(f32)
    dl = np.abs(np.linspace(math.log(1e-2) / 1.5, math.log(1e-2) / 0.3, 1024).astype(f32))
    dec = np.exp(-tl[:, None] * dl[None, :]).astype(f32)
    out["dec"] = np.ascontiguousarray(dec.reshape(2, 2, 128, 2, 512).transpose(3, 0, 2, 1, 4).reshape(2, 2, 128, 1024))

    def rope(dim):
        row = np.repeat(np.arange(8), 64).astype(f32)
        col = np.tile(np.arange(64), 8).astype(f32)
        q = dim // 4
        fr = (f32(10000.0) ** (-np.arange(q, dtype=f32) / f32(q))).astype(f32)
        ar, ac = row[:, None] * fr, col[:, None] * fr
        a = np.concatenate([ar, ar, ac, ac], -1)
        return np.cos(a).T.astype(f32), np.sin(a).T.astype(f32)

    c32, s32 = rope(32)
    c64, s64 = rope(64)
    z = np.zeros((32, 512), f32)
    r96c = np.concatenate([np.ones((64, 512), f32), c32, z])
    r96s = np.concatenate([np.zeros((64, 512), f32), s32, z])
    out["rope"] = np.concatenate([r96c, r96s, np.tile(c64, (2, 1)), np.tile(s64, (2, 1))], 1)
    return {k: np.ascontiguousarray(v, dtype=f32) for k, v in out.items()}


def _arrays(p):
    p = {k: np.asarray(v) for k, v in p.items()}
    a = _constants()
    a["xT"], a["ctxT"], a["ctxT2"] = _fm(p["x"][0]), _fm(p["ctx"][0]), _fm(p["ctx_2"][0])
    a["wmod"] = _tiles(p["w_mod"][0])
    a["wmod2"] = np.concatenate([_tiles(p["w_mod_2"][i]) for i in range(2)])
    win = p["w_in"][0]
    a["win"] = _tiles(np.concatenate([win[:, :3072], win[:, 3104:]], 1))
    a["wdt"] = np.ascontiguousarray(win[:, 3072:3104].reshape(8, 128, 32).transpose(1, 0, 2).reshape(128, 256))
    w12 = np.zeros((64, 128), np.float32)
    w12[:33, :64] = p["hy_w1"][0]
    w12[:, 64:] = p["hy_w2"][0]
    a["hyw12"] = w12
    w3 = p["hy_w3"][0].reshape(64, 2, 2, 2, 512)
    a["hyw3"] = np.ascontiguousarray(w3.transpose(1, 3, 0, 2, 4).reshape(2, 2, 64, 1024))
    a["wout"] = np.ascontiguousarray(_tiles(p["w_out"][0]).reshape(8, 128, 2, 1024).transpose(0, 2, 1, 3))
    a["wq"] = _tiles(p["peer_wq"][0])
    a["subkeys"] = np.ascontiguousarray(p["peer_subkeys"][0].transpose(2, 0, 1).reshape(128, 256))
    a["peeru"] = np.ascontiguousarray(p["peer_u"][0].reshape(128, 128, 8, 128).transpose(0, 3, 2, 1).reshape(128, 128, 1024))
    a["peerv"] = np.ascontiguousarray(p["peer_v"][0].reshape(128, 128, 1024))

    def pad(v):
        o = np.zeros((128, 1), np.float32)
        o[:v.size, 0] = v.reshape(-1)
        return o

    def taps(w):
        k, n = w.shape
        return np.ascontiguousarray(w.reshape(k, n // 128, 128).transpose(2, 1, 0).reshape(128, -1))

    c2 = lambda x, y: np.ascontiguousarray(np.stack([_cols(x), _cols(y)], 2).reshape(128, 16))
    v = {"norm1": _cols(p["norm1"]), "convw": taps(p["ssd_conv_w"][0]), "convb": _cols(p["ssd_conv_b"]),
         "ssd_norm": _cols(p["ssd_norm"]), "hyw": taps(p["hy_short_w"][0]), "hyb": _cols(p["hy_short_b"]),
         "hbias": _cols(p["hy_filt_bias"]), "hy_norm": _cols(p["hy_norm"]), "norm2": _cols(p["norm2"]),
         "final_norm": _cols(p["final_norm"]), "bmod": _cols(p["b_mod"]), "dtb": pad(p["ssd_dt_bias"]),
         "hyb1": pad(p["hy_b1"]), "hyb2": pad(p["hy_b2"]), "fr0": pad(p["hy_sin_freq"][0, 0]),
         "fr1": pad(p["hy_sin_freq"][0, 1]), "ln1g": _cols(p["ln1_g_2"]), "ln1b": _cols(p["ln1_b_2"]),
         "ln2g": _cols(p["ln2_g_2"]), "ln2b": _cols(p["ln2_b_2"]),
         "fcw": np.concatenate([taps(p["ffn_conv_w_2"][i]) for i in range(2)], 1), "fcb": _cols(p["ffn_conv_b_2"]),
         "bmod2": _cols(p["b_mod_2"]), "qn": _cols(p["mla_q_norm_2"]), "kvn": _cols(p["mla_kv_norm_2"]),
         "subln": _cols(p["diff_subln_g_2"]), "c1": c2(p["c"], p["c_ctx"]), "c2": c2(p["c_2"], p["c_ctx_2"])}
    a["vecs"] = np.concatenate([v[n] for n, _ in VECS], 1)
    r = {"alog": p["ssd_a_log"], "dskip": p["ssd_d"], "sink": p["swa_sink_2"], "lq1": p["diff_lam_q1_2"],
         "lk1": p["diff_lam_k1_2"], "lq2": p["diff_lam_q2_2"], "lk2": p["diff_lam_k2_2"],
         "i16": np.arange(16, dtype=np.float32)}
    a["rows"] = np.tile(np.concatenate([r[n].reshape(-1) for n, _ in ROWS])[None], (128, 1))
    w = p["ab_w_in_2"][0]
    qs = w[:, 256:768].reshape(1024, 2, 4, 64).transpose(0, 2, 1, 3).reshape(1024, 512)
    kr = np.concatenate([np.zeros((1024, 64), np.float32), w[:, 896:928], np.zeros((1024, 32), np.float32)], 1)
    a["abin"] = _tiles(np.concatenate([w[:, :256], qs, w[:, 768:896], w[:, 928:1056], kr, w[:, 1056:]], 1))
    wq = p["mla_w_qb_2"][0].reshape(2, 128, 8, 96)
    a["wqb"] = np.ascontiguousarray(wq.transpose(2, 1, 0, 3).reshape(8, 128, 192))
    wk = p["mla_w_kvb_2"][0].reshape(128, 8, 128)
    a["wkvb"] = np.ascontiguousarray(np.concatenate([wk[:, :, :64].reshape(128, 512), wk[:, :, 64:].reshape(128, 512)], 1))
    wo = p["ab_w_out_2"][0]
    wos = wo[512:].reshape(2, 4, 64, 1024).transpose(1, 0, 2, 3).reshape(512, 1024)
    a["about"] = _tiles(np.concatenate([wo[:512], wos], 0))
    w = p["diff_w_in_2"][0]
    a["dqk"] = _tiles(w[:, :2048])
    a["dv"] = np.ascontiguousarray(w[:, 2048:].reshape(8, 128, 1024))
    a["dout"] = _tiles(p["diff_w_out_2"][0])
    a["wgate"] = np.concatenate([_tiles(p["ffn_w_gate_2"][i]) for i in range(2)])
    a["wup"] = np.concatenate([_tiles(p["ffn_w_up_2"][i]) for i in range(2)])
    wd = np.stack([_tiles(p["ffn_w_down_2"][i]) for i in range(2)])
    a["wdown"] = wd
    return {k: np.ascontiguousarray(x, dtype=np.float32) for k, x in a.items()}


def build(nc, d, out, part="all", dump=None):
    with ExitStack() as ctx:
        k = Core(nc, d, ctx)
        k.setup()
        if part != "second":
            k.in_projection()
            k.ssd()
            t = k.hyena()
            t = k.out_projection(t)
            t = k.peer(t)
        if part != "first":
            t = k.second(part == "second")
        so = k.dsem()
        t = k.sp.dma(out, k.h, so, t)
        k.sp.wait(t)
        block = ctx.enter_context(nc.Block())
        for deco, q in ((block.tensor, k.pe), (block.vector, k.dve), (block.scalar, k.act), (block.gpsimd, k.pool),
                        (block.sync, k.sp)):
            deco(lambda e, q=q: q.run(e))


def kernel(**inputs):
    import concourse.bacc as bacc
    from concourse.bass_utils import run_bass_kernel_spmd as run

    nc = bacc.Bacc("TRN2", target_bir_lowering=False, num_devices=1)
    arrays = _arrays(inputs)
    d = {n: nc.dram_tensor(n, a.shape, F, kind="ExternalInput").ap() for n, a in arrays.items()}
    d["gates"] = nc.dram_tensor("gates", (128, 128, 512), F, kind="Internal").ap()
    out = nc.dram_tensor("out", (128, 8, 512), F, kind="ExternalOutput").ap()
    build(nc, d, out)
    r = run(nc, [arrays], core_ids=[0]).results[0]["out"]
    return np.ascontiguousarray(np.asarray(r).transpose(2, 1, 0).reshape(1, 512, 1024))
```

```python
import math
from contextlib import ExitStack

import numpy as np

import concourse.bass as bass
from concourse import mybir

F = mybir.dt.float32
FR = mybir.dt.float32r
U32 = mybir.dt.uint32
ALU = mybir.AluOpType
AF = mybir.ActivationFunctionType
AX = mybir.AxisListType.X

L, C, T = 512, 256, 768
EPS = 1e-6
LN_EPS = 1e-5
ALPHA = 4.0 ** 0.25
NEG = -1e30
LOW = -3e38
LAMBDA_INIT = 0.8 - 0.6 * math.exp(-0.3)

SQ = ["ident", "ones", "le", "ge", "gt", "lt", "m256", "m1024", "m64", "m128", "iota", "r96", "r128",
      "bandlo", "bandhi"]
VECS = [("norm1", 8), ("convw", 80), ("convb", 16), ("ssd_norm", 8), ("hyw", 72), ("hyb", 24), ("hbias", 16),
        ("hy_norm", 8), ("norm2", 8), ("final_norm", 8), ("bmod", 48), ("dtb", 1), ("hyb1", 1), ("hyb2", 1),
        ("fr0", 1), ("fr1", 1), ("ln1g", 16), ("ln1b", 16), ("ln2g", 16), ("ln2b", 16), ("fcw", 132),
        ("fcb", 44), ("bmod2", 96), ("qn", 2), ("kvn", 1), ("subln", 1), ("c1", 16), ("c2", 16)]
ROWS = [("alog", 32), ("dskip", 16), ("sink", 8), ("lq1", 64), ("lk1", 64), ("lq2", 64), ("lk2", 64), ("i16", 16)]


class Queue:

    def __init__(self, sem):
        self.sem, self.n, self.ops, self.seen = sem, 0, [], {}

    def wait(self, *toks):
        for t in toks:
            if t is None:
                continue
            if isinstance(t, list):
                self.wait(*t)
                continue
            sem, v = t
            if self.seen.get(id(sem), 0) < v:
                self.seen[id(sem)] = v
                self.ops.append((None, sem, v))

    def do(self, fn, *toks):
        self.wait(*toks)
        self.n += 1
        self.ops.append((fn, self.sem, 1))
        return (self.sem, self.n)

    def quiet(self, fn, *toks):
        self.wait(*toks)
        self.ops.append((fn, None, 0))

    def dma(self, out, in_, sem, *toks):
        self.wait(*toks)
        sem[1] += 16
        self.ops.append((lambda e: e.dma_start(out, in_), sem[0], 16))
        return (sem[0], sem[1])

    def last(self):
        return (self.sem, self.n) if self.n else None

    def run(self, e):
        for fn, sem, v in self.ops:
            if fn is None:
                e.wait_ge(sem, v)
            else:
                i = fn(e)
                if sem is not None:
                    i.then_inc(sem, v)


class Arena:

    def __init__(self, nc, size, offset):
        self.nc, self.full, self.size, self.offset, self.at, self.names = nc, size, size, offset, 0, {}
        self.ap = nc.alloc_sbuf_tensor_at("arena", [128, size], F, offset=offset)

    def place(self, n):
        a = self.at
        self.at += n
        assert self.at <= self.size, (self.at, self.size)
        return a

    def take(self, n):
        a = self.place(n)
        return self.ap[:, a:a + n]

    def rounded(self, n):
        self.at += -self.at % 8
        return self.rounded_at(self.place(n), n)

    def rounded_at(self, a, n):
        if (a, n) not in self.names:
            self.names[a, n] = self.nc.alloc_sbuf_tensor_at(f"rounded_{a}_{n}", [128, n], FR, offset=self.offset + 4 * a)
        return self.names[a, n][:, :]


class Banks:

    def __init__(self, ap):
        self.ap, self.at, self.rel = ap, 0, [[] for _ in range(8)]

    def take(self, n=1):
        for i in range(8):
            b = (self.at + i) % 8
            if b % n == 0 and all(self.rel[j] is not None for j in range(b, b + n)):
                break
        else:
            assert False, "no bank is free"
        self.at = b + n
        toks = []
        for i in range(b, b + n):
            toks += self.rel[i]
            self.rel[i] = None
        return self.ap[:, 512 * b:512 * (b + n)], range(b, b + n), toks

    def free(self, banks, *toks):
        for i in banks:
            self.rel[i] = list(toks)


class Ring:

    def __init__(self, ap, n, sems, sp):
        self.ap, self.n, self.sems, self.sp, self.at = ap, n, sems, sp, 0
        self.rel = [[] for _ in range(n)]

    def take(self, src, cols=1024, *toks, parts=128):
        s = self.at % self.n
        self.at += 1
        assert self.rel[s] is not None, "slot not given back"
        out = self.ap[0:parts, 1024 * s:1024 * s + cols]
        t = self.sp.dma(out, src, self.sems[s], self.rel[s], *toks)
        self.rel[s] = None
        return out, t, s

    def free(self, s, *toks):
        self.rel[s] = list(toks)


class Stream:

    def __init__(self, core, aps, ahead, srcs, rest):
        self.core, self.aps, self.n, self.ahead, self.srcs, self.rest = core, aps, len(aps), ahead, srcs, rest
        n = self.n
        self.rel, self.got, self.at = [[] for _ in range(n)], [], 0
        for _ in range(ahead):
            self.split()

    def split(self):
        i = len(self.got)
        if i == len(self.srcs):
            return
        c, s = self.core, i % self.n
        src, w = self.srcs[i]
        assert self.rel[s] is not None, "pair not given back"
        hi, lo = self.aps[s][:, 0:w], self.aps[s][:, 1024:1024 + w]
        raw, t, r = c.ring.take(src, w)
        th, tl = c.parts(raw, hi, lo, t, self.rel[s], q=self.rest(i))
        c.ring.free(r, th, tl)
        self.rel[s] = None
        self.got.append((hi, lo, [th, tl], s))

    def next(self):
        self.split()
        self.at += 1
        return self.got[self.at - 1]

    def free(self, s, *toks):
        self.rel[s] = list(toks)


def v3(ap, b):
    return ap.rearrange("p (a b) -> p a b", b=b)


def v4(ap, b, c):
    return ap.rearrange("p (a b c) -> p a b c", b=b, c=c)


def bc(ap, axis, shape):
    return ap.unsqueeze(axis).to_broadcast(shape)


class Core:
    def __init__(self, nc, d, ctx):
        self.nc, self.d = nc, d
        sem = lambda n: ctx.enter_context(nc.semaphore(n))
        self.sem = sem
        self.pe, self.dve, self.act = Queue(sem("s_pe")), Queue(sem("s_dve")), Queue(sem("s_act"))
        self.pool, self.sp = Queue(sem("s_pool")), Queue(sem("s_sp"))
        self.ar = Arena(nc, 53184, 16512)
        ps = ctx.enter_context(nc.psum_tensor("psum", [128, 4096], F))
        self.ps = Banks(ps)
        self.rsem = [[sem(f"s_r{i}"), 0] for i in range(13)]
        self.floor = []
        self.rings(13)
        self.nsem = 0

    def dsem(self):
        self.nsem += 1
        return [self.sem(f"s_d{self.nsem}"), 0]

    def fence(self, *more):
        toks = [q.last() for q in (self.pe, self.dve, self.act, self.pool)] + list(more)
        for q in (self.pe, self.dve, self.act, self.pool):
            q.wait(toks)
        self.floor = toks

    def rings(self, n, pairs=0, ahead=0, srcs=(), rest=None):
        ar = self.ar
        ar.size = ar.full - 1024 * n - 2048 * pairs
        self.sp.wait(self.floor)
        self.ring = Ring(ar.ap[:, ar.full - 1024 * n:ar.full], n, self.rsem, self.sp)
        if pairs:
            self.stream = Stream(self, [ar.rounded_at(ar.size + 2048 * i, 2048) for i in range(pairs)], ahead, srcs, rest)

    def parts(self, x, hi, lo, *toks, q=None, copy=None):
        t = (copy or self.act).do(lambda e: e.copy(hi, x) if copy is None else e.tensor_copy(hi, x), *toks)
        return t, self.tt(lo, x, hi.bitcast(F), ALU.subtract, t, *toks, q=q)

    def mm3(self, out, trios, *toks, start=True, stop=True):
        pairs = []
        for (wh, wl), (xh, xl) in trios:
            pairs += [(wh, xh), (wh, xl), (wl, xh)]
        return self.mm(out, pairs, *toks, start=start, stop=stop)

    def proj3(self, x, segs, *toks, M=128):
        hi, lo, tw, s = self.stream.next()
        out = []
        for a, b in segs:
            bank, ids, rel = self.ps.take()
            t = self.mm3(bank[:, 0:b - a], [((hi[:, 128 * k:128 * k + 128], lo[:, 128 * k:128 * k + 128]), x(k, a, b))
                                            for k in range(8)], tw, rel, *toks)
            out.append((bank, ids, t))
        self.stream.free(s, t)
        return out

    def load(self, out, src, *toks):
        return self.pool.dma(out, src, self.dsem(), self.floor, *toks)

    def mm(self, out, pairs, *toks, start=True, stop=True, mark=True):
        self.pe.wait(*toks)
        n = len(pairs)
        for i, (l, r) in enumerate(pairs):
            s0, s1 = start and i == 0, stop and i == n - 1
            f = lambda e, l=l, r=r, s0=s0, s1=s1: e.matmul(out, l, r, start=s0, stop=s1, skip_group_check=True)
            if mark and i == n - 1:
                return self.pe.do(f)
            self.pe.quiet(f)

    def tr(self, out, in_, *toks, mark=True):
        k = in_.shape[0]
        p0 = in_.start_partition if not callable(in_.start_partition) else in_.start_partition()
        ident = self.sq["ident"][p0:p0 + k, p0:p0 + k]
        f = lambda e: e.transpose(out, in_, ident)
        return self.pe.do(f, *toks) if mark else self.pe.quiet(f, *toks)

    def tt(self, out, a, b, op, *toks, q=None):
        return (q or self.dve).do(lambda e: e.tensor_tensor(out, a, b, op), *toks)

    def ts(self, out, a, s1, s2, op0, op1, *toks, q=None):
        if op1 is None:
            return (q or self.dve).do(lambda e: e.tensor_scalar(out, a, s1, None, op0), *toks)
        return (q or self.dve).do(lambda e: e.tensor_scalar(out, a, s1, s2, op0, op1), *toks)

    def stt(self, out, a, s, b, op0, op1, *toks):
        return self.dve.do(lambda e: e.scalar_tensor_tensor(out=out, in0=a, scalar=s, in1=b, op0=op0, op1=op1), *toks)

    def cp(self, out, a, *toks, q=None):
        return (q or self.dve).do(lambda e: e.tensor_copy(out, a), *toks)

    def red(self, out, a, op, *toks):
        return self.dve.do(lambda e: e.tensor_reduce(out, a, AX, op), *toks)

    def rec(self, out, a, *toks):
        return self.dve.do(lambda e: e.reciprocal(out, a), *toks)

    def zero(self, out, *toks, q=None):
        return (q or self.pool).do(lambda e: e.memset(out, 0.0), *toks)

    def ac(self, out, a, func, *toks, scale=1.0, bias=None, accum=None):
        def f(e):
            kw = {}
            if bias is not None:
                kw["bias"] = bias
            if accum is not None:
                kw["accum_out"] = accum
            return e.activation(out, a, func, scale=scale, **kw)
        return self.act.do(f, *toks)

    def acp(self, out, a, *toks):
        return self.act.do(lambda e: e.copy(out, a), *toks)

    def proj(self, units, rhs, segs, M=128, toks=(), p0=0):
        got = [self.ring.take(u, w) for u, w in units]
        out = []
        for a, b in segs:
            bank, ids, rel = self.ps.take()
            pairs = []
            for ui, (w, _, _) in enumerate(got):
                m = M
                nk = units[ui][1] // m
                pairs += [(w[:, k * m:(k + 1) * m], rhs(8 * ui + k, a, b)) for k in range(nk)]
            t = self.mm(bank[p0:p0 + M, 0:b - a], pairs, [g[1] for g in got], rel, *toks)
            out.append((bank, ids, t))
        for g in got:
            self.ring.free(g[2], out[-1][2])
        return out

    def rms(self, src, n, out, tmp, mean, eps, segs, *toks):
        banks = [self.ps.take() for _ in segs]
        t = None
        free = [self.pe.last()] * 2
        for k in range(n):
            s = tmp[k % 2]
            t = self.act.do(lambda e, s=s, x=src(k): e.square(s, x), free[k % 2], *toks)
            for i, (a, b) in enumerate(segs):
                f = lambda e, i=i, a=a, b=b, s=s, k=k: e.matmul(banks[i][0][:, 0:b - a], mean, s[:, a:b],
                                                               start=(k == 0), stop=(k == n - 1), skip_group_check=True)
                free[k % 2] = self.pe.do(f, t, banks[i][2])
        r = []
        for i, (a, b) in enumerate(segs):
            o = out[:, a:b]
            u = self.ts(o, banks[i][0][:, 0:b - a], eps, None, ALU.add, None, free[(n - 1) % 2])
            self.ps.free(banks[i][1], u)
            u = self.ac(o, o, AF.Sqrt, u)
            u = self.rec(o, o, u)
            r.append(u)
        return r

    def setup(self):
        d, ar = self.d, self.ar
        nsq, nv, nr = len(SQ), sum(n for _, n in VECS), sum(n for _, n in ROWS)
        a = ar.take(nsq * 128)
        b = ar.take(nv)
        c = ar.take(nr)
        self.t_const = [self.load(a, d["squares"]), self.load(b, d["vecs"]), self.load(c, d["rows"])]
        for q in (self.pe, self.dve, self.act, self.pool):
            q.wait(self.t_const)
        self.sq = {n: a[:, 128 * i:128 * i + 128] for i, n in enumerate(SQ)}
        self.vec, self.row = {}, {}
        at = 0
        for n, w in VECS:
            self.vec[n] = b[:, at:at + w]
            at += w
        at = 0
        for n, w in ROWS:
            self.row[n] = c[:, at:at + w]
            at += w
        self.mods = [ar.take(96) for _ in range(3)]
        self.gain_l, self.gain_c = ar.take(8), ar.take(8)
        ar.at += -ar.at % 8
        self.base = ar.at

    def modulation(self, n, wname, i0, bias, cb, junk):
        mod = v3(self.mods[n], 2)
        state = {"junk": None}

        def step(j, both):
            w, tw, s = self.ring.take(self.d[wname][i0 + j])
            t = None
            if both:
                o, (c, tc) = mod[:, j, 1:2], cb[1]
                t = state["junk"] = self.dve.do(
                    lambda e: e.tensor_tensor_reduce(junk, w, c, 1.0, 0.0, ALU.mult, ALU.add, o), tw, tc, state["junk"])
            o2, (c2, tc2) = mod[:, j, 0:1], cb[0]
            t = self.dve.do(lambda e: e.tensor_tensor_reduce(w, w, c2, 1.0, 0.0, ALU.mult, ALU.add, o2), tw, tc2, t)
            self.ring.free(s, t)

        def done(a, b, both):
            t = self.dve.last()
            for s in range(2 if both else 1):
                u = self.tt(mod[:, a:b, s], mod[:, a:b, s], bias[:, a:b], ALU.add, t)
            return u

        return mod, step, done

    def condition(self, out, i):
        t = self.load(out, self.d["crow"][i])
        return out, self.ac(out, out, AF.Silu, t)

    def gains(self, out, mod, t, j0, g, s):
        return self.stt(out, mod[:, j0:j0 + 8, s], 1.0, g, ALU.add, ALU.mult, t)

    def in_projection(self):
        d, ar, V, S = self.d, self.ar, self.vec, self.sq
        gl, gc = self.gain_l, self.gain_c
        ar.at = self.base
        fT = ar.take(4096)
        zT = ar.take(4096)
        xl = ar.take(4096)
        BT, CT = ar.take(2048), ar.take(2048)
        self.small = ar.take(1600)
        self.Sprev = ar.take(8192)
        self.rest = ar.at
        xc, Btok = ar.take(2048), ar.take(3072)
        fc = self.Sprev[:, 0:2048]
        sqt = [self.Sprev[:, 2048 + 768 * i:2816 + 768 * i] for i in range(2)]
        rstd = self.Sprev[:, 3584:4352]
        raws = [self.Sprev[:, 4352 + 776 * i:5128 + 776 * i] for i in range(2)]
        accs = [self.Sprev[:, 5904 + 768 * i:6672 + 768 * i] for i in range(2)]
        sil = [ar.take(768) for i in range(2)]
        cb0 = self.condition(ar.take(1024), 0)
        cb1 = self.condition(zT[:, 0:1024], 1)
        m, step, done = self.modulation(0, "wmod", 0, V["bmod"], [cb0, cb1], zT[:, 1024:2048])
        self.mod1 = m
        for j in range(16):
            step(j, True)
        tm = done(0, 16, True)
        tg = [self.gains(gl, m, tm, 8, V["norm1"], 0), self.gains(gc, m, tm, 8, V["norm1"], 1)]
        f3, c3 = v3(fT, 512), v3(fc, 256)
        th = [self.load(f3, d["xT"]), self.load(c3, d["ctxT"])]
        tz = [self.zero(r) for r in raws]

        for lo, hi, src, g, s in ((0, 512, f3, gl, 0), (512, 768, c3, gc, 1)):
            r = self.rms(lambda k: src[:, k, :], 8, rstd[:, lo:hi], [q[:, 0:hi - lo] for q in sqt], S["m1024"], EPS,
                         [(0, hi - lo)], th)
            for k in range(8):
                t = self.tt(src[:, k, :], src[:, k, :], rstd[:, lo:hi], ALU.mult, r, th)
                t = self.ac(src[:, k, :], src[:, k, :], AF.Identity, t, tg, scale=g[:, k:k + 1], bias=m[:, k, s:s + 1])
        tf = self.act.last()
        self.fT, self.tf = f3, tf
        seg2, seg1 = [(0, 512), (512, 768)], [(0, 512)]
        rhs = lambda k, a, b: f3[:, k, :] if a == 0 else c3[:, k, :]

        z3 = v3(zT, 512)
        for j in range(8):
            (bank, ids, t), = self.proj([(d["win"][j], 1024)], rhs, seg1, toks=(tf,))
            t = self.ac(z3[:, j, :], bank, AF.Silu, t, tm)
            self.ps.free(ids, t)
            step(16 + j, False)

        xl3, xc3, B3, C3, Bt3 = v3(xl, 1024), v3(xc, 1024), v3(BT, 512), v3(CT, 512), v3(Btok, 512)
        tr_free = [None, None]
        raw_free, acc_free = [[tz], [tz]], [[], []]

        def turn(j, i, lat, si, t):
            bank, ids, rel = self.ps.take(2)
            for q in range(6):
                src = lat[:, 128 * q:128 * q + 128] if q < 4 else si[:, 128 * q:128 * q + 128]
                t2 = self.tr(bank[:, 128 * q:128 * q + 128], src, t, rel, mark=(q == 5))
            tr_free[i] = [t2]
            if j < 8:
                c0 = slice(128 * j, 128 * j + 128)
                u = [self.cp(xl3[:, :, c0], v3(bank[:, 0:512], 128), t2), self.cp(xc3[:, :, c0], v3(bank[:, 512:768], 128), t2)]
            else:
                c0 = slice(128 * (j - 8), 128 * (j - 8) + 128)
                u = [self.cp(Bt3[:, :, c0], v3(bank[:, 0:768], 128), t2)]
            self.ps.free(ids, u)

        lag = []
        for j in range(16):
            i = j % 2
            raw, acc, si = raws[i], accs[i], sil[i]
            segs = seg2 if j < 12 else seg1
            got = self.proj([(d["win"][8 + j], 1024)], rhs, segs, toks=(tf,))
            tc = []
            for (bank, ids, t), off, n in zip(got, (2, 518), (512, 256)):
                t = self.acp(raw[:, off:off + n], bank[:, 0:n], t, raw_free[i])
                self.ps.free(ids, t)
                tc.append(t)
            w = V["convw"][:, 5 * j:5 * j + 5]
            last = []
            for lo, n, base in ((0, 512, 0), (512, 256, 516))[:len(segs)]:
                a = acc[:, lo:lo + n]
                t = self.ts(a, raw[:, base:base + n], w[:, 0:1], V["convb"][:, j:j + 1], ALU.mult, ALU.add,
                            tc, acc_free[i])
                for k in range(1, 5):
                    t = self.stt(a, raw[:, base + k:base + k + n], w[:, k:k + 1], a, ALU.mult, ALU.add, t)
                last.append(t)
            raw_free[i] = last
            step(24 + j, False)
            if j >= 12:
                acc_free[i] = [self.ac(C3[:, j - 12, :], acc[:, 0:512], AF.Silu, last)]
                if lag:
                    turn(*lag.pop(0))
                continue
            if j < 8:
                t = self.ac(si, acc, AF.Silu, last, tr_free[i])
                acc_free[i], lat = [t], si[:, 0:512]
            else:
                t = self.ac(B3[:, j - 8, :], acc[:, 0:512], AF.Silu, last)
                t = self.ac(si[:, 512:768], acc[:, 512:768], AF.Silu, t, tr_free[i])
                acc_free[i], lat = [t], B3[:, j - 8, :]
            lag.append((j, i, lat, si, t))
            if len(lag) > 1:
                turn(*lag.pop(0))
        for j in range(40, 48):
            step(j, False)
        done(16, 48, False)

        sm = self.small
        dtT = sil[0][0:32, :]
        got = self.proj([(d["wdt"], 256)], rhs, seg2, M=32, toks=(tf,))
        t2 = []
        for (bank, ids, t), (a, b) in zip(got, seg2):
            u = self.ts(dtT[:, a:b], bank[0:32, 0:b - a], V["dtb"][0:32, :], None, ALU.add, None, t, tr_free[0])
            self.ps.free(ids, u)
            t2.append(u)
        bank, ids, rel = self.ps.take()
        for q in range(6):
            t = self.tr(bank[:, 32 * q:32 * q + 32], dtT[:, 128 * q:128 * q + 128], t2, rel)
        x, e, s, q, p, dt, a, A = (sm[:, 192 * i:192 * i + 192] for i in range(8))
        t = self.cp(x, bank[:, 0:192], t)
        self.ps.free(ids, t)
        t = self.stt(e, x, -1.0, x, ALU.mult, ALU.max, t)
        t = self.ac(e, e, AF.Exp, t, scale=-1.0)
        t = self.ts(s, e, 2.0, None, ALU.add, None, t)
        t = self.rec(s, s, t)
        t = self.tt(s, s, e, ALU.mult, t)
        t = self.tt(q, s, s, ALU.mult, t)
        t = self.ts(p, q, 1.0 / 17, None, ALU.mult, None, t)
        for n in (15, 13, 11, 9, 7, 5, 3):
            t = self.stt(p, p, 1.0 / n, q, ALU.add, ALU.mult, t)
        t = self.stt(p, p, 1.0, s, ALU.add, ALU.mult, t)
        t = self.ts(x, x, 0.0, None, ALU.max, None, t)
        t = self.stt(dt, p, 2.0, x, ALU.mult, ALU.add, t)
        A = A[:, 0:32]
        u = self.ac(A, self.row["alog"], AF.Exp)
        u = self.ts(A, A, -1.0, None, ALU.mult, None, u)
        t = self.tt(v3(a, 32), v3(dt, 32), bc(A, 1, [128, 6, 32]), ALU.mult, t, u)
        self.dt, self.a = v3(dt, 32), v3(a, 32)
        self.zT, self.xl, self.xc, self.BT, self.CT, self.Btok = z3, xl3, xc3, B3, C3, Bt3
        return t

    def ssd(self):
        V, S, ar, sm = self.vec, self.sq, self.ar, self.small
        self.fence()
        dt, a = self.dt, self.a
        E = sm[:, 0:576]
        wd = sm[:, 576:768]
        b0, i0, r0 = self.ps.take()
        b1, i1, r1 = self.ps.take()
        masks = ["le", "ge", "gt", "lt", "ones", "ones"]
        for n, mk in enumerate(masks):
            o = b0[:, 96 * n:96 * n + 96] if n < 5 else b1[:, 0:96]
            t = self.mm(o, [(S[mk], a[:, :, 16 * (n % 2):16 * (n % 2) + 16])], r0, r1)
        u = [self.ac(E[:, 0:480], b0[:, 0:480], AF.Exp, t), self.ac(E[:, 480:576], b1[:, 0:96], AF.Exp, t)]
        self.ps.free(i0, u)
        self.ps.free(i1, u)
        E5 = E.rearrange("p (k d c h) -> p k d c h", k=3, d=2, c=6)
        wd4 = wd.rearrange("p (d c h) -> p d c h", d=2, c=6)
        tw = []
        for k in range(2):
            tw.append(self.tt(wd4[:, k], dt[:, :, 16 * k:16 * k + 16], E5[:, 1, k], ALU.mult, u))
        ar.at = self.rest + 5120
        xws = [ar.take(1024) for _ in range(2)]
        Sp = self.Sprev.rearrange("p (d c n) -> p d c n", d=2, c=4)
        xw_free = [None, None]
        n = 0
        t_s = []
        for k, order in ((0, (4, 5, 0, 1, 2)), (1, (5, 4, 3, 2, 1))):
            prev, cur, tp = None, (0 if k == 0 else 3), None
            for step, c in enumerate(order):
                xw = xws[n % 2]
                xs = self.xl[:, c, :] if c < 4 else self.xc[:, c - 4, :]
                t = self.tt(v3(xw, 64), v3(xs, 64), bc(wd4[:, k, c], 2, [128, 16, 64]), ALU.mult, tw, xw_free[n % 2],
                            q=self.pool)
                bank, ids, rel = self.ps.take(2)
                for g in range(4):
                    t2 = self.mm(bank[:, 256 * g:256 * g + 256],
                                 [(self.Btok[:, c, 128 * g:128 * g + 128], xw[:, 256 * g:256 * g + 256])], t, rel,
                                 mark=(g == 3))
                xw_free[n % 2] = t2
                n += 1
                if step >= 2:
                    prev, cur = cur, cur + (1 if k == 0 else -1)
                else:
                    prev = cur
                dst = Sp[:, k, cur, :]
                if step == 0:
                    tp = self.cp(dst, bank, t2)
                else:
                    tp = self.tt(v3(dst, 64), v3(Sp[:, k, prev, :], 64), bc(E5[:, 2, k, c], 2, [128, 16, 64]), ALU.mult,
                                 tp, u)
                    tp = self.tt(dst, dst, bank, ALU.add, tp, t2)
                self.ps.free(ids, tp)
            t_s.append(tp)
        self.fence()
        ar.at = self.rest
        CB = [ar.take(512) for _ in range(2)]
        xd = [ar.take(1024) for _ in range(2)]
        aL = [ar.take(512) for _ in range(2)]
        M = [ar.take(512) for _ in range(4)]
        ys = [ar.take(1024) for _ in range(2)]
        tmp = ar.take(1024)
        aL_free, M_free, y_free = [None] * 2, [None] * 4, [None] * 2
        mk = [("le", "gt", "le"), ("ge", "lt", "ge")]
        t_xd, t_y, t_z = None, None, None
        for c in range(4):
            cs = slice(128 * c, 128 * c + 128)
            bank, ids, rel = self.ps.take()
            for g in range(4):
                t = self.mm(bank[:, 128 * g:128 * g + 128], [(self.BT[:, g, cs], self.CT[:, g, cs])], rel, mark=(g == 3))
            tcb = [self.tt(v3(CB[k], 128), v3(bank, 128), bc(S[mk[k][0]], 1, [128, 4, 128]), ALU.mult, t, M_free)
                   for k in range(2)]
            self.ps.free(ids, tcb)
            txd = [self.tt(v3(xd[k], 64), v3(self.xl[:, c, :], 64), bc(dt[:, c, 16 * k:16 * k + 16], 2, [128, 16, 64]),
                           ALU.mult, t_xd, q=self.pool) for k in range(2)]
            y = ys[c % 2]
            offs = []
            for k in range(2):
                bank, ids, rel = self.ps.take(2)
                for g in range(4):
                    t = self.mm(bank[:, 256 * g:256 * g + 256], [(self.CT[:, g, cs], Sp[:, k, c, 256 * g:256 * g + 256])],
                                rel, mark=(g == 3))
                offs.append((bank, ids, t))
            (bf, idf, tf), (bb, idb, tb) = offs
            ty = self.tt(v3(y, 64), v3(bf, 64), bc(E5[:, 0, 0, c], 2, [128, 16, 64]), ALU.mult, tf, y_free[c % 2])
            self.ps.free(idf, ty)
            tt2 = self.tt(v3(tmp, 64), v3(bb, 64), bc(E5[:, 0, 1, c], 2, [128, 16, 64]), ALU.mult, tb, t_y)
            self.ps.free(idb, tt2)
            ty = self.tt(y, y, tmp, ALU.add, ty, tt2)
            tt2 = self.tt(v3(tmp, 64), v3(self.xl[:, c, :], 64), bc(self.row["dskip"], 2, [128, 16, 64]), ALU.mult, ty)
            ty = self.tt(y, y, tmp, ALU.add, tt2)
            t_y = ty
            yb, idy, rely = self.ps.take(2)
            for g in range(4):
                tms = []
                for k in range(2):
                    h0 = 16 * k + 4 * g
                    t = self.tt(v3(aL[k], 128), bc(S[mk[k][1]], 1, [128, 4, 128]), bc(a[:, c, h0:h0 + 4], 2, [128, 4, 128]),
                                ALU.mult, aL_free[k], q=self.pool)
                    bank, ids, rel = self.ps.take()
                    for h in range(4):
                        t2 = self.mm(bank[:, 128 * h:128 * h + 128], [(aL[k][:, 128 * h:128 * h + 128], S[mk[k][2]])], t, rel,
                                     mark=(h == 3))
                    aL_free[k] = t2
                    mi = 2 * (g % 2) + k
                    t = self.ac(M[mi], bank, AF.Exp, t2, M_free[mi])
                    self.ps.free(ids, t)
                    tms.append(self.tt(v3(M[mi], 128), v3(M[mi], 128), bc(CB[k][:, 128 * g:128 * g + 128], 1, [128, 4, 128]),
                                       ALU.mult, t, tcb))
                for h in range(4):
                    o = slice(256 * g + 64 * h, 256 * g + 64 * h + 64)
                    t = self.mm(yb[:, o], [(M[2 * (g % 2) + k][:, 128 * h:128 * h + 128], xd[k][:, o]) for k in range(2)],
                                tms, txd, rely, mark=(h == 3))
                M_free[2 * (g % 2)] = M_free[2 * (g % 2) + 1] = t
            t_xd = t
            ty = self.tt(y, y, yb, ALU.add, t, ty)
            self.ps.free(idy, ty)
            for i in range(2):
                bank, ids, rel = self.ps.take()
                for q in range(4):
                    f = 4 * i + q
                    t = self.tr(bank[:, 128 * q:128 * q + 128], y[:, 128 * f:128 * f + 128], ty, rel, mark=(q == 3))
                z = self.zT[:, 4 * i:4 * i + 4, cs]
                u = self.tt(z, z, v3(bank, 128), ALU.mult, t)
                self.ps.free(ids, u)
            y_free[c % 2] = t
        for g in range(4):
            sq = [tmp[:, 0:512], tmp[:, 512:1024]]
            r = self.rms(lambda k: self.zT[:, 2 * g + k, :], 2, M[g], sq, S["m256"], EPS, [(0, 512)], u, self.dve.last(),
                         self.pe.last())
            for k in range(2):
                z = self.zT[:, 2 * g + k, :]
                u = self.stt(z, z, V["ssd_norm"][:, 2 * g + k:2 * g + k + 1], M[g], ALU.mult, ALU.mult, r)
        return u

    def hyena(self):
        d, ar, V, S = self.d, self.ar, self.vec, self.sq
        self.fence()
        ar.at = self.base + 8192
        vT, x1, x2 = ar.take(4096), ar.take(4096), ar.take(4096)
        Cm, Sm = ar.take(2048), ar.take(2048)
        IS0, NY = ar.take(512), ar.take(512)
        top = ar.at
        raws = [ar.take(516) for _ in range(2)]
        accs = [ar.take(512) for _ in range(2)]
        C3, S3 = v3(Cm, 512), v3(Sm, 512)
        tdft = [self.load(C3, d["dftc"]), self.load(S3, d["dfts"]), self.load(IS0, d["is0"]), self.load(v3(NY, 128), d["nyq"])]
        tz = [self.zero(r, *self.floor) for r in raws]
        dst = [v3(q, 512) for q in (vT, x1, x2)]
        v, x1, x2 = dst
        raw_free = [tz, tz]
        rhs = lambda k, a, b: self.fT[:, k, :]
        for j in range(24):
            i = j % 2
            (bank, ids, t), = self.proj([(d["win"][24 + j], 1024)], rhs, [(0, 512)])
            t = self.acp(raws[i][:, 2:514], bank, t, raw_free[i])
            self.ps.free(ids, t)
            w = V["hyw"][:, 3 * j:3 * j + 3]
            o = dst[j // 8][:, j % 8, :]
            t = self.ts(accs[i], raws[i][:, 1:513], w[:, 0:1], V["hyb"][:, j:j + 1], ALU.mult, ALU.add, t)
            t = self.stt(accs[i], raws[i][:, 2:514], w[:, 1:2], accs[i], ALU.mult, ALU.add, t)
            t = self.stt(o, raws[i][:, 3:515], w[:, 2:3], accs[i], ALU.mult, ALU.add, t)
            raw_free[i] = [t]
        self.fence()
        ar.at = top
        h1, h2 = ar.take(512), ar.take(512)
        e, o = v3(ar.take(2048), 512), v3(ar.take(2048), 512)
        Kr, Ki = v3(ar.take(2048), 512), v3(ar.take(2048), 512)
        at2 = ar.at
        ar.at = self.base
        ut = v3(ar.take(2048), 512)
        P, Q = ar.take(512), ar.take(512)
        W = [ar.take(512) for _ in range(2)]
        ar.at = at2
        W += [ar.take(512) for _ in range(2)]
        zp, tzp, sz = self.ring.take(d["zpos"], 512, parts=33)
        w12, tw, sw = self.ring.take(d["hyw12"], 128, parts=64)

        def sine(out, bank, t, b, fr):
            t = self.ts(h1[0:64, :], bank[0:64, :], b[0:64, :], fr[0:64, :], ALU.add, ALU.mult, t)
            t = self.ts(P[0:64, :], h1[0:64, :], 1.0 / (2 * math.pi), 12582912.0, ALU.mult, ALU.add, t)
            t = self.ts(P[0:64, :], P[0:64, :], 12582912.0, None, ALU.subtract, None, t)
            for cst in (6.28125, 0.0019340515136718750, 2 * math.pi - 6.28125 - 0.0019340515136718750):
                t = self.stt(h1[0:64, :], P[0:64, :], -cst, h1[0:64, :], ALU.mult, ALU.add, t)
            t = self.ts(h1[0:64, :], h1[0:64, :], 3.1415925, -3.1415925, ALU.min, ALU.max, t)
            return self.ac(out[0:64, :], h1[0:64, :], AF.Sin, t)

        bank, ids, rel = self.ps.take()
        t = self.mm(bank[0:64, :], [(w12[0:33, 0:64], zp)], tzp, tw, rel)
        self.ring.free(sz, t)
        t = sine(h2, bank, t, V["hyb1"], V["fr0"])
        self.ps.free(ids, self.dve.last())
        bank, ids, rel = self.ps.take()
        t = self.mm(bank[0:64, :], [(w12[0:64, 64:128], h2[0:64, :])], t, rel)
        self.ring.free(sw, t)
        th2 = sine(h2, bank, t, V["hyb2"], V["fr1"])
        self.ps.free(ids, self.dve.last())
        self.pe.wait(tdft)

        K_free, e_free, u_free = [None], [None], [None]
        for hf in range(2):
            for od in range(2):
                w3, tw3, s3 = self.ring.take(d["hyw3"][od, hf], parts=64)
                decs = [self.ring.take(d["dec"][hf, i]) for i in range(2)]
                tPQ = [self.pool.last()]
                for tt in range(4):
                    dec = decs[tt // 2]
                    dm = dec[0][:, 512 * (tt % 2):512 * (tt % 2) + 512]
                    tp = []
                    for buf, c0 in ((P, 0), (Q, 512)):
                        bank, ids, rel = self.ps.take()
                        t = self.mm(bank, [(h2[0:64, 128 * tt:128 * tt + 128], w3[:, c0:c0 + 512])], tw3, th2, rel)
                        u = self.tt(buf, bank, dm, ALU.mult, t, dec[1], tPQ)
                        self.ps.free(ids, u)
                        tp.append(u)
                    if tt == 0:
                        tp.append(self.zero(Q[0:1, :], tp, q=self.dve))
                    tPQ = [self.tt(e[:, tt, :], P, Q, ALU.add, tp, e_free, q=self.pool),
                           self.tt(o[:, tt, :], P, Q, ALU.subtract, tp, e_free, q=self.pool)]
                self.ring.free(s3, t)
                for i in range(2):
                    self.ring.free(decs[i][2], u)
                tk = []
                for ft in range(4):
                    fs = slice(128 * ft, 128 * ft + 128)
                    for Kx, Mx, x in ((Kr, C3, e), (Ki, S3, o)):
                        bank, ids, rel = self.ps.take()
                        pairs = [(Mx[:, tt, fs], x[:, tt, :]) for tt in range(4)]
                        if Kx is Ki and ft == 0:
                            pairs += [(NY[:, 128 * tt:128 * tt + 128], e[:, tt, :]) for tt in range(4)]
                        t = self.mm(bank, pairs, tPQ, rel)
                        u = self.act.do(lambda q, o_=Kx[:, ft, :], b_=bank: q.mul(o_, b_, 2.0 / 1024), t, K_free)
                        self.ps.free(ids, u)
                        if ft == 0:
                            u = self.ts(Kx[0:1, 0, :], Kx[0:1, 0, :], 0.5, None, ALU.mult, None, u)
                        tk.append(u)
                te = self.pe.last()
                tu = []
                for tt in range(4):
                    bank, ids, rel = self.ps.take()
                    for j in range(4):
                        src = v[:, 4 * hf + j, 128 * tt:128 * tt + 128]
                        t = self.tr(bank[:, 128 * j:128 * j + 128], src, rel, tu_in if od else None, mark=(j == 3))
                    u = self.acp(ut[:, tt, :], bank, t, u_free)
                    self.ps.free(ids, u)
                    tu.append(u)
                ty = []
                for ft in range(4):
                    fs = slice(128 * ft, 128 * ft + 128)
                    br, idr, rr = self.ps.take()
                    t1 = self.mm(br, [(C3[:, tt, fs], ut[:, tt, :]) for tt in range(4)], tu, rr)
                    bi, idi, ri = self.ps.take()
                    pairs = [(S3[:, tt, fs], ut[:, tt, :]) for tt in range(4)]
                    if ft == 0:
                        pairs += [(NY[:, 128 * tt:128 * tt + 128], ut[:, tt, :]) for tt in range(4)]
                    t2 = self.mm(bi, pairs, ri)
                    a1 = self.tt(W[0], br, Kr[:, ft, :], ALU.mult, t1, tk, ty, self.pool.last())
                    a2 = self.tt(W[1], bi, Ki[:, ft, :], ALU.mult, t2)
                    a3 = self.tt(W[2], br, Ki[:, ft, :], ALU.mult)
                    a4 = self.tt(W[3], bi, Kr[:, ft, :], ALU.mult)
                    self.ps.free(idr, a3)
                    self.ps.free(idi, a4)
                    y1 = self.tt(e[:, ft, :], W[0], W[1], ALU.subtract, a4, te, q=self.pool)
                    y2 = self.tt(o[:, ft, :], W[2], W[3], ALU.add, a4, q=self.pool)
                    if ft == 0:
                        y1 = self.cp(e[0:1, 0, :], W[0][0:1, :], y1, y2)
                        y2 = self.cp(o[0:1, 0, :], W[1][0:1, :], y1, y2)
                    ty += [y1, y2]
                K_free = [self.dve.last()]
                u_free = [t2]
                outs = []
                for j in range(4):
                    bank, ids, rel = self.ps.take()
                    js = slice(128 * j, 128 * j + 128)
                    pairs = [(e[:, ft, js], C3[:, ft, :]) for ft in range(4)]
                    pairs += [(o[:, ft, js], S3[:, ft, :] if ft else IS0) for ft in range(4)]
                    t = self.mm(bank, pairs, ty, rel)
                    m = 4 * hf + j
                    hb = V["hbias"][:, 8 * od + m:8 * od + m + 1]
                    turned = v[:, m, :].rearrange("p (c r) -> p r c", r=8)
                    if od == 0:
                        u = self.stt(W[j], v[:, m, :], hb, bank, ALU.mult, ALU.add, t)
                        self.ps.free(ids, u)
                        outs.append(self.tt(turned, v3(W[j], 64), v3(x1[:, m, :], 64), ALU.mult, u))
                    else:
                        u = self.stt(v[:, m, :], v[:, m, :], hb, bank, ALU.mult, ALU.add, t)
                        self.ps.free(ids, u)
                        outs.append(self.tt(v3(x2[:, m, :], 64), v3(x2[:, m, :], 64), turned, ALU.mult, u))
                e_free = [t]
                tu_in = outs
        for m in range(8):
            sq = [W[0], W[1]]
            r = self.rms(lambda k: x2[:, m, :], 1, P if m % 2 else Q, [sq[m % 2]] * 2, S["m64"], EPS, [(0, 512)],
                         self.dve.last(), self.pe.last())
            z = x2[:, m, :]
            u = self.stt(z, z, V["hy_norm"][:, m:m + 1], P if m % 2 else Q, ALU.mult, ALU.mult, r)
        self.x2 = x2
        return u

    def out_projection(self, t):
        d, ar = self.d, self.ar
        self.fence()
        ar.at = self.base
        keep = ar.at
        ar.at = self.base + 8192
        h = v3(ar.take(4096), 512)
        th = self.load(h, d["xT"])
        for j in range(8):
            rhs = lambda k, a, b: self.zT[:, k, :] if k < 8 else self.x2[:, k - 8, :]
            (bank, ids, t), = self.proj([(d["wout"][j, i], 1024) for i in range(2)], rhs, [(0, 512)])
            t = self.stt(h[:, j, :], bank, self.mod1[:, 16 + j, 0:1], h[:, j, :], ALU.mult, ALU.add, t, th)
            self.ps.free(ids, t)
        self.h = h
        return t

    def peer(self, t):
        d, ar, V, S = self.d, self.ar, self.vec, self.sq
        m, h = self.mod1, self.h
        self.fence()
        ar.at = self.base
        fh, fl = [ar.rounded(512) for _ in range(8)], [ar.rounded(512) for _ in range(8)]
        ar.at = self.base + 12288
        low = ar.at
        self.rings(4, 4, 2, [(d["wq"][n], 1024) for n in range(16)], lambda i: self.pool)
        sqt = [ar.take(512) for _ in range(2)]
        rstd, g2 = ar.take(512), ar.take(8)
        ft = [ar.take(512) for _ in range(2)]
        tg = self.gains(g2, m, None, 32, V["norm2"], 0)
        r = self.rms(lambda k: h[:, k, :], 8, rstd, sqt, S["m1024"], EPS, [(0, 512)], t)
        tf, free = [], [None, None]
        for k in range(8):
            x = ft[k % 2]
            t = self.tt(x, h[:, k, :], rstd, ALU.mult, r, free[k % 2])
            t = self.ac(x, x, AF.Identity, t, tg, scale=g2[:, k:k + 1], bias=m[:, 24 + k, 0:1])
            free[k % 2] = self.parts(x, fh[k], fl[k], t)[1]
            tf.append(free[k % 2])
        fx = lambda k, a, b: (fh[k][:, a:b], fl[k][:, a:b])
        self.fence()
        ar.at = low
        EG = [ar.take(512) for _ in range(3)]
        kt = ar.take(256)
        tk = self.load(kt, d["subkeys"])
        at1 = ar.at
        qs = [ar.take(512) for _ in range(2)]
        sc = [ar.take(512) for _ in range(3)]
        s2 = [ar.take(512) for _ in range(2)]
        val, idx = v3(ar.take(1024), 256), v3(ar.take(1024).bitcast(U32), 256)
        fidx = v3(ar.take(1024), 256)
        q_free, sc_free = [None, None], [None] * 3
        lag, ti = [], []

        def scores(n, t):
            q = qs[n % 2]
            bank, ids, rel = self.ps.take()
            for tt in range(4):
                t2 = self.mm(bank[:, 128 * tt:128 * tt + 128],
                             [(q[:, 128 * tt:128 * tt + 128], kt[:, 128 * (n % 2):128 * (n % 2) + 128])], t, tk, rel,
                             mark=(tt == 3))
            q_free[n % 2] = t2
            s = sc[n % 3]
            u = self.acp(s, bank, t2, sc_free[n % 3])
            self.ps.free(ids, u)
            groups = [(s[:, 128 * tt:128 * tt + 128], val[:, tt, 16 * n:16 * n + 16], idx[:, tt, 16 * n:16 * n + 16],
                       s2[n % 2][:, 128 * tt:128 * tt + 128]) for tt in range(4)]
            sc_free[n % 3] = self.top16(groups, u)

        for n in range(16):
            (bank, ids, t), = self.proj3(fx, [(0, 512)], tf)
            t = self.acp(qs[n % 2], bank, t, q_free[n % 2])
            self.ps.free(ids, t)
            lag.append((n, t))
            if n:
                scores(*lag.pop(0))
        scores(*lag.pop(0))
        t = self.cp(fidx, idx, sc_free[0])
        cand, oh = ar.take(2048), ar.take(2048)
        best, ci, hi, hf = ar.take(128), ar.take(128).bitcast(U32), ar.take(128).bitcast(U32), ar.take(128)
        mx, esel, gate = ar.take(8), ar.take(256), ar.take(128)
        at2 = ar.at
        ar.at = at1
        NO = 12
        o1 = [ar.take(128) for _ in range(NO)]
        o2 = [ar.take(128) for _ in range(NO)]
        ar.at = at2
        stage = [ar.take(4096) for _ in range(2)]
        f1, st_free = [None] * NO, [None] * 2
        gd = d["gates"]
        t_w = []
        self.fence()

        def choose(tt):
            t = self.dve.last()
            v4_ = val[:, tt, :].rearrange("p (h s k) -> p h s k", h=8, s=2)
            f4 = fidx[:, tt, :].rearrange("p (h s k) -> p h s k", h=8, s=2)
            ts = []
            for hd in range(8):
                c = cand[:, 256 * hd:256 * hd + 256]
                ts.append(self.tt(v3(c, 16), bc(v4_[:, hd, 0, :], 2, [128, 16, 16]), bc(v4_[:, hd, 1, :], 1, [128, 16, 16]),
                                  ALU.add, t))
            groups = [tuple(x[:, w * hd:w * hd + w] for x, w in ((cand, 256), (best, 16), (ci, 16), (oh, 256)))
                      for hd in range(8)]
            t = self.top16(groups, ts[-1])
            b3, g3 = v3(best, 16), v3(gate, 16)
            tg = self.tt(g3, b3, b3[:, :, 0:1].to_broadcast([128, 8, 16]), ALU.subtract, t, self.pe.last())
            tg = self.ac(gate, gate, AF.Exp, tg)
            o4 = v4(oh, 16, 16)
            for s in range(2):
                if s == 0:
                    t = self.ts(hi, ci, 4, None, ALU.logical_shift_right, None, t)
                else:
                    t = self.ts(hi, ci, 15, None, ALU.bitwise_and, None, t)
                t = self.cp(hf, hi, t)
                h3 = v3(hf, 16)
                t = self.tt(o4, bc(h3, 3, [128, 8, 16, 16]), self.row["i16"].unsqueeze(1).unsqueeze(1).to_broadcast(
                    [128, 8, 16, 16]), ALU.is_equal, t)
                t = self.tt(o4, o4, bc(f4[:, :, s, :], 2, [128, 8, 16, 16]), ALU.mult, t)
                t = self.red(esel[:, 128 * s:128 * s + 128], v3(oh, 16), ALU.add, t)
            tg = self.red(mx, g3, ALU.add, tg)
            tg = self.rec(mx, mx, tg)
            tg = self.tt(g3, g3, bc(mx, 2, [128, 8, 16]), ALU.mult, tg)
            bank, ids, rel = self.ps.take()
            for i, src in enumerate((esel[:, 0:128], esel[:, 128:256], gate)):
                t2 = self.tr(bank[:, 128 * i:128 * i + 128], src, t, tg, rel, mark=(i == 2))
            us = [self.cp(EG[i][:, 128 * tt:128 * tt + 128], bank[:, 128 * i:128 * i + 128], t2) for i in range(3)]
            self.ps.free(ids, us)
            return us[-1]

        def spread(ch, te):
            sg = v3(stage[ch % 2], 32)
            tcp = []
            for q in range(8):
                bank, ids, rel = self.ps.take()
                for i in range(4):
                    tk = 32 * ch + 4 * q + i
                    n = tk % NO
                    ta = self.ts(o1[n], S["iota"], EG[0][:, tk:tk + 1], EG[2][:, tk:tk + 1], ALU.is_equal, ALU.mult, te, f1[n])
                    tb = self.ts(o2[n], S["iota"], EG[1][:, tk:tk + 1], None, ALU.is_equal, None, te, f1[n], q=self.pool)
                    tm = self.mm(bank[:, 128 * i:128 * i + 128], [(o2[n], o1[n])], ta, tb, rel)
                    f1[n] = tm
                u = self.acp(sg[:, :, 4 * q:4 * q + 4], bank.rearrange("p (t e) -> p e t", e=128), tm, st_free[ch % 2])
                self.ps.free(ids, u)
                tcp.append(u)
            w = self.sp.dma(gd[ch], stage[ch % 2], self.dsem(), tcp)
            st_free[ch % 2] = w
            t_w.append(w)

        for tt in range(4):
            te = choose(tt)
            for ch in range(4 * tt, 4 * tt + 4):
                spread(ch, te)
        self.fence(*t_w)
        ar.at = low
        NG = 32
        srcs = [(d["peeru"][n], 1024) for n in range(4)]
        for gi in range(NG):
            if gi + 1 < NG:
                srcs += [(d["peeru"][n], 1024) for n in range(4 * gi + 4, 4 * gi + 8)]
            srcs += [(d["peerv"][n], 1024) for n in range(4 * gi, 4 * gi + 4)]
        Ah, Al = [ar.rounded(512) for _ in range(8)], [ar.rounded(512) for _ in range(8)]
        gl, pr = [ar.take(512) for _ in range(3)], [ar.take(512) for _ in range(3)]
        Gb, Gs = [ar.take(2048) for _ in range(2)], [self.dsem() for _ in range(2)]
        steps = self.modulations2()
        self.rings(6, 6, 2, srcs, lambda i: self.pool)
        A_free, x_free, G_free = [None] * 8, [None] * 3, [[], []]
        tacc = [None] * 8
        tA, tG = {}, {}

        def fetch(gi):
            tG[gi] = self.sp.dma(v3(Gb[gi % 2], 128), gd[:, :, 128 * gi:128 * gi + 128].rearrange("c p x -> p c x"), Gs[gi % 2],
                                 G_free[gi % 2])

        def up(gi):
            if gi + 1 < NG:
                fetch(gi + 1)
            G4 = Gb[gi % 2].rearrange("p (c e t) -> p c e t", c=16, e=4)
            for i in range(4):
                n = 4 * gi + i
                (bank, ids, t), = self.proj3(fx, [(0, 512)])
                x, y = gl[n % 3], pr[n % 3]
                t = self.ac(x, bank, AF.Gelu, t, x_free[n % 3])
                self.ps.free(ids, t)
                t = self.tt(v3(y, 32), v3(x, 32), G4[:, :, i, :], ALU.mult, t, tG[gi])
                G_free[gi % 2] = [t]
                tA[n] = list(self.parts(y, Ah[n % 8], Al[n % 8], t, A_free[n % 8]))
                x_free[n % 3] = tA[n]

        def down(gi):
            ns = range(4 * gi, 4 * gi + 4)
            vs = [self.stream.next() for _ in ns]
            for j in range(8):
                bank, ids, rel = self.ps.take()
                js = slice(128 * j, 128 * j + 128)
                t = self.mm3(bank, [((w[0][:, js], w[1][:, js]), (Ah[n % 8], Al[n % 8])) for w, n in zip(vs, ns)],
                             [w[2] for w in vs], [tA[n] for n in ns], rel)
                tacc[j] = self.stt(h[:, j, :], bank, m[:, 40 + j, 0:1], h[:, j, :], ALU.mult, ALU.add, t, tacc[j])
                self.ps.free(ids, tacc[j])
            for n, w in zip(ns, vs):
                self.stream.free(w[3], t)
                A_free[n % 8] = t

        fetch(0)
        up(0)
        for gi in range(NG):
            if gi + 1 < NG:
                up(gi + 1)
            for step in steps[4 * gi:4 * gi + 4]:
                step()
            down(gi)
        self.fence()
        ar.at = low
        sqt = [ar.take(512) for _ in range(2)]
        rstd = ar.take(512)
        r = self.rms(lambda k: h[:, k, :], 8, rstd, sqt, S["m1024"], EPS, [(0, 512)], *tacc)
        for j in range(8):
            t = self.stt(h[:, j, :], h[:, j, :], V["final_norm"][:, j:j + 1], rstd, ALU.mult, ALU.mult, r)
        self.fence()
        self.rings(13)
        return t

    def top16(self, groups, t):
        D = self.dve.do
        t1 = [D(lambda e, a=a, v=v: e.max(v[:, 0:8], a), t) for a, v, x, tmp in groups]
        t2 = [D(lambda e, a=a, v=v, tmp=tmp: e.match_replace(tmp, v[:, 0:8], a, LOW), u)
              for (a, v, x, tmp), u in zip(groups, t1)]
        for a, v, x, tmp in groups:
            D(lambda e, a=a, v=v, x=x: e.max_index(x[:, 0:8], v[:, 0:8], a))
        t3 = [D(lambda e, v=v, tmp=tmp: e.max(v[:, 8:16], tmp), u) for (a, v, x, tmp), u in zip(groups, t2)]
        t4 = [D(lambda e, v=v, x=x, tmp=tmp: e.max_index(x[:, 8:16], v[:, 8:16], tmp), u)
              for (a, v, x, tmp), u in zip(groups, t3)]
        return t4[-1]

    def affine(self, X, H, m, j0, segs, t, tm):
        one = self.ones16
        t1 = [self.ts(one[:, 8 * s:8 * s + 8], m[:, j0 + 8:j0 + 16, s], 1.0, None, ALU.add, None, tm, self.act.last())
              for s in range(len(segs))]
        for k in range(8):
            for s, (a, b) in enumerate(segs):
                u = self.ac(H[:, k, a:b], X[:, k, a:b], AF.Identity, t, t1, scale=one[:, 8 * s + k:8 * s + k + 1],
                            bias=m[:, j0 + k, s:s + 1])
        return u

    def residual_norm(self, X, units, rhs, m, jg, g, b, segs, rstd, sqt, *toks):
        n = segs[-1][1]
        t = None
        for k in range(8):
            x = X[:, k, 0:n]
            ta = self.act.do(lambda e, x=x: e.mul(x, x, ALPHA), *toks)
            got = self.proj(units(k), rhs, segs, toks=toks)
            for s, ((bank, ids, t), (lo, hi)) in enumerate(zip(got, segs)):
                x = X[:, k, lo:hi]
                t = self.stt(x, bank[:, 0:hi - lo], m[:, jg + k, s:s + 1], x, ALU.mult, ALU.add, t, ta)
                self.ps.free(ids, t)
        means = []
        for lo, hi in segs:
            bank, ids, rel = self.ps.take()
            u = self.mm(bank[:, 0:hi - lo], [(self.sq["m1024"], X[:, k, lo:hi]) for k in range(8)], t, rel)
            means.append((bank, ids, u))
        for k in range(8):
            for (bank, ids, u), (lo, hi) in zip(means, segs):
                t = self.tt(X[:, k, lo:hi], X[:, k, lo:hi], bank[:, 0:hi - lo], ALU.subtract, u)
        for bank, ids, u in means:
            self.ps.free(ids, t)
        r = self.rms(lambda k: X[:, k, 0:n], 8, rstd, [s[:, 0:n] for s in sqt], self.sq["m1024"], LN_EPS, segs, t)
        for k in range(8):
            x = X[:, k, 0:n]
            t = self.tt(x, x, rstd[:, 0:n], ALU.mult, r)
            t = self.ac(x, x, AF.Identity, t, scale=g[:, k:k + 1], bias=b[:, k:k + 1])
        return t

    def turn(self, x, R, cos, sin, tmp, t, p=128):
        bank, ids, rel = self.ps.take()
        u = self.mm(bank[0:p, :], [(R[0:p, 0:p], x)], t, rel)
        w = self.tt(tmp[0:p, :], bank[0:p, :], sin[0:p, :], ALU.mult, u, self.pool.last())
        self.ps.free(ids, w)
        u = self.tt(x, x, cos[0:p, :], ALU.mult, u, q=self.pool)
        return self.tt(x, x, tmp[0:p, :], ALU.add, u, w, q=self.pool)

    def attend(self, units, P, PT, st, P2=()):
        P, nP = [*P, *P2], len(P)
        P_free, PT_free, st_free = [None] * len(P), [None] * len(PT), [None] * len(st)
        pend, late, cnt, banks = [], [], [0, 0, 0, 0], {}

        def first(u):
            ps = []
            for which, segs in enumerate(u["segs"]):
                n = sum(x[3] for x in segs)
                bank, ids, rel = self.ps.take(2)
                for i, (q, k, c, w) in enumerate(segs):
                    t = self.mm(bank[:, c:c + w], [(q, k)], rel, u["toks"], mark=True)
                for c, mk in u.get("masks", ()):
                    t = self.tt(bank[:, c:c + 128], bank[:, c:c + 128], self.sq[mk], ALU.add, t)
                pi = nP + cnt[3] % 2 if which else cnt[0] % nP
                cnt[3 if which else 0] += 1
                si = cnt[1] % len(st)
                cnt[1] += 1
                p, s = P[pi], st[si]
                t = self.red(s[:, 0:1], bank[:, 0:n], ALU.max, t, st_free[si])
                sc = u["scale"]
                if u.get("sink") is not None:
                    t = self.ts(s[:, 0:1], s[:, 0:1], sc, u["sink"], ALU.mult, ALU.max, t)
                    t = self.ts(s[:, 0:1], s[:, 0:1], -1.0, None, ALU.mult, None, t)
                else:
                    t = self.ts(s[:, 0:1], s[:, 0:1], -sc, None, ALU.mult, None, t)
                t = self.ac(p[:, 0:n], bank[:, 0:n], AF.Exp, t, P_free[pi], scale=sc, bias=s[:, 0:1], accum=s[:, 1:2])
                self.ps.free(ids, t)
                if u.get("sink") is not None:
                    t = self.ac(s[:, 2:3], u["sink"], AF.Exp, t, bias=s[:, 0:1])
                    t = self.tt(s[:, 1:2], s[:, 1:2], s[:, 2:3], ALU.add, t)
                t = self.rec(s[:, 1:2], s[:, 1:2], t)
                ps.append((p, s, pi, si, n, t))
            p, s, pi, si, n, t = ps[0]
            if len(ps) == 2:
                p2, s2, pi2, si2, _, t2 = ps[1]
                t2 = self.tt(s2[:, 1:2], s2[:, 1:2], self.lam, ALU.mult, t2)
                t2 = self.ts(p2[:, 0:n], p2[:, 0:n], s2[:, 1:2], None, ALU.mult, None, t2)
                t = self.stt(p[:, 0:n], p[:, 0:n], s[:, 1:2], p2[:, 0:n], ALU.mult, ALU.subtract, t, t2)
                P_free[pi2] = st_free[si2] = t
            else:
                t = self.ts(p[:, 0:n], p[:, 0:n], s[:, 1:2], None, ALU.mult, None, t)
            st_free[si] = t
            return p, pi, n, t

        def turned(u, p, pi, n, t):
            xi = cnt[2] % len(PT)
            cnt[2] += 1
            pt = PT[xi]
            bank, ids, rel = self.ps.take(2)
            for c in range(n // 128):
                t2 = self.tr(bank[:, 128 * c:128 * c + 128], p[:, 128 * c:128 * c + 128], t, rel, mark=True)
            P_free[pi] = t2
            h = min(n, 512)
            ta = self.acp(pt[:, 0:h], bank[:, 0:h], t2, PT_free[xi])
            tb = self.cp(pt[:, h:n], bank[:, h:n], t2, PT_free[xi]) if n > h else None
            self.ps.free(ids, [ta, tb])
            return n, pt, xi, ta, tb

        def values(u, n, pt, xi, ta, tb):
            out, p0, M, col, width, key, lastu = u["out"]
            if key not in banks:
                banks[key] = self.ps.take()
            ob, oid, orel = banks[key]
            t = self.mm(ob[p0:p0 + M, col:col + 128],
                        [(v, pt[:, 128 * c:128 * c + 128]) for c, v in enumerate(u["vals"])], ta, tb, orel)
            PT_free[xi] = t
            if lastu:
                t = self.acp(out, ob[p0:p0 + M, 0:width], t)
                self.ps.free(oid, t)
                del banks[key]
            return t

        t = None
        for u in [*units, None, None, None]:
            if u is not None:
                pend.append((u, first(u)))
            if len(pend) > 2 or (u is None and pend):
                v, a = pend.pop(0)
                late.append((v, turned(v, *a)))
            if len(late) > 1 or (not pend and late):
                v, a = late.pop(0)
                t = values(v, *a)
        for v, a in late:
            t = values(v, *a)
        return t

    def ffn(self, i, X, H, m, segs, hid, raws, accs, t):
        d, V = self.d, self.vec
        n = segs[-1][1]
        th = self.affine(X, H, m, 24, segs, t, None)
        rhs = lambda k, a, b: H[:, k, a:b]
        tz = [self.zero(r, self.floor) for r in raws]
        raw_free, acc_free = [tz, tz], [None, None]
        for j in range(22):
            r, acc = raws[j % 2], accs[j % 2]
            got = self.proj([(d["wgate"][22 * i + j], 1024)], rhs, segs, toks=(th,))
            tc = []
            for (bank, ids, t), off, (a, b) in zip(got, (2, 518), segs):
                u = self.acp(r[:, off:off + b - a], bank[:, 0:b - a], t, raw_free[j % 2])
                self.ps.free(ids, u)
                tc.append(u)
            w = V["fcw"][:, 66 * i + 3 * j:66 * i + 3 * j + 3]
            last = []
            for base, (a, b) in zip((1, 517), segs):
                o, w0 = acc[:, a:b], b - a
                t = self.ts(o, r[:, base:base + w0], w[:, 0:1], V["fcb"][:, 22 * i + j:22 * i + j + 1], ALU.mult, ALU.add, tc,
                            acc_free[j % 2])
                for k in (1, 2):
                    t = self.stt(o, r[:, base + k:base + k + w0], w[:, k:k + 1], o, ALU.mult, ALU.add, t)
                last.append(t)
            raw_free[j % 2] = last
            ts = self.ac(acc[:, 0:n], acc[:, 0:n], AF.Silu, last)
            got = self.proj([(d["wup"][22 * i + j], 1024)], rhs, segs)
            for (bank, ids, t), (a, b) in zip(got, segs):
                u = self.tt(hid[:, j, a:b], acc[:, a:b], bank[:, 0:b - a], ALU.mult, t, ts)
                self.ps.free(ids, u)
            acc_free[j % 2] = u
        return u

    def modulations2(self):
        cb = [self.condition(self.ar.take(1024), 2 + i) for i in range(2)]
        junk = self.ar.take(1024)
        self.mod2, steps = [], []
        for i in range(2):
            m, step, done = self.modulation(1 + i, "wmod2", 48 * i, self.vec["bmod2"][:, 48 * i:48 * i + 48], cb, junk)
            self.mod2.append(m)
            both = 48 if i == 0 else 16
            steps += [lambda j=j, step=step, both=both: step(j, j < both) for j in range(48)]
            if i == 0:
                steps.append(lambda done=done: done(0, 48, True))
            else:
                steps += [lambda done=done: done(0, 16, True), lambda done=done: done(16, 48, False)]
        return steps

    def second(self, alone):
        d, ar, V, S = self.d, self.ar, self.vec, self.sq
        seg2, seg1 = [(0, 512), (512, 768)], [(0, 512)]
        if alone:
            ar.at = self.base + 16384
            for step in self.modulations2():
                step()
        m, m1 = self.mod2
        self.fence()
        ar.at = self.base
        X = v3(ar.take(6144), 768)
        assert ar.at <= self.base + 8192
        if alone:
            tx = self.load(X[:, :, 0:512], d["xT"])
        else:
            tx = self.cp(X[:, :, 0:512], self.h, self.floor)
        tc = self.load(X[:, :, 512:768], d["ctxT2"])
        self.fence()
        self.ones16 = ar.take(16)
        lamb = ar.take(8)
        sub = ar.take(1)
        st = [ar.take(4) for _ in range(6)]
        top = ar.at
        H = v3(ar.take(6144), 768)
        O1 = ar.take(6144)
        O = v3(O1, 768)
        qa, kva, kr = v3(ar.take(1536), 768), ar.take(768), ar.take(768)
        Vm, wkv, rope = v3(ar.take(3072), 512), ar.take(1024), ar.take(2048)
        qb, kb = [ar.take(768) for _ in range(2)], [ar.take(768) for _ in range(2)]
        tmp = O1[:, 3072:3584]
        rstd, sqt = O1[:, 3584:4352], [O1[:, 4352 + 768 * i:5120 + 768 * i] for i in range(2)]
        P = [ar.take(768) for _ in range(3)]
        PT = [ar.take(768) for _ in range(2)]
        trp, twk = self.load(rope, d["rope"]), self.load(wkv, d["wkvb"])
        c96, s96, c128, s128 = (rope[:, 512 * i:512 * i + 512] for i in range(4))
        th = self.affine(X, H, m, 0, seg2, [tx, tc], None)
        rhs = lambda k, a, b: H[:, k, a:b]

        def project(j, out, p=128):
            ts = []
            for (bank, ids, t), (a, b) in zip(self.proj([(d["abin"][j], 1024)], rhs, seg2, toks=(th,)), seg2):
                u = self.acp(out[0:p, a:b], bank[0:p, 0:b - a], t)
                self.ps.free(ids, u)
                ts.append(u)
            return ts

        t0 = [project(j, qa[:, j, :]) for j in range(2)]
        r = self.rms(lambda k: qa[:, k, :], 2, rstd, sqt, S["m256"], EPS, seg2, t0)
        tq = [self.stt(qa[:, k, :], qa[:, k, :], V["qn"][:, k:k + 1], rstd, ALU.mult, ALU.mult, r) for k in range(2)]
        t0 = project(6, kva)
        r = self.rms(lambda k: kva, 1, rstd, sqt, S["m128"], EPS, seg2, t0, tq)
        tk = self.stt(kva, kva, V["kvn"], rstd, ALU.mult, ALU.mult, r)
        t0 = project(8, kr, 96)
        tkr = self.turn(kr[0:96, 0:512], S["r96"], c96, s96, tmp, [t0, trp], 96)
        tv = []
        for c in range(6):
            bank, ids, rel = self.ps.take()
            t = self.mm(bank, [(kva[:, 128 * c:128 * c + 128], wkv[:, 512:1024])], tk, twk, rel)
            u = self.acp(Vm[:, c, :], bank, t)
            self.ps.free(ids, u)
            tv.append(u)
        qk_free = [None, None]
        scale = 96 ** -0.5

        def prepare(h):
            q, k = qb[h % 2], kb[h % 2]
            w, tw, s = self.ring.take(d["wqb"][h], 192)
            ts = []
            for a, b in seg2:
                bank, ids, rel = self.ps.take()
                t = self.mm(bank[0:96, 0:b - a], [(w[:, 96 * i:96 * i + 96], qa[:, i, a:b]) for i in range(2)], tw, tq, rel)
                u = self.acp(q[0:96, a:b], bank[0:96, 0:b - a], t, qk_free[h % 2])
                self.ps.free(ids, u)
                ts.append(u)
            self.ring.free(s, t)
            ts.append(self.turn(q[0:96, 0:512], S["r96"], c96, s96, tmp, ts, 96))
            for a, b in seg2:
                bank, ids, rel = self.ps.take()
                t = self.mm(bank[0:64, 0:b - a], [(wkv[:, 64 * h:64 * h + 64], kva[:, a:b])], rel)
                u = self.acp(k[0:64, a:b], bank[0:64, 0:b - a], t, qk_free[h % 2])
                self.ps.free(ids, u)
                ts.append(u)
            ts.append(self.cp(k[64:96, :], kr[64:96, :], tkr, t0, qk_free[h % 2]))
            return ts

        tp = prepare(0)
        for h in range(8):
            tn = prepare(h + 1) if h < 7 else None
            q, k = qb[h % 2], kb[h % 2]
            p0 = 64 * (h % 2)
            units = []
            vals = [Vm[:, c, 64 * h:64 * h + 64] for c in range(6)]
            for qt in range(6):
                ql = q[0:96, 128 * qt:128 * qt + 128]
                lat = qt < 4
                if lat:
                    segs = [(ql, k[0:96, 0:512], 0, 512), (ql, k[0:96, 512:768], 512, 256)]
                else:
                    segs = [(ql, k[0:96, 512:768], 0, 256)]
                o = O[p0:p0 + 64, h // 2, 0:512] if lat else O[p0:p0 + 64, h // 2, 512:768]
                units.append(dict(segs=[segs], scale=scale, toks=[tp, tv], vals=vals if lat else vals[4:],
                                  out=(o, p0, 64, 128 * (qt % 4), 512 if lat else 256, (h, lat), qt in (3, 5))))
            self.attend(units, P, PT, st)
            qk_free[h % 2] = self.pe.last()
            tp = tn
        self.fence()
        ar.at = top + 12288
        qs, ks, Vs = v3(ar.take(3072), 768), ar.take(768), v3(ar.take(768), 128)
        tmp = ar.take(512)
        assert ar.at <= top + 12288 + 1536 + 768 + 768 + 3072
        ts = []
        for j in range(4):
            t0 = project(2 + j, qs[:, j, :])
            ts.append([t0, self.turn(qs[:, j, 0:512], S["r128"], c128, s128, tmp, t0)])
        t0 = project(7, ks)
        ts.append([t0, self.turn(ks[:, 0:512], S["r128"], c128, s128, tmp, t0)])
        w, tw, s = self.ring.take(d["abin"][9])
        for c in range(6):
            bank, ids, rel = self.ps.take()
            t = self.mm(bank[:, 0:128], [(H[:, k, 128 * c:128 * c + 128], w[:, 128 * k:128 * k + 128]) for k in range(8)], tw, rel)
            u = self.acp(Vs[:, c, :], bank[:, 0:128], t)
            self.ps.free(ids, u)
            ts.append(u)
        self.ring.free(s, t)
        units = []
        for i in range(4):
            for kv in range(2):
                p0 = 64 * kv
                ps = slice(p0, p0 + 64)
                sk = self.row["sink"][:, i + 4 * kv:i + 4 * kv + 1]
                for qt in range(6):
                    ql = qs[ps, i, 128 * qt:128 * qt + 128]
                    segs = [(ql, ks[ps, 512:768], 0, 256)]
                    tiles, masks = [4, 5], []
                    if qt < 4:
                        lo, hi = max(qt - 1, 0), min(qt + 1, 3)
                        segs.append((ql, ks[ps, 128 * lo:128 * lo + 256], 256, 256))
                        if hi - lo == 2:
                            segs.append((ql, ks[ps, 128 * hi:128 * hi + 128], 512, 128))
                        tiles += range(lo, hi + 1)
                        if qt > 0:
                            masks.append((256, "bandlo"))
                        if qt < 3:
                            masks.append((256 + 128 * (hi - lo), "bandhi"))
                    o = O[ps, 4 + i, 0:512] if qt < 4 else O[ps, 4 + i, 512:768]
                    units.append(dict(segs=[segs], scale=0.125, toks=[ts], masks=masks, sink=sk,
                                      vals=[Vs[:, c, p0:p0 + 64] for c in tiles],
                                      out=(o, p0, 64, 128 * (qt % 4), 512 if qt < 4 else 256, (i, kv, qt < 4), qt in (3, 5))))
        self.attend(units, P, PT, st)
        self.fence()
        ar.at = top + 12288
        rstd, sqt = ar.take(768), [ar.take(768) for _ in range(2)]
        t = self.residual_norm(X, lambda k: [(d["about"][k], 1024)], lambda k, a, b: O[:, k, a:b], m, 16, V["ln1g"][:, 0:8],
                               V["ln1b"][:, 0:8], seg2, rstd, sqt)
        t = self.feed(0, X, m, seg2, top, t, V)
        self.fence()
        ar.at = top
        H1 = ar.take(6144)
        H, O = v3(H1, 768), v3(H1[:, 0:4096], 512)
        q, k = v3(ar.take(4096), 512), v3(ar.take(6144), 768)
        Vd = v3(ar.take(6144), 1024)
        rope = ar.take(1024)
        tmp = ar.take(512)
        P, P2 = [ar.take(768) for _ in range(3)], [H1[:, 4096 + 768 * i:4864 + 768 * i] for i in range(2)]
        PT = [ar.take(768) for _ in range(2)]
        trp = self.load(rope, d["rope"][:, 1024:2048])
        c128, s128 = rope[:, 0:512], rope[:, 512:1024]
        self.lam = lamb[:, 0:1]
        pr = tmp[:, 0:64]
        t = self.floor
        for i, (a, b) in enumerate((("lq1", "lk1"), ("lq2", "lk2"))):
            t = self.tt(pr, self.row[a], self.row[b], ALU.mult, t)
            t = self.red(lamb[:, 2 + i:3 + i], pr, ALU.add, t)
            t = self.ac(lamb[:, 2 + i:3 + i], lamb[:, 2 + i:3 + i], AF.Exp, t)
        t = self.tt(lamb[:, 0:1], lamb[:, 2:3], lamb[:, 3:4], ALU.subtract, t)
        t = self.ts(lamb[:, 0:1], lamb[:, 0:1], LAMBDA_INIT, None, ALU.add, None, t)
        t = self.ts(sub, V["subln"], 1.0 - LAMBDA_INIT, None, ALU.mult, None, t)
        th = self.affine(X, H, m1, 0, seg2, t, None)
        rhs = lambda k, a, b: H[:, k, a:b]
        ts = []
        for j in range(16):
            dst, segs = (q[:, j, :], seg1) if j < 8 else (k[:, j - 8, :], seg2)
            t0 = []
            for (bank, ids, t), (a, b) in zip(self.proj([(d["dqk"][j], 1024)], rhs, segs, toks=(th,)), segs):
                u = self.acp(dst[:, a:b], bank[:, 0:b - a], t)
                self.ps.free(ids, u)
                t0.append(u)
            ts += [t0, self.turn(dst[:, 0:512], S["r128"], c128, s128, tmp, [t0, trp])]
        ws = [self.ring.take(d["dv"][i]) for i in range(8)]
        for c in range(6):
            for hf in range(2):
                bank, ids, rel = self.ps.take()
                t = self.mm(bank, [(H[:, i, 128 * c:128 * c + 128], ws[i][0][:, 512 * hf:512 * hf + 512]) for i in range(8)],
                            [w[1] for w in ws], rel)
                u = self.acp(Vd[:, c, 512 * hf:512 * hf + 512], bank, t)
                self.ps.free(ids, u)
                ts.append(u)
        for w in ws:
            self.ring.free(w[2], t)
        self.act.wait(t)
        units = []
        for h in range(8):
            for qt in range(4):
                sg = []
                for s in range(2):
                    ps = slice(64 * s, 64 * s + 64)
                    ql = q[ps, h, 128 * qt:128 * qt + 128]
                    sg.append([(ql, k[ps, h, 0:512], 0, 512), (ql, k[ps, h, 512:768], 512, 256)])
                units.append(dict(segs=sg, scale=0.125, toks=[ts], vals=[Vd[:, c, 128 * h:128 * h + 128] for c in range(6)],
                                  out=(O[:, h, :], 0, 128, 128 * qt, 512, h, qt == 3)))
        t = self.attend(units, P, PT, st, P2)
        self.fence()
        for h in range(8):
            r = self.rms(lambda k: O[:, h, :], 1, P[h % 2][:, 0:512], [P2[h % 2][:, 0:512]] * 2, S["m128"], EPS, seg1, t)
            u = self.stt(O[:, h, :], O[:, h, :], sub, P[h % 2][:, 0:512], ALU.mult, ALU.mult, r)
        t = self.residual_norm(X, lambda k: [(d["dout"][k], 1024)], lambda k, a, b: O[:, k, a:b], m1, 16, V["ln1g"][:, 8:16],
                               V["ln1b"][:, 8:16], seg1, P[0], P[1:3], u)
        t = self.feed(1, X, m1, seg1, top, t, V)
        self.h = X[:, :, 0:512]
        return t

    def feed(self, i, X, m, segs, top, t, V):
        d, ar = self.d, self.ar
        self.fence()
        ar.at = top
        H = v3(ar.take(6144), 768)
        hid = v3(ar.take(22 * 768), 768)
        raws = [ar.take(776) for _ in range(2)]
        accs = [ar.take(768) for _ in range(2)]
        rstd, sqt = ar.take(768), [ar.take(768) for _ in range(2)]
        t = self.ffn(i, X, H, m, segs, hid, raws, accs, t)
        units = lambda k: [(d["wdown"][i, k][:, a:b], b - a) for a, b in ((0, 1024), (1024, 2048), (2048, 2816))]
        return self.residual_norm(X, units, lambda k, a, b: hid[:, k, a:b], m, 40, V["ln2g"][:, 8 * i:8 * i + 8],
                                  V["ln2b"][:, 8 * i:8 * i + 8], segs, rstd, sqt, t)


def _tiles(w):
    k, n = w.shape
    return np.ascontiguousarray(w.reshape(k // 128, 128, n // 128, 128).transpose(2, 1, 0, 3).reshape(n // 128, 128, k))


def _cols(v):
    return np.ascontiguousarray(np.asarray(v).reshape(-1, 128).T)


def _fm(x):
    t, f = x.shape
    return np.ascontiguousarray(x.T.reshape(f // 128, 128, t).transpose(1, 0, 2))


def _constants():
    f32 = np.float32
    i = np.arange(128)
    j, l = i[:, None], i[None, :]
    sq = {"ident": j == l, "ones": j >= 0 * l, "le": j <= l, "ge": j >= l, "gt": j > l, "lt": j < l}
    sq = {k: (v + 0 * l).astype(f32) for k, v in sq.items()}
    sq["ones"][:] = 1
    sq["m256"] = np.full((128, 128), 1 / 256, f32)
    sq["m1024"] = np.full((128, 128), 1 / 1024, f32)
    sq["m128"] = np.full((128, 128), 1 / 128, f32)
    sq["m64"] = ((j // 64 == l // 64) / 64).astype(f32)
    sq["iota"] = np.broadcast_to(l, (128, 128)).astype(f32)

    def rot(n, blocks, start):
        r = np.zeros((128, 128), f32)
        q = n // 4
        for b in blocks:
            o = start + b * n
            for k in range(q):
                r[o + q + k, o + k] = -1
                r[o + k, o + q + k] = 1
                r[o + 3 * q + k, o + 2 * q + k] = -1
                r[o + 2 * q + k, o + 3 * q + k] = 1
        return r

    sq["r96"] = rot(32, [0], 64)
    sq["r128"] = rot(64, [0, 1], 0)
    sq["bandlo"] = np.where(l >= j, 0, NEG).astype(f32)
    sq["bandhi"] = np.where(l <= j, 0, NEG).astype(f32)
    out = {"squares": np.concatenate([sq[n] for n in SQ], 1)}
    t = np.arange(512)
    ang = 2 * np.pi * ((t[:, None] * t[None, :]) % 1024) / 1024
    c, s = np.cos(ang), np.sin(ang)
    s[0, :] = 0
    s[:, 0] = 0
    tm = lambda a: np.ascontiguousarray(a.reshape(4, 128, -1).transpose(1, 0, 2)).astype(f32)
    out["dftc"], out["dfts"] = tm(c), tm(s)
    is0 = s[0:128].copy()
    is0[0] = (-1.0) ** t
    out["is0"] = is0.astype(f32)
    ny = np.zeros((512, 128))
    ny[:, 0] = (-1.0) ** t
    out["nyq"] = tm(ny)
    tl = np.linspace(0.0, 1.0, 512).astype(f32)
    wa = (f32(2 * np.pi) * t.astype(f32) / f32(512)).astype(f32)
    bands = np.linspace(1e-4, 15, 16).astype(f32)
    an = (wa[:, None] * bands[None, :]).astype(f32)
    out["zpos"] = np.ascontiguousarray(np.concatenate([tl[:, None], np.cos(an), -np.sin(an)], -1).T).astype(f32)
    dl = np.abs(np.linspace(math.log(1e-2) / 1.5, math.log(1e-2) / 0.3, 1024).astype(f32))
    dec = np.exp(-tl[:, None] * dl[None, :]).astype(f32)
    out["dec"] = np.ascontiguousarray(dec.reshape(2, 2, 128, 2, 512).transpose(3, 0, 2, 1, 4).reshape(2, 2, 128, 1024))

    def rope(dim):
        row = np.repeat(np.arange(8), 64).astype(f32)
        col = np.tile(np.arange(64), 8).astype(f32)
        q = dim // 4
        fr = (f32(10000.0) ** (-np.arange(q, dtype=f32) / f32(q))).astype(f32)
        ar, ac = row[:, None] * fr, col[:, None] * fr
        a = np.concatenate([ar, ar, ac, ac], -1)
        return np.cos(a).T.astype(f32), np.sin(a).T.astype(f32)

    c32, s32 = rope(32)
    c64, s64 = rope(64)
    z = np.zeros((32, 512), f32)
    r96c = np.concatenate([np.ones((64, 512), f32), c32, z])
    r96s = np.concatenate([np.zeros((64, 512), f32), s32, z])
    out["rope"] = np.concatenate([r96c, r96s, np.tile(c64, (2, 1)), np.tile(s64, (2, 1))], 1)
    return {k: np.ascontiguousarray(v, dtype=f32) for k, v in out.items()}


def _arrays(p):
    p = {k: np.asarray(v) for k, v in p.items()}
    a = _constants()
    a["xT"], a["ctxT"], a["ctxT2"] = _fm(p["x"][0]), _fm(p["ctx"][0]), _fm(p["ctx_2"][0])
    a["wmod"] = np.ascontiguousarray(p["w_mod"][0].T).reshape(48, 128, 1024)
    a["wmod2"] = np.ascontiguousarray(p["w_mod_2"].transpose(0, 2, 1)).reshape(96, 128, 1024)
    a["crow"] = np.tile(np.stack([p["c"][0], p["c_ctx"], p["c_2"][0], p["c_ctx_2"]])[:, None], (1, 128, 1))
    win = p["w_in"][0]
    a["win"] = _tiles(np.concatenate([win[:, :3072], win[:, 3104:]], 1))
    a["wdt"] = np.ascontiguousarray(win[:, 3072:3104].reshape(8, 128, 32).transpose(1, 0, 2).reshape(128, 256))
    w12 = np.zeros((64, 128), np.float32)
    w12[:33, :64] = p["hy_w1"][0]
    w12[:, 64:] = p["hy_w2"][0]
    a["hyw12"] = w12
    w3 = p["hy_w3"][0].reshape(64, 2, 2, 2, 512)
    a["hyw3"] = np.ascontiguousarray(w3.transpose(1, 3, 0, 2, 4).reshape(2, 2, 64, 1024))
    a["wout"] = np.ascontiguousarray(_tiles(p["w_out"][0]).reshape(8, 128, 2, 1024).transpose(0, 2, 1, 3))
    a["wq"] = _tiles(p["peer_wq"][0])
    a["subkeys"] = np.ascontiguousarray(p["peer_subkeys"][0].transpose(2, 0, 1).reshape(128, 256))
    a["peeru"] = np.ascontiguousarray(p["peer_u"][0].reshape(128, 128, 8, 128).transpose(0, 3, 2, 1).reshape(128, 128, 1024))
    a["peerv"] = np.ascontiguousarray(p["peer_v"][0].reshape(128, 128, 1024))

    def pad(v):
        o = np.zeros((128, 1), np.float32)
        o[:v.size, 0] = v.reshape(-1)
        return o

    def taps(w):
        k, n = w.shape
        return np.ascontiguousarray(w.reshape(k, n // 128, 128).transpose(2, 1, 0).reshape(128, -1))

    c2 = lambda x, y: np.ascontiguousarray(np.stack([_cols(x), _cols(y)], 2).reshape(128, 16))
    v = {"norm1": _cols(p["norm1"]), "convw": taps(p["ssd_conv_w"][0]), "convb": _cols(p["ssd_conv_b"]),
         "ssd_norm": _cols(p["ssd_norm"]), "hyw": taps(p["hy_short_w"][0]), "hyb": _cols(p["hy_short_b"]),
         "hbias": _cols(p["hy_filt_bias"]), "hy_norm": _cols(p["hy_norm"]), "norm2": _cols(p["norm2"]),
         "final_norm": _cols(p["final_norm"]), "bmod": _cols(p["b_mod"]), "dtb": pad(p["ssd_dt_bias"]),
         "hyb1": pad(p["hy_b1"]), "hyb2": pad(p["hy_b2"]), "fr0": pad(p["hy_sin_freq"][0, 0]),
         "fr1": pad(p["hy_sin_freq"][0, 1]), "ln1g": _cols(p["ln1_g_2"]), "ln1b": _cols(p["ln1_b_2"]),
         "ln2g": _cols(p["ln2_g_2"]), "ln2b": _cols(p["ln2_b_2"]),
         "fcw": np.concatenate([taps(p["ffn_conv_w_2"][i]) for i in range(2)], 1), "fcb": _cols(p["ffn_conv_b_2"]),
         "bmod2": _cols(p["b_mod_2"]), "qn": _cols(p["mla_q_norm_2"]), "kvn": _cols(p["mla_kv_norm_2"]),
         "subln": _cols(p["diff_subln_g_2"]), "c1": c2(p["c"], p["c_ctx"]), "c2": c2(p["c_2"], p["c_ctx_2"])}
    a["vecs"] = np.concatenate([v[n] for n, _ in VECS], 1)
    r = {"alog": p["ssd_a_log"], "dskip": p["ssd_d"], "sink": p["swa_sink_2"], "lq1": p["diff_lam_q1_2"],
         "lk1": p["diff_lam_k1_2"], "lq2": p["diff_lam_q2_2"], "lk2": p["diff_lam_k2_2"],
         "i16": np.arange(16, dtype=np.float32)}
    a["rows"] = np.tile(np.concatenate([r[n].reshape(-1) for n, _ in ROWS])[None], (128, 1))
    w = p["ab_w_in_2"][0]
    qs = w[:, 256:768].reshape(1024, 2, 4, 64).transpose(0, 2, 1, 3).reshape(1024, 512)
    kr = np.concatenate([np.zeros((1024, 64), np.float32), w[:, 896:928], np.zeros((1024, 32), np.float32)], 1)
    a["abin"] = _tiles(np.concatenate([w[:, :256], qs, w[:, 768:896], w[:, 928:1056], kr, w[:, 1056:]], 1))
    wq = p["mla_w_qb_2"][0].reshape(2, 128, 8, 96)
    a["wqb"] = np.ascontiguousarray(wq.transpose(2, 1, 0, 3).reshape(8, 128, 192))
    wk = p["mla_w_kvb_2"][0].reshape(128, 8, 128)
    a["wkvb"] = np.ascontiguousarray(np.concatenate([wk[:, :, :64].reshape(128, 512), wk[:, :, 64:].reshape(128, 512)], 1))
    wo = p["ab_w_out_2"][0]
    wos = wo[512:].reshape(2, 4, 64, 1024).transpose(1, 0, 2, 3).reshape(512, 1024)
    a["about"] = _tiles(np.concatenate([wo[:512], wos], 0))
    w = p["diff_w_in_2"][0]
    a["dqk"] = _tiles(w[:, :2048])
    a["dv"] = np.ascontiguousarray(w[:, 2048:].reshape(8, 128, 1024))
    a["dout"] = _tiles(p["diff_w_out_2"][0])
    a["wgate"] = np.concatenate([_tiles(p["ffn_w_gate_2"][i]) for i in range(2)])
    a["wup"] = np.concatenate([_tiles(p["ffn_w_up_2"][i]) for i in range(2)])
    wd = np.stack([_tiles(p["ffn_w_down_2"][i]) for i in range(2)])
    a["wdown"] = wd
    return {k: np.ascontiguousarray(x, dtype=np.float32) for k, x in a.items()}


def build(nc, d, out, part="all", dump=None):
    with ExitStack() as ctx:
        k = Core(nc, d, ctx)
        k.setup()
        if part != "second":
            k.in_projection()
            k.ssd()
            t = k.hyena()
            t = k.out_projection(t)
            t = k.peer(t)
        if part != "first":
            t = k.second(part == "second")
        so = k.dsem()
        t = k.sp.dma(out, k.h, so, t)
        k.sp.wait(t)
        block = ctx.enter_context(nc.Block())
        for deco, q in ((block.tensor, k.pe), (block.vector, k.dve), (block.scalar, k.act), (block.gpsimd, k.pool),
                        (block.sync, k.sp)):
            deco(lambda e, q=q: q.run(e))


def kernel(**inputs):
    import concourse.bacc as bacc
    from concourse.bass_utils import run_bass_kernel_spmd as run

    nc = bacc.Bacc("TRN2", target_bir_lowering=False, num_devices=1)
    arrays = _arrays(inputs)
    d = {n: nc.dram_tensor(n, a.shape, F, kind="ExternalInput").ap() for n, a in arrays.items()}
    d["gates"] = nc.dram_tensor("gates", (16, 128, 4096), F, kind="Internal").ap()
    out = nc.dram_tensor("out", (128, 8, 512), F, kind="ExternalOutput").ap()
    build(nc, d, out)
    r = run(nc, [arrays], core_ids=[0]).results[0]["out"]
    return np.ascontiguousarray(np.asarray(r).transpose(2, 1, 0).reshape(1, 512, 1024))
```

```python
import math
from contextlib import ExitStack

import numpy as np

import concourse.bass as bass
from concourse import mybir

F = mybir.dt.float32
FR = mybir.dt.float32r
U32 = mybir.dt.uint32
ALU = mybir.AluOpType
AF = mybir.ActivationFunctionType
AX = mybir.AxisListType.X

L, C, T = 512, 256, 768
EPS = 1e-6
LN_EPS = 1e-5
ALPHA = 4.0 ** 0.25
NEG = -1e30
LOW = -3e38
LAMBDA_INIT = 0.8 - 0.6 * math.exp(-0.3)

SQ = ["ident", "ones", "le", "ge", "gt", "lt", "m256", "m1024", "m64", "m128", "iota", "r96", "r128",
      "bandlo", "bandhi"]
VECS = [("norm1", 8), ("convw", 80), ("convb", 16), ("ssd_norm", 8), ("hyw", 72), ("hyb", 24), ("hbias", 16),
        ("hy_norm", 8), ("norm2", 8), ("final_norm", 8), ("bmod", 48), ("dtb", 1), ("hyb1", 1), ("hyb2", 1),
        ("fr0", 1), ("fr1", 1), ("ln1g", 16), ("ln1b", 16), ("ln2g", 16), ("ln2b", 16), ("fcw", 132),
        ("fcb", 44), ("bmod2", 96), ("qn", 2), ("kvn", 1), ("subln", 1), ("c1", 16)]
ROWS = [("alog", 32), ("dskip", 16), ("sink", 8), ("lq1", 64), ("lk1", 64), ("lq2", 64), ("lk2", 64), ("i16", 16)]


class Queue:

    def __init__(self, sem):
        self.sem, self.n, self.ops, self.seen = sem, 0, [], {}

    def wait(self, *toks):
        for t in toks:
            if t is None:
                continue
            if isinstance(t, list):
                self.wait(*t)
                continue
            sem, v = t
            if self.seen.get(id(sem), 0) < v:
                self.seen[id(sem)] = v
                self.ops.append((None, sem, v))

    def do(self, fn, *toks):
        self.wait(*toks)
        self.n += 1
        self.ops.append((fn, self.sem, 1))
        return (self.sem, self.n)

    def quiet(self, fn, *toks):
        self.wait(*toks)
        self.ops.append((fn, None, 0))

    def dma(self, out, in_, sem, *toks):
        self.wait(*toks)
        sem[1] += 16
        self.ops.append((lambda e: e.dma_start(out, in_), sem[0], 16))
        return (sem[0], sem[1])

    def last(self):
        return (self.sem, self.n) if self.n else None

    def run(self, e):
        for fn, sem, v in self.ops:
            if fn is None:
                e.wait_ge(sem, v)
            else:
                i = fn(e)
                if sem is not None:
                    i.then_inc(sem, v)


class Arena:

    def __init__(self, nc, size, offset):
        self.nc, self.full, self.size, self.offset, self.at, self.names = nc, size, size, offset, 0, {}
        self.ap = nc.alloc_sbuf_tensor_at("arena", [128, size], F, offset=offset)

    def place(self, n):
        a = self.at
        self.at += n
        assert self.at <= self.size, (self.at, self.size)
        return a

    def take(self, n):
        a = self.place(n)
        return self.ap[:, a:a + n]

    def rounded(self, n):
        self.at += -self.at % 8
        return self.rounded_at(self.place(n), n)

    def rounded_at(self, a, n):
        if (a, n) not in self.names:
            self.names[a, n] = self.nc.alloc_sbuf_tensor_at(f"rounded_{a}_{n}", [128, n], FR, offset=self.offset + 4 * a)
        return self.names[a, n][:, :]


class Banks:

    def __init__(self, ap):
        self.ap, self.at, self.rel = ap, 0, [[] for _ in range(8)]

    def take(self, n=1):
        for i in range(8):
            b = (self.at + i) % 8
            if b % n == 0 and all(self.rel[j] is not None for j in range(b, b + n)):
                break
        else:
            assert False, "no bank is free"
        self.at = b + n
        toks = []
        for i in range(b, b + n):
            toks += self.rel[i]
            self.rel[i] = None
        return self.ap[:, 512 * b:512 * (b + n)], range(b, b + n), toks

    def free(self, banks, *toks):
        for i in banks:
            self.rel[i] = list(toks)


class Ring:

    def __init__(self, ap, n, sems, sp):
        self.ap, self.n, self.sems, self.sp, self.at = ap, n, sems, sp, 0
        self.rel = [[] for _ in range(n)]

    def take(self, src, cols=1024, *toks, parts=128):
        s = self.at % self.n
        self.at += 1
        assert self.rel[s] is not None, "slot not given back"
        out = self.ap[0:parts, 1024 * s:1024 * s + cols]
        t = self.sp.dma(out, src, self.sems[s], self.rel[s], *toks)
        self.rel[s] = None
        return out, t, s

    def free(self, s, *toks):
        self.rel[s] = list(toks)


class Stream:

    def __init__(self, core, aps, ahead, srcs, rest):
        self.core, self.aps, self.n, self.ahead, self.srcs, self.rest = core, aps, len(aps), ahead, srcs, rest
        n = self.n
        self.rel, self.got, self.at = [[] for _ in range(n)], [], 0
        for _ in range(ahead):
            self.split()

    def split(self):
        i = len(self.got)
        if i == len(self.srcs):
            return
        c, s = self.core, i % self.n
        src, w = self.srcs[i]
        assert self.rel[s] is not None, "pair not given back"
        hi, lo = self.aps[s][:, 0:w], self.aps[s][:, 1024:1024 + w]
        raw, t, r = c.ring.take(src, w)
        th, tl = c.parts(raw, hi, lo, t, self.rel[s], q=self.rest(i))
        c.ring.free(r, th, tl)
        self.rel[s] = None
        self.got.append((hi, lo, [th, tl], s))

    def next(self):
        self.split()
        self.at += 1
        return self.got[self.at - 1]

    def free(self, s, *toks):
        self.rel[s] = list(toks)


def v3(ap, b):
    return ap.rearrange("p (a b) -> p a b", b=b)


def v4(ap, b, c):
    return ap.rearrange("p (a b c) -> p a b c", b=b, c=c)


def bc(ap, axis, shape):
    return ap.unsqueeze(axis).to_broadcast(shape)


class Core:
    def __init__(self, nc, d, ctx):
        self.nc, self.d = nc, d
        sem = lambda n: ctx.enter_context(nc.semaphore(n))
        self.sem = sem
        self.pe, self.dve, self.act = Queue(sem("s_pe")), Queue(sem("s_dve")), Queue(sem("s_act"))
        self.pool, self.sp = Queue(sem("s_pool")), Queue(sem("s_sp"))
        self.ar = Arena(nc, 53184, 16512)
        ps = ctx.enter_context(nc.psum_tensor("psum", [128, 4096], F))
        self.ps = Banks(ps)
        self.rsem = [[sem(f"s_r{i}"), 0] for i in range(13)]
        self.floor = []
        self.rings(13)
        self.nsem = 0

    def dsem(self):
        self.nsem += 1
        return [self.sem(f"s_d{self.nsem}"), 0]

    def fence(self, *more):
        toks = [q.last() for q in (self.pe, self.dve, self.act, self.pool)] + list(more)
        for q in (self.pe, self.dve, self.act, self.pool):
            q.wait(toks)
        self.floor = toks

    def rings(self, n, pairs=0, ahead=0, srcs=(), rest=None):
        ar = self.ar
        ar.size = ar.full - 1024 * n - 2048 * pairs
        self.sp.wait(self.floor)
        self.ring = Ring(ar.ap[:, ar.full - 1024 * n:ar.full], n, self.rsem, self.sp)
        if pairs:
            self.stream = Stream(self, [ar.rounded_at(ar.size + 2048 * i, 2048) for i in range(pairs)], ahead, srcs, rest)

    def parts(self, x, hi, lo, *toks, q=None, copy=None):
        t = (copy or self.act).do(lambda e: e.copy(hi, x) if copy is None else e.tensor_copy(hi, x), *toks)
        return t, self.tt(lo, x, hi.bitcast(F), ALU.subtract, t, *toks, q=q)

    def mm3(self, out, trios, *toks, start=True, stop=True):
        pairs = []
        for (wh, wl), (xh, xl) in trios:
            pairs += [(wh, xh), (wh, xl), (wl, xh)]
        return self.mm(out, pairs, *toks, start=start, stop=stop)

    def proj3(self, x, segs, *toks, M=128):
        hi, lo, tw, s = self.stream.next()
        out = []
        for a, b in segs:
            bank, ids, rel = self.ps.take()
            t = self.mm3(bank[0:M, 0:b - a], [((hi[:, M * k:M * k + M], lo[:, M * k:M * k + M]), x(k, a, b))
                                              for k in range(8)], tw, rel, *toks)
            out.append((bank, ids, t))
        self.stream.free(s, t)
        return out

    def load(self, out, src, *toks):
        return self.pool.dma(out, src, self.dsem(), self.floor, *toks)

    def mm(self, out, pairs, *toks, start=True, stop=True, mark=True):
        self.pe.wait(*toks)
        n = len(pairs)
        for i, (l, r) in enumerate(pairs):
            s0, s1 = start and i == 0, stop and i == n - 1
            f = lambda e, l=l, r=r, s0=s0, s1=s1: e.matmul(out, l, r, start=s0, stop=s1, skip_group_check=True)
            if mark and i == n - 1:
                return self.pe.do(f)
            self.pe.quiet(f)

    def tr(self, out, in_, *toks, mark=True):
        k = in_.shape[0]
        p0 = in_.start_partition if not callable(in_.start_partition) else in_.start_partition()
        ident = self.sq["ident"][p0:p0 + k, p0:p0 + k]
        f = lambda e: e.transpose(out, in_, ident)
        return self.pe.do(f, *toks) if mark else self.pe.quiet(f, *toks)

    def tt(self, out, a, b, op, *toks, q=None):
        return (q or self.dve).do(lambda e: e.tensor_tensor(out, a, b, op), *toks)

    def ts(self, out, a, s1, s2, op0, op1, *toks, q=None):
        if op1 is None:
            return (q or self.dve).do(lambda e: e.tensor_scalar(out, a, s1, None, op0), *toks)
        return (q or self.dve).do(lambda e: e.tensor_scalar(out, a, s1, s2, op0, op1), *toks)

    def stt(self, out, a, s, b, op0, op1, *toks):
        return self.dve.do(lambda e: e.scalar_tensor_tensor(out=out, in0=a, scalar=s, in1=b, op0=op0, op1=op1), *toks)

    def cp(self, out, a, *toks, q=None):
        return (q or self.dve).do(lambda e: e.tensor_copy(out, a), *toks)

    def red(self, out, a, op, *toks):
        return self.dve.do(lambda e: e.tensor_reduce(out, a, AX, op), *toks)

    def rec(self, out, a, *toks):
        return self.dve.do(lambda e: e.reciprocal(out, a), *toks)

    def zero(self, out, *toks, q=None):
        return (q or self.pool).do(lambda e: e.memset(out, 0.0), *toks)

    def ac(self, out, a, func, *toks, scale=1.0, bias=None, accum=None):
        def f(e):
            kw = {}
            if bias is not None:
                kw["bias"] = bias
            if accum is not None:
                kw["accum_out"] = accum
            return e.activation(out, a, func, scale=scale, **kw)
        return self.act.do(f, *toks)

    def acp(self, out, a, *toks):
        return self.act.do(lambda e: e.copy(out, a), *toks)

    def proj(self, units, rhs, segs, M=128, toks=(), p0=0):
        got = [self.ring.take(u, w) for u, w in units]
        out = []
        for a, b in segs:
            bank, ids, rel = self.ps.take()
            pairs = []
            for ui, (w, _, _) in enumerate(got):
                m = M
                nk = units[ui][1] // m
                pairs += [(w[:, k * m:(k + 1) * m], rhs(8 * ui + k, a, b)) for k in range(nk)]
            t = self.mm(bank[p0:p0 + M, 0:b - a], pairs, [g[1] for g in got], rel, *toks)
            out.append((bank, ids, t))
        for g in got:
            self.ring.free(g[2], out[-1][2])
        return out

    def rms(self, src, n, out, tmp, mean, eps, segs, *toks):
        banks = [self.ps.take() for _ in segs]
        t = None
        free = [self.pe.last()] * 2
        for k in range(n):
            s = tmp[k % 2]
            t = self.act.do(lambda e, s=s, x=src(k): e.square(s, x), free[k % 2], *toks)
            for i, (a, b) in enumerate(segs):
                f = lambda e, i=i, a=a, b=b, s=s, k=k: e.matmul(banks[i][0][:, 0:b - a], mean, s[:, a:b],
                                                               start=(k == 0), stop=(k == n - 1), skip_group_check=True)
                free[k % 2] = self.pe.do(f, t, banks[i][2])
        r = []
        for i, (a, b) in enumerate(segs):
            o = out[:, a:b]
            u = self.ts(o, banks[i][0][:, 0:b - a], eps, None, ALU.add, None, free[(n - 1) % 2])
            self.ps.free(banks[i][1], u)
            u = self.ac(o, o, AF.Sqrt, u)
            u = self.rec(o, o, u)
            r.append(u)
        return r

    def norms(self, groups, out, sq, mean, eps, finish, *toks):
        t0, n = [], 0
        for g, tiles in enumerate(groups):
            bank, ids, rel = self.ps.take()
            for i, x in enumerate(tiles):
                s = sq[:, 512 * n:512 * n + 512]
                n += 1
                t = self.act.do(lambda e, s=s, x=x: e.square(s, x), *toks)
                t = self.mm(bank, [(mean, s)], t, rel, start=(i == 0), stop=(i == len(tiles) - 1))
            r = out[:, 512 * g:512 * g + 512]
            t0.append((bank, ids, r, t))
        t1 = []
        for bank, ids, r, t in t0:
            t = self.ts(r, bank, eps, None, ALU.add, None, t, *toks)
            self.ps.free(ids, t)
            t1.append(self.ac(r, r, AF.Sqrt, t))
        for g, ((_, _, r, _), t) in enumerate(zip(t0, t1)):
            u = finish(g, r, self.rec(r, r, t))
        return u


    def setup(self):
        d, ar = self.d, self.ar
        nsq, nv, nr = len(SQ), sum(n for _, n in VECS), sum(n for _, n in ROWS)
        a = ar.take(nsq * 128)
        b = ar.take(nv)
        c = ar.take(nr)
        self.t_const = [self.load(a, d["squares"]), self.load(b, d["vecs"]), self.load(c, d["rows"])]
        for q in (self.pe, self.dve, self.act, self.pool):
            q.wait(self.t_const)
        self.sq = {n: a[:, 128 * i:128 * i + 128] for i, n in enumerate(SQ)}
        self.vec, self.row = {}, {}
        at = 0
        for n, w in VECS:
            self.vec[n] = b[:, at:at + w]
            at += w
        at = 0
        for n, w in ROWS:
            self.row[n] = c[:, at:at + w]
            at += w
        self.mods = [ar.take(96) for _ in range(3)]
        self.gain_l, self.gain_c = ar.take(8), ar.take(8)
        ar.at += -ar.at % 8
        self.base = ar.at

    def modulation(self, n, wname, i0, bias, cb, junk):
        mod = v3(self.mods[n], 2)
        state = {"junk": None}

        def step(j, both):
            w, tw, s = self.ring.take(self.d[wname][i0 + j])
            t = None
            if both:
                o, (c, tc) = mod[:, j, 1:2], cb[1]
                t = state["junk"] = self.dve.do(
                    lambda e: e.tensor_tensor_reduce(junk, w, c, 1.0, 0.0, ALU.mult, ALU.add, o), tw, tc, state["junk"])
            o2, (c2, tc2) = mod[:, j, 0:1], cb[0]
            t = self.dve.do(lambda e: e.tensor_tensor_reduce(w, w, c2, 1.0, 0.0, ALU.mult, ALU.add, o2), tw, tc2, t)
            self.ring.free(s, t)

        def done(a, b, both):
            t = self.dve.last()
            for s in range(2 if both else 1):
                u = self.tt(mod[:, a:b, s], mod[:, a:b, s], bias[:, a:b], ALU.add, t)
            return u

        return mod, step, done

    def condition(self, out, i):
        t = self.load(out, self.d["crow"][i])
        return out, self.ac(out, out, AF.Silu, t)

    def gains(self, out, mod, t, j0, g, s):
        return self.stt(out, mod[:, j0:j0 + 8, s], 1.0, g, ALU.add, ALU.mult, t)

    def in_projection(self):
        d, ar, V, S = self.d, self.ar, self.vec, self.sq
        gl, gc = self.gain_l, self.gain_c
        self.rings(4, 4, 2, [(d["win"][j], 1024) for j in range(24)] + [(d["wdt"], 256)], lambda i: self.pool)
        ar.at = self.base
        fh, fl = [ar.rounded(512) for _ in range(8)], [ar.rounded(512) for _ in range(8)]
        zT = ar.take(4096)
        xl = ar.take(4096)
        BT, CT = ar.take(2048), ar.take(2048)
        self.small = ar.take(1600)
        sprev = ar.at
        self.Sprev = ar.take(8192)
        self.rest = ar.at
        xcb = ar.take(5120)
        xc, Btok = xcb[:, 0:2048], xcb[:, 2048:5120]
        sil = [ar.take(768) for i in range(2)]
        ar.at = sprev
        ch, cl = [ar.rounded(256) for _ in range(8)], [ar.rounded(256) for _ in range(8)]
        raws, accs = [ar.take(776) for _ in range(2)], [ar.take(768) for _ in range(2)]
        f3, c3 = v3(xcb[:, 0:4096], 512), v3(zT[:, 0:2048], 256)
        sqt, rstd, row = [xl[:, 768 * i:768 * i + 768] for i in range(2)], xl[:, 1536:2304], BT
        th = [self.load(f3, d["xT"]), self.load(c3, d["ctxT"])]
        inputs = ((0, 512, f3, gl, 0, fh, fl), (512, 768, c3, gc, 1, ch, cl))
        tn = []
        for lo, hi, src, g, s, xh, xo in inputs:
            r = self.rms(lambda k: src[:, k, :], 8, rstd[:, lo:hi], [q[:, 0:hi - lo] for q in sqt], S["m1024"], EPS,
                         [(0, hi - lo)], th)
            tn.append([self.tt(src[:, k, :], src[:, k, :], rstd[:, lo:hi], ALU.mult, r, th) for k in range(8)])
        cond = V["c1"]
        tc = self.ac(cond, cond, AF.Silu)
        cb0 = self.condition(self.small[:, 0:1024], 0)
        m, step, done = self.modulation(0, "wmod", -16, V["bmod"], [cb0], None)
        self.mod1 = m
        banks = [self.ps.take() for _ in range(4)]
        for k in range(8):
            for hf in range(2):
                w, tw, s = self.ring.take(d["wmod0"][k][:, 1024 * hf:1024 * hf + 1024])
                for q in range(2):
                    bank, ids, rel = banks[2 * hf + q]
                    t = self.mm(bank[0:2, :], [(cond[:, 2 * k:2 * k + 2], w[:, 512 * q:512 * q + 512])], tc, tw, rel,
                                start=(k == 0), stop=(k == 7))
                self.ring.free(s, t)
        tr = []
        for q, (bank, ids, rel) in enumerate(banks):
            u = self.acp(row[0:2, 512 * q:512 * q + 512], bank[0:2, :], t)
            self.ps.free(ids, u)
            tr.append(u)
        bank, ids, rel = self.ps.take()
        for j in range(16):
            t = self.tr(bank[:, 2 * j:2 * j + 2], row[0:2, 128 * j:128 * j + 128], tr, rel)
        tm = self.tt(m[:, 0:16, :], v3(bank[:, 0:32], 2), bc(V["bmod"][:, 0:16], 2, [128, 16, 2]), ALU.add, t)
        self.ps.free(ids, tm)
        tg = [self.gains(gl, m, tm, 8, V["norm1"], 0), self.gains(gc, m, tm, 8, V["norm1"], 1)]
        tz = [self.zero(r) for r in raws]
        tf = []
        for (lo, hi, src, g, s, xh, xo), t0 in zip(inputs, tn):
            for k in range(8):
                t = self.ac(src[:, k, :], src[:, k, :], AF.Identity, t0[k], tg, scale=g[:, k:k + 1], bias=m[:, k, s:s + 1])
                tf.append(self.parts(src[:, k, :], xh[k], xo[k], t)[1])
        seg2, seg1 = [(0, 512), (512, 768)], [(0, 512)]
        self.fx = lambda k, a, b: (fh[k], fl[k]) if a == 0 else (ch[k], cl[k])

        z3 = v3(zT, 512)
        for j in range(8):
            (bank, ids, t), = self.proj3(self.fx, seg1, tf)
            t = self.ac(z3[:, j, :], bank, AF.Silu, t, tm)
            self.ps.free(ids, t)
            step(16 + j, False)

        xl3, xc3, B3, C3, Bt3 = v3(xl, 1024), v3(xc, 1024), v3(BT, 512), v3(CT, 512), v3(Btok, 512)
        tr_free = [None, None]
        raw_free, acc_free = [[tz], [tz]], [[], []]

        def turn(j, i, lat, si, t):
            bank, ids, rel = self.ps.take(2)
            for q in range(6):
                src = lat[:, 128 * q:128 * q + 128] if q < 4 else si[:, 128 * q:128 * q + 128]
                t2 = self.tr(bank[:, 128 * q:128 * q + 128], src, t, rel, mark=(q == 5))
            tr_free[i] = [t2]
            if j < 8:
                c0 = slice(128 * j, 128 * j + 128)
                u = [self.cp(xl3[:, :, c0], v3(bank[:, 0:512], 128), t2), self.cp(xc3[:, :, c0], v3(bank[:, 512:768], 128), t2)]
            else:
                c0 = slice(128 * (j - 8), 128 * (j - 8) + 128)
                u = [self.cp(Bt3[:, :, c0], v3(bank[:, 0:768], 128), t2)]
            self.ps.free(ids, u)

        lag = []
        for j in range(16):
            i = j % 2
            raw, acc, si = raws[i], accs[i], sil[i]
            segs = seg2 if j < 12 else seg1
            got = self.proj3(self.fx, segs, tf)
            tc = []
            for (bank, ids, t), off, n in zip(got, (2, 518), (512, 256)):
                t = self.acp(raw[:, off:off + n], bank[:, 0:n], t, raw_free[i])
                self.ps.free(ids, t)
                tc.append(t)
            w = V["convw"][:, 5 * j:5 * j + 5]
            last = []
            for lo, n, base in ((0, 512, 0), (512, 256, 516))[:len(segs)]:
                a = acc[:, lo:lo + n]
                t = self.ts(a, raw[:, base:base + n], w[:, 0:1], V["convb"][:, j:j + 1], ALU.mult, ALU.add,
                            tc, acc_free[i])
                for k in range(1, 5):
                    t = self.stt(a, raw[:, base + k:base + k + n], w[:, k:k + 1], a, ALU.mult, ALU.add, t)
                last.append(t)
            raw_free[i] = last
            if j >= 12:
                acc_free[i] = [self.ac(C3[:, j - 12, :], acc[:, 0:512], AF.Silu, last)]
                if lag:
                    turn(*lag.pop(0))
                step(24 + j, False)
                continue
            if j < 8:
                t = self.ac(si, acc, AF.Silu, last, tr_free[i])
                acc_free[i], lat = [t], si[:, 0:512]
            else:
                t = self.ac(B3[:, j - 8, :], acc[:, 0:512], AF.Silu, last)
                t = self.ac(si[:, 512:768], acc[:, 512:768], AF.Silu, t, tr_free[i])
                acc_free[i], lat = [t], B3[:, j - 8, :]
            lag.append((j, i, lat, si, t))
            if len(lag) > 1:
                turn(*lag.pop(0))
            step(24 + j, False)
        for j in range(40, 48):
            step(j, False)
        done(16, 48, False)

        sm = self.small
        dtT = sil[0][0:32, :]
        got = self.proj3(self.fx, seg2, tf, M=32)
        t2 = []
        for (bank, ids, t), (a, b) in zip(got, seg2):
            u = self.ts(dtT[:, a:b], bank[0:32, 0:b - a], V["dtb"][0:32, :], None, ALU.add, None, t, tr_free[0])
            self.ps.free(ids, u)
            t2.append(u)
        bank, ids, rel = self.ps.take()
        for q in range(6):
            t = self.tr(bank[:, 32 * q:32 * q + 32], dtT[:, 128 * q:128 * q + 128], t2, rel)
        x, e, s, q, p, dt, a, A = (sm[:, 192 * i:192 * i + 192] for i in range(8))
        t = self.cp(x, bank[:, 0:192], t, self.dve.last())
        self.ps.free(ids, t)
        t = self.stt(e, x, -1.0, x, ALU.mult, ALU.max, t)
        t = self.ac(e, e, AF.Exp, t, scale=-1.0)
        t = self.ts(s, e, 2.0, None, ALU.add, None, t)
        t = self.rec(s, s, t)
        t = self.tt(s, s, e, ALU.mult, t)
        t = self.tt(q, s, s, ALU.mult, t)
        t = self.ts(p, q, 1.0 / 17, None, ALU.mult, None, t)
        for n in (15, 13, 11, 9, 7, 5, 3):
            t = self.stt(p, p, 1.0 / n, q, ALU.add, ALU.mult, t)
        t = self.stt(p, p, 1.0, s, ALU.add, ALU.mult, t)
        t = self.ts(x, x, 0.0, None, ALU.max, None, t)
        t = self.stt(dt, p, 2.0, x, ALU.mult, ALU.add, t)
        A = A[:, 0:32]
        u = self.ac(A, self.row["alog"], AF.Exp)
        u = self.ts(A, A, -1.0, None, ALU.mult, None, u)
        t = self.tt(v3(a, 32), v3(dt, 32), bc(A, 1, [128, 6, 32]), ALU.mult, t, u)
        self.dt, self.a = v3(dt, 32), v3(a, 32)
        self.zT, self.xl, self.xc, self.BT, self.CT, self.Btok = z3, xl3, xc3, B3, C3, Bt3
        return t

    def ssd(self):
        V, S, ar, sm = self.vec, self.sq, self.ar, self.small
        self.fence()
        self.rings(0)
        dt, a = self.dt, self.a
        E = sm[:, 0:576]
        wd = sm[:, 576:768]
        b0, i0, r0 = self.ps.take()
        b1, i1, r1 = self.ps.take()
        masks = ["le", "ge", "gt", "lt", "ones", "ones"]
        for n, mk in enumerate(masks):
            o = b0[:, 96 * n:96 * n + 96] if n < 5 else b1[:, 0:96]
            t = self.mm(o, [(S[mk], a[:, :, 16 * (n % 2):16 * (n % 2) + 16])], r0, r1)
        u = [self.ac(E[:, 0:480], b0[:, 0:480], AF.Exp, t), self.ac(E[:, 480:576], b1[:, 0:96], AF.Exp, t)]
        self.ps.free(i0, u)
        self.ps.free(i1, u)
        E5 = E.rearrange("p (k d c h) -> p k d c h", k=3, d=2, c=6)
        wd4 = wd.rearrange("p (d c h) -> p d c h", d=2, c=6)
        tw = []
        for k in range(2):
            tw.append(self.tt(wd4[:, k], dt[:, :, 16 * k:16 * k + 16], E5[:, 1, k], ALU.mult, u))
        ar.at = self.rest + 5120
        xws = [ar.take(1024) for _ in range(2)]
        Sp = self.Sprev.rearrange("p (d c n) -> p d c n", d=2, c=4)
        xw_free = [None, None]
        n = 0
        t_s = []
        for k, order in ((0, (4, 5, 0, 1, 2)), (1, (5, 4, 3, 2, 1))):
            prev, cur, tp = None, (0 if k == 0 else 3), None
            for step, c in enumerate(order):
                xw = xws[n % 2]
                xs = self.xl[:, c, :] if c < 4 else self.xc[:, c - 4, :]
                t = self.tt(v3(xw, 64), v3(xs, 64), bc(wd4[:, k, c], 2, [128, 16, 64]), ALU.mult, tw, xw_free[n % 2],
                            q=self.pool)
                bank, ids, rel = self.ps.take(2)
                for g in range(4):
                    t2 = self.mm(bank[:, 256 * g:256 * g + 256],
                                 [(self.Btok[:, c, 128 * g:128 * g + 128], xw[:, 256 * g:256 * g + 256])], t, rel,
                                 mark=(g == 3))
                xw_free[n % 2] = t2
                n += 1
                if step >= 2:
                    prev, cur = cur, cur + (1 if k == 0 else -1)
                else:
                    prev = cur
                dst = Sp[:, k, cur, :]
                if step == 0:
                    tp = self.cp(dst, bank, t2)
                else:
                    tp = self.tt(v3(dst, 64), v3(Sp[:, k, prev, :], 64), bc(E5[:, 2, k, c], 2, [128, 16, 64]), ALU.mult,
                                 tp, u)
                    tp = self.tt(dst, dst, bank, ALU.add, tp, t2)
                self.ps.free(ids, tp)
            t_s.append(tp)
        self.fence()
        ar.at = self.rest
        CB = [ar.take(512) for _ in range(2)]
        xd = [ar.take(1024) for _ in range(2)]
        aL = [ar.take(512) for _ in range(2)]
        M = [ar.take(512) for _ in range(4)]
        ys = [ar.take(1024) for _ in range(2)]
        tmp = ar.take(1024)
        aL_free, M_free, y_free = [None] * 2, [None] * 4, [None] * 2
        mk = [("le", "gt", "le"), ("ge", "lt", "ge")]
        t_xd, t_y, t_z = None, None, None
        for c in range(4):
            cs = slice(128 * c, 128 * c + 128)
            bank, ids, rel = self.ps.take()
            for g in range(4):
                t = self.mm(bank[:, 128 * g:128 * g + 128], [(self.BT[:, g, cs], self.CT[:, g, cs])], rel, mark=(g == 3))
            tcb = [self.tt(v3(CB[k], 128), v3(bank, 128), bc(S[mk[k][0]], 1, [128, 4, 128]), ALU.mult, t, M_free)
                   for k in range(2)]
            self.ps.free(ids, tcb)
            txd = [self.tt(v3(xd[k], 64), v3(self.xl[:, c, :], 64), bc(dt[:, c, 16 * k:16 * k + 16], 2, [128, 16, 64]),
                           ALU.mult, t_xd, q=self.pool) for k in range(2)]
            y = ys[c % 2]
            offs = []
            for k in range(2):
                bank, ids, rel = self.ps.take(2)
                for g in range(4):
                    t = self.mm(bank[:, 256 * g:256 * g + 256], [(self.CT[:, g, cs], Sp[:, k, c, 256 * g:256 * g + 256])],
                                rel, mark=(g == 3))
                offs.append((bank, ids, t))
            (bf, idf, tf), (bb, idb, tb) = offs
            ty = self.tt(v3(y, 64), v3(bf, 64), bc(E5[:, 0, 0, c], 2, [128, 16, 64]), ALU.mult, tf, y_free[c % 2])
            self.ps.free(idf, ty)
            tt2 = self.tt(v3(tmp, 64), v3(bb, 64), bc(E5[:, 0, 1, c], 2, [128, 16, 64]), ALU.mult, tb, t_y)
            self.ps.free(idb, tt2)
            ty = self.tt(y, y, tmp, ALU.add, ty, tt2)
            tt2 = self.tt(v3(tmp, 64), v3(self.xl[:, c, :], 64), bc(self.row["dskip"], 2, [128, 16, 64]), ALU.mult, ty)
            ty = self.tt(y, y, tmp, ALU.add, tt2)
            t_y = ty
            yb, idy, rely = self.ps.take(2)
            for g in range(4):
                tms = []
                for k in range(2):
                    h0 = 16 * k + 4 * g
                    t = self.tt(v3(aL[k], 128), bc(S[mk[k][1]], 1, [128, 4, 128]), bc(a[:, c, h0:h0 + 4], 2, [128, 4, 128]),
                                ALU.mult, aL_free[k], q=self.pool)
                    bank, ids, rel = self.ps.take()
                    for h in range(4):
                        t2 = self.mm(bank[:, 128 * h:128 * h + 128], [(aL[k][:, 128 * h:128 * h + 128], S[mk[k][2]])], t, rel,
                                     mark=(h == 3))
                    aL_free[k] = t2
                    mi = 2 * (g % 2) + k
                    t = self.ac(M[mi], bank, AF.Exp, t2, M_free[mi])
                    self.ps.free(ids, t)
                    tms.append(self.tt(v3(M[mi], 128), v3(M[mi], 128), bc(CB[k][:, 128 * g:128 * g + 128], 1, [128, 4, 128]),
                                       ALU.mult, t, tcb))
                for h in range(4):
                    o = slice(256 * g + 64 * h, 256 * g + 64 * h + 64)
                    t = self.mm(yb[:, o], [(M[2 * (g % 2) + k][:, 128 * h:128 * h + 128], xd[k][:, o]) for k in range(2)],
                                tms, txd, rely, mark=(h == 3))
                M_free[2 * (g % 2)] = M_free[2 * (g % 2) + 1] = t
            t_xd = t
            ty = self.tt(y, y, yb, ALU.add, t, ty)
            self.ps.free(idy, ty)
            for i in range(2):
                bank, ids, rel = self.ps.take()
                for q in range(4):
                    f = 4 * i + q
                    t = self.tr(bank[:, 128 * q:128 * q + 128], y[:, 128 * f:128 * f + 128], ty, rel, mark=(q == 3))
                z = self.zT[:, 4 * i:4 * i + 4, cs]
                u = self.tt(z, z, v3(bank, 128), ALU.mult, t)
                self.ps.free(ids, u)
            y_free[c % 2] = t
        def finish(g, r, t):
            for i in (2 * g, 2 * g + 1):
                z = self.zT[:, i, :]
                t = self.stt(z, z, V["ssd_norm"][:, i:i + 1], r, ALU.mult, ALU.mult, t)
            return t

        self.fence()
        return self.norms([[self.zT[:, 2 * g + k, :] for k in range(2)] for g in range(4)],
                          self.BT.rearrange("p a b -> p (a b)"), self.xl.rearrange("p a b -> p (a b)"), S["m256"], EPS, finish)

    def hyena(self):
        d, ar, V, S = self.d, self.ar, self.vec, self.sq
        self.fence()
        self.rings(5, 5, 2, [(d["win"][24 + j], 1024) for j in range(24)], lambda i: self.pool)
        ar.at = self.base + 12288
        vT, x1, x2 = ar.take(4096), ar.take(4096), ar.take(4096)
        Cm, Sm = ar.take(2048), ar.take(2048)
        IS0, NY = ar.take(512), ar.take(512)
        top = ar.at
        raws = [ar.take(516) for _ in range(2)]
        accs = [ar.take(512) for _ in range(2)]
        C3, S3 = v3(Cm, 512), v3(Sm, 512)
        tdft = [self.load(C3, d["dftc"]), self.load(S3, d["dfts"]), self.load(IS0, d["is0"]), self.load(v3(NY, 128), d["nyq"])]
        tz = [self.zero(r, *self.floor) for r in raws]
        dst = [v3(q, 512) for q in (vT, x1, x2)]
        v, x1, x2 = dst
        raw_free = [tz, tz]
        for j in range(24):
            i = j % 2
            (bank, ids, t), = self.proj3(self.fx, [(0, 512)])
            t = self.acp(raws[i][:, 2:514], bank, t, raw_free[i])
            self.ps.free(ids, t)
            w = V["hyw"][:, 3 * j:3 * j + 3]
            o = dst[j // 8][:, j % 8, :]
            t = self.ts(accs[i], raws[i][:, 1:513], w[:, 0:1], V["hyb"][:, j:j + 1], ALU.mult, ALU.add, t)
            t = self.stt(accs[i], raws[i][:, 2:514], w[:, 1:2], accs[i], ALU.mult, ALU.add, t)
            t = self.stt(o, raws[i][:, 3:515], w[:, 2:3], accs[i], ALU.mult, ALU.add, t)
            raw_free[i] = [t]
        self.fence()
        self.rings(8)
        ar.at = top
        h1, h2 = ar.take(512), ar.take(512)
        eo, KK = ar.take(4096), ar.take(4096)
        e, o = (v3(eo[:, 2048 * i:2048 * i + 2048], 512) for i in range(2))
        Kr, Ki = (v3(KK[:, 2048 * i:2048 * i + 2048], 512) for i in range(2))
        at2 = ar.at
        ar.at = self.base
        ut = v3(ar.take(2048), 512)
        P, Q = ar.take(512), ar.take(512)
        W = [ar.take(512) for _ in range(2)]
        ar.at = at2
        W += [ar.take(512) for _ in range(2)]
        zp, tzp, sz = self.ring.take(d["zpos"], 512, parts=33)
        w12, tw, sw = self.ring.take(d["hyw12"], 128, parts=64)

        def sine(out, bank, t, b, fr):
            t = self.ts(h1[0:64, :], bank[0:64, :], b[0:64, :], fr[0:64, :], ALU.add, ALU.mult, t)
            t = self.ts(P[0:64, :], h1[0:64, :], 1.0 / (2 * math.pi), 12582912.0, ALU.mult, ALU.add, t)
            t = self.ts(P[0:64, :], P[0:64, :], 12582912.0, None, ALU.subtract, None, t)
            for cst in (6.28125, 0.0019340515136718750, 2 * math.pi - 6.28125 - 0.0019340515136718750):
                t = self.stt(h1[0:64, :], P[0:64, :], -cst, h1[0:64, :], ALU.mult, ALU.add, t)
            t = self.ts(h1[0:64, :], h1[0:64, :], 3.1415925, -3.1415925, ALU.min, ALU.max, t)
            return self.ac(out[0:64, :], h1[0:64, :], AF.Sin, t)

        bank, ids, rel = self.ps.take()
        t = self.mm(bank[0:64, :], [(w12[0:33, 0:64], zp)], tzp, tw, rel)
        self.ring.free(sz, t)
        t = sine(h2, bank, t, V["hyb1"], V["fr0"])
        self.ps.free(ids, self.dve.last())
        bank, ids, rel = self.ps.take()
        t = self.mm(bank[0:64, :], [(w12[0:64, 64:128], h2[0:64, :])], t, rel)
        self.ring.free(sw, t)
        th2 = sine(h2, bank, t, V["hyb2"], V["fr1"])
        self.ps.free(ids, self.dve.last())
        self.pe.wait(tdft)

        K_free, e_free, u_free = [None], [None], [None]
        for hf in range(2):
            for od in range(2):
                w3, tw3, s3 = self.ring.take(d["hyw3"][od, hf], parts=64)
                decs = [self.ring.take(d["dec"][hf, i]) for i in range(2)]
                tPQ = [self.pool.last()]
                for tt in range(4):
                    dec = decs[tt // 2]
                    dm = dec[0][:, 512 * (tt % 2):512 * (tt % 2) + 512]
                    tp = []
                    for buf, c0 in ((P, 0), (Q, 512)):
                        bank, ids, rel = self.ps.take()
                        t = self.mm(bank, [(h2[0:64, 128 * tt:128 * tt + 128], w3[:, c0:c0 + 512])], tw3, th2, rel)
                        u = self.tt(buf, bank, dm, ALU.mult, t, dec[1], tPQ)
                        self.ps.free(ids, u)
                        tp.append(u)
                    if tt == 0:
                        tp.append(self.zero(Q[0:1, :], tp, q=self.dve))
                    tPQ = [self.tt(e[:, tt, :], P, Q, ALU.add, tp, e_free, q=self.pool),
                           self.tt(o[:, tt, :], P, Q, ALU.subtract, tp, e_free, q=self.pool)]
                self.ring.free(s3, t)
                for i in range(2):
                    self.ring.free(decs[i][2], u)
                tk = []
                for ft in range(4):
                    fs = slice(128 * ft, 128 * ft + 128)
                    for Kx, Mx, x in ((Kr, C3, e), (Ki, S3, o)):
                        bank, ids, rel = self.ps.take()
                        pairs = [(Mx[:, tt, fs], x[:, tt, :]) for tt in range(4)]
                        if Kx is Ki and ft == 0:
                            pairs += [(NY[:, 128 * tt:128 * tt + 128], e[:, tt, :]) for tt in range(4)]
                        t = self.mm(bank, pairs, tPQ, rel)
                        u = self.act.do(lambda q, o_=Kx[:, ft, :], b_=bank: q.mul(o_, b_, 2.0 / 1024), t, K_free)
                        self.ps.free(ids, u)
                        if ft == 0:
                            u = self.ts(Kx[0:1, 0, :], Kx[0:1, 0, :], 0.5, None, ALU.mult, None, u)
                        tk.append(u)
                te = self.pe.last()
                tu = []
                for tt in range(4):
                    bank, ids, rel = self.ps.take()
                    for j in range(4):
                        src = v[:, 4 * hf + j, 128 * tt:128 * tt + 128]
                        t = self.tr(bank[:, 128 * j:128 * j + 128], src, rel, tu_in if od else None, mark=(j == 3))
                    u = self.acp(ut[:, tt, :], bank, t, u_free)
                    self.ps.free(ids, u)
                    tu.append(u)
                ty = []
                for ft in range(4):
                    fs = slice(128 * ft, 128 * ft + 128)
                    br, idr, rr = self.ps.take()
                    t1 = self.mm(br, [(C3[:, tt, fs], ut[:, tt, :]) for tt in range(4)], tu, rr)
                    bi, idi, ri = self.ps.take()
                    pairs = [(S3[:, tt, fs], ut[:, tt, :]) for tt in range(4)]
                    if ft == 0:
                        pairs += [(NY[:, 128 * tt:128 * tt + 128], ut[:, tt, :]) for tt in range(4)]
                    t2 = self.mm(bi, pairs, ri)
                    a1 = self.tt(W[0], br, Kr[:, ft, :], ALU.mult, t1, tk, ty, self.pool.last())
                    a2 = self.tt(W[1], bi, Ki[:, ft, :], ALU.mult, t2)
                    a3 = self.tt(W[2], br, Ki[:, ft, :], ALU.mult)
                    a4 = self.tt(W[3], bi, Kr[:, ft, :], ALU.mult)
                    self.ps.free(idr, a3)
                    self.ps.free(idi, a4)
                    y1 = self.tt(e[:, ft, :], W[0], W[1], ALU.subtract, a4, te, q=self.pool)
                    y2 = self.tt(o[:, ft, :], W[2], W[3], ALU.add, a4, q=self.pool)
                    if ft == 0:
                        y1 = self.cp(e[0:1, 0, :], W[0][0:1, :], y1, y2)
                        y2 = self.cp(o[0:1, 0, :], W[1][0:1, :], y1, y2)
                    ty += [y1, y2]
                K_free = [self.dve.last()]
                u_free = [t2]
                outs = []
                for j in range(4):
                    bank, ids, rel = self.ps.take()
                    js = slice(128 * j, 128 * j + 128)
                    pairs = [(e[:, ft, js], C3[:, ft, :]) for ft in range(4)]
                    pairs += [(o[:, ft, js], S3[:, ft, :] if ft else IS0) for ft in range(4)]
                    t = self.mm(bank, pairs, ty, rel)
                    m = 4 * hf + j
                    hb = V["hbias"][:, 8 * od + m:8 * od + m + 1]
                    turned = v[:, m, :].rearrange("p (c r) -> p r c", r=8)
                    if od == 0:
                        u = self.stt(W[j], v[:, m, :], hb, bank, ALU.mult, ALU.add, t)
                        self.ps.free(ids, u)
                        outs.append(self.tt(turned, v3(W[j], 64), v3(x1[:, m, :], 64), ALU.mult, u))
                    else:
                        u = self.stt(v[:, m, :], v[:, m, :], hb, bank, ALU.mult, ALU.add, t)
                        self.ps.free(ids, u)
                        outs.append(self.tt(v3(x2[:, m, :], 64), v3(x2[:, m, :], 64), turned, ALU.mult, u))
                e_free = [t]
                tu_in = outs
        def finish(m, r, t):
            return self.stt(x2[:, m, :], x2[:, m, :], V["hy_norm"][:, m:m + 1], r, ALU.mult, ALU.mult, t)

        u = self.norms([[x2[:, m, :]] for m in range(8)], KK, eo, S["m64"], EPS, finish, self.dve.last(), self.pe.last(),
                       self.pool.last())
        self.x2 = x2
        return u

    def out_projection(self, t):
        d, ar = self.d, self.ar
        self.fence()
        ar.at = self.base
        h = v3(ar.take(4096), 512)
        th = self.load(h, d["xT"])
        for j in range(8):
            rhs = lambda k, a, b: self.zT[:, k, :] if k < 8 else self.x2[:, k - 8, :]
            (bank, ids, t), = self.proj([(d["wout"][j, i], 1024) for i in range(2)], rhs, [(0, 512)])
            t = self.stt(h[:, j, :], bank, self.mod1[:, 16 + j, 0:1], h[:, j, :], ALU.mult, ALU.add, t, th)
            self.ps.free(ids, t)
        self.h = h
        return t

    def peer(self, t):
        d, ar, V, S = self.d, self.ar, self.vec, self.sq
        m, h = self.mod1, self.h
        self.fence()
        ar.at = self.base + 4096
        fh, fl = [ar.rounded(512) for _ in range(8)], [ar.rounded(512) for _ in range(8)]
        ar.at = self.base + 12288
        low = ar.at
        self.rings(4, 4, 2, [(d["wq"][n], 1024) for n in range(16)], lambda i: self.pool)
        sqt = [ar.take(512) for _ in range(2)]
        rstd, g2 = ar.take(512), ar.take(8)
        ft = [ar.take(512) for _ in range(2)]
        tg = self.gains(g2, m, None, 32, V["norm2"], 0)
        r = self.rms(lambda k: h[:, k, :], 8, rstd, sqt, S["m1024"], EPS, [(0, 512)], t)
        tf, free = [], [None, None]
        for k in range(8):
            x = ft[k % 2]
            t = self.tt(x, h[:, k, :], rstd, ALU.mult, r, free[k % 2])
            t = self.ac(x, x, AF.Identity, t, tg, scale=g2[:, k:k + 1], bias=m[:, 24 + k, 0:1])
            free[k % 2] = self.parts(x, fh[k], fl[k], t)[1]
            tf.append(free[k % 2])
        fx = lambda k, a, b: (fh[k][:, a:b], fl[k][:, a:b])
        self.fence()
        ar.at = low
        EG = [ar.take(512) for _ in range(3)]
        kt = ar.take(256)
        tk = self.load(kt, d["subkeys"])
        at1 = ar.at
        qs = [ar.take(512) for _ in range(2)]
        sc = [ar.take(512) for _ in range(3)]
        s2 = [ar.take(512) for _ in range(2)]
        val, idx = v3(ar.take(1024), 256), v3(ar.take(1024).bitcast(U32), 256)
        fidx = v3(ar.take(1024), 256)
        q_free, sc_free = [None, None], [None] * 3
        lag, ti = [], []

        def scores(n, t):
            q = qs[n % 2]
            bank, ids, rel = self.ps.take()
            for tt in range(4):
                t2 = self.mm(bank[:, 128 * tt:128 * tt + 128],
                             [(q[:, 128 * tt:128 * tt + 128], kt[:, 128 * (n % 2):128 * (n % 2) + 128])], t, tk, rel,
                             mark=(tt == 3))
            q_free[n % 2] = t2
            s = sc[n % 3]
            u = self.acp(s, bank, t2, sc_free[n % 3])
            self.ps.free(ids, u)
            groups = [(s[:, 128 * tt:128 * tt + 128], val[:, tt, 16 * n:16 * n + 16], idx[:, tt, 16 * n:16 * n + 16],
                       s2[n % 2][:, 128 * tt:128 * tt + 128]) for tt in range(4)]
            sc_free[n % 3] = self.top16(groups, u)

        for n in range(16):
            (bank, ids, t), = self.proj3(fx, [(0, 512)], tf)
            t = self.acp(qs[n % 2], bank, t, q_free[n % 2])
            self.ps.free(ids, t)
            lag.append((n, t))
            if n:
                scores(*lag.pop(0))
        scores(*lag.pop(0))
        t = self.cp(fidx, idx, sc_free[0])
        cand, oh = ar.take(2048), ar.take(2048)
        best, ci, hi, hf = ar.take(128), ar.take(128).bitcast(U32), ar.take(128).bitcast(U32), ar.take(128)
        mx, esel, gate = ar.take(8), ar.take(256), ar.take(128)
        at2 = ar.at
        ar.at = at1
        NO = 3
        o1 = [ar.take(512) for _ in range(NO)]
        o2 = [ar.take(512) for _ in range(NO)]
        ar.at = at2
        stage = [ar.take(4096) for _ in range(2)]
        f1, st_free, t_e = [None] * NO, [None] * 2, []
        gd = d["gates"]
        t_w = []
        self.fence()

        def choose(tt):
            t = self.dve.last()
            v4_ = val[:, tt, :].rearrange("p (h s k) -> p h s k", h=8, s=2)
            f4 = fidx[:, tt, :].rearrange("p (h s k) -> p h s k", h=8, s=2)
            ts = []
            for hd in range(8):
                c = cand[:, 256 * hd:256 * hd + 256]
                ts.append(self.tt(v3(c, 16), bc(v4_[:, hd, 0, :], 2, [128, 16, 16]), bc(v4_[:, hd, 1, :], 1, [128, 16, 16]),
                                  ALU.add, t))
                if hd % 2:
                    yield
            groups = [tuple(x[:, w * hd:w * hd + w] for x, w in ((cand, 256), (best, 16), (ci, 16), (oh, 256)))
                      for hd in range(8)]
            for i in range(0, 8, 2):
                t = self.top16(groups[i:i + 2], ts[-1])
                yield
            b3, g3 = v3(best, 16), v3(gate, 16)
            tg = self.tt(g3, b3, b3[:, :, 0:1].to_broadcast([128, 8, 16]), ALU.subtract, t, self.pe.last())
            tg = self.ac(gate, gate, AF.Exp, tg)
            o4 = v4(oh, 16, 16)
            for s in range(2):
                if s == 0:
                    t = self.ts(hi, ci, 4, None, ALU.logical_shift_right, None, t)
                else:
                    t = self.ts(hi, ci, 15, None, ALU.bitwise_and, None, t)
                t = self.cp(hf, hi, t)
                h3 = v3(hf, 16)
                t = self.tt(o4, bc(h3, 3, [128, 8, 16, 16]), self.row["i16"].unsqueeze(1).unsqueeze(1).to_broadcast(
                    [128, 8, 16, 16]), ALU.is_equal, t)
                t = self.tt(o4, o4, bc(f4[:, :, s, :], 2, [128, 8, 16, 16]), ALU.mult, t)
                yield
                t = self.red(esel[:, 128 * s:128 * s + 128], v3(oh, 16), ALU.add, t)
                yield
            tg = self.red(mx, g3, ALU.add, tg)
            tg = self.rec(mx, mx, tg)
            tg = self.tt(g3, g3, bc(mx, 2, [128, 8, 16]), ALU.mult, tg)
            bank, ids, rel = self.ps.take()
            for i, src in enumerate((esel[:, 0:128], esel[:, 128:256], gate)):
                t2 = self.tr(bank[:, 128 * i:128 * i + 128], src, t, tg, rel, mark=(i == 2))
            us = [self.cp(EG[i][:, 128 * tt:128 * tt + 128], bank[:, 128 * i:128 * i + 128], t2) for i in range(3)]
            self.ps.free(ids, us)
            t_e.append(us[-1])

        def spread(ch, te):
            sg = v3(stage[ch % 2], 32)
            tcp = []
            for q in range(8):
                bank, ids, rel = self.ps.take()
                tk, n = 32 * ch + 4 * q, (8 * ch + q) % NO
                if q % 4 == 3:
                    tb = self.tt(v3(o2[n], 128), S["iota"].unsqueeze(1).to_broadcast([128, 4, 128]),
                                 bc(EG[1][:, tk:tk + 4], 2, [128, 4, 128]), ALU.is_equal, te, f1[n])
                for i in range(4):
                    o, k = slice(128 * i, 128 * i + 128), tk + i
                    if q % 4 < 3:
                        tb = self.ts(o2[n][:, o], S["iota"], EG[1][:, k:k + 1], None, ALU.is_equal, None, te, f1[n],
                                     q=self.pool)
                    ta = self.ts(o1[n][:, o], S["iota"], EG[0][:, k:k + 1], EG[2][:, k:k + 1], ALU.is_equal, ALU.mult, te, f1[n])
                    tm = self.mm(bank[:, o], [(o2[n][:, o], o1[n][:, o])], ta, tb, rel)
                f1[n] = tm
                u = self.acp(sg[:, :, 4 * q:4 * q + 4], bank.rearrange("p (t e) -> p e t", e=128), tm, st_free[ch % 2])
                self.ps.free(ids, u)
                tcp.append(u)
                yield
            w = self.sp.dma(gd[ch], stage[ch % 2], self.dsem(), tcp)
            st_free[ch % 2] = w
            t_w.append(w)

        for _ in choose(0):
            pass
        for tt in range(4):
            nxt = choose(tt + 1) if tt < 3 else iter(())
            te = t_e[tt]
            for ch in range(4 * tt, 4 * tt + 4):
                for _ in spread(ch, te):
                    next(nxt, None)
            for _ in nxt:
                pass
        self.fence(*t_w)
        ar.at = low
        NG = 64
        srcs = [(d["peeru"][n], 1024) for n in range(2)]
        for gi in range(NG):
            if gi + 1 < NG:
                srcs += [(d["peeru"][n], 1024) for n in range(2 * gi + 2, 2 * gi + 4)]
            srcs += [(d["peerv"][n], 1024) for n in range(2 * gi, 2 * gi + 2)]
        Ah, Al = [ar.rounded(512) for _ in range(4)], [ar.rounded(512) for _ in range(4)]
        gl, pr = [ar.take(512) for _ in range(3)], [ar.take(512) for _ in range(3)]
        Gb, Gs = [ar.take(2048) for _ in range(2)], [self.dsem() for _ in range(2)]
        steps = self.modulations2()
        self.rings(6, 8, 5, srcs, lambda i: self.pool)
        A_free, x_free, G_free = [None] * 4, [None] * 3, [[], []]
        tacc = [None] * 8
        tA, tG = {}, {}

        def fetch(b):
            tG[b] = self.sp.dma(v3(Gb[b % 2], 128), gd[:, :, 128 * b:128 * b + 128].rearrange("c p x -> p c x"), Gs[b % 2],
                                G_free[b % 2])

        def up(gi):
            b = gi // 2
            if gi % 2 == 0 and b + 1 < NG // 2:
                fetch(b + 1)
            G4 = Gb[b % 2].rearrange("p (c e t) -> p c e t", c=16, e=4)
            for n in (2 * gi, 2 * gi + 1):
                (bank, ids, t), = self.proj3(fx, [(0, 512)])
                x, y = gl[n % 3], pr[n % 3]
                t = self.ac(x, bank, AF.Gelu, t, x_free[n % 3])
                self.ps.free(ids, t)
                t = self.tt(v3(y, 32), v3(x, 32), G4[:, :, n % 4, :], ALU.mult, t, tG[b])
                G_free[b % 2] = [t]
                tA[n] = list(self.parts(y, Ah[n % 4], Al[n % 4], t, A_free[n % 4]))
                x_free[n % 3] = tA[n]

        def down(gi):
            ns = (2 * gi, 2 * gi + 1)
            vs = [self.stream.next() for _ in ns]
            for j in range(8):
                bank, ids, rel = self.ps.take()
                js = slice(128 * j, 128 * j + 128)
                t = self.mm3(bank, [((w[0][:, js], w[1][:, js]), (Ah[n % 4], Al[n % 4])) for w, n in zip(vs, ns)],
                             [w[2] for w in vs], [tA[n] for n in ns], rel)
                tacc[j] = self.stt(h[:, j, :], bank, m[:, 40 + j, 0:1], h[:, j, :], ALU.mult, ALU.add, t, tacc[j])
                self.ps.free(ids, tacc[j])
            for n, w in zip(ns, vs):
                self.stream.free(w[3], t)
                A_free[n % 4] = t

        fetch(0)
        up(0)
        for gi in range(NG):
            if gi + 1 < NG:
                up(gi + 1)
            for step in steps[2 * gi:2 * gi + 2]:
                step()
            down(gi)
        self.fence()
        ar.at = low
        sqt = [ar.take(512) for _ in range(2)]
        rstd = ar.take(512)
        self.h = v3(ar.take(4096), 512)
        r = self.rms(lambda k: h[:, k, :], 8, rstd, sqt, S["m1024"], EPS, [(0, 512)], *tacc)
        for j in range(8):
            t = self.stt(self.h[:, j, :], h[:, j, :], V["final_norm"][:, j:j + 1], rstd, ALU.mult, ALU.mult, r)
        self.fence()
        self.rings(13)
        return t

    def top16(self, groups, t):
        D = self.dve.do
        t1 = [D(lambda e, a=a, v=v: e.max(v[:, 0:8], a), t) for a, v, x, tmp in groups]
        t2 = [D(lambda e, a=a, v=v, tmp=tmp: e.match_replace(tmp, v[:, 0:8], a, LOW), u)
              for (a, v, x, tmp), u in zip(groups, t1)]
        for a, v, x, tmp in groups:
            D(lambda e, a=a, v=v, x=x: e.max_index(x[:, 0:8], v[:, 0:8], a))
        t3 = [D(lambda e, v=v, tmp=tmp: e.max(v[:, 8:16], tmp), u) for (a, v, x, tmp), u in zip(groups, t2)]
        t4 = [D(lambda e, v=v, x=x, tmp=tmp: e.max_index(x[:, 8:16], v[:, 8:16], tmp), u)
              for (a, v, x, tmp), u in zip(groups, t3)]
        return t4[-1]

    def affine(self, X, fh, fl, tmp, m, j0, segs, *toks):
        one, n = self.ones16, segs[-1][1]
        t1 = [self.ts(one[:, 8 * s:8 * s + 8], m[:, j0 + 8:j0 + 16, s], 1.0, None, ALU.add, None, self.act.last())
              for s in range(len(segs))]
        free, th, tX = [None, None], [], []
        for k in range(8):
            x = tmp[k % 2][:, 0:n]
            for s, (a, b) in enumerate(segs):
                u = self.ac(x[:, a:b], X[:, k, a:b], AF.Identity, t1, free[k % 2], *toks,
                            scale=one[:, 8 * s + k:8 * s + k + 1], bias=m[:, j0 + k, s:s + 1])
            free[k % 2] = self.parts(x, fh[k][:, 0:n], fl[k][:, 0:n], u)[1]
            th.append(free[k % 2])
            tX.append(u)
        return th, tX

    def residual_norm(self, X, x3, m, jg, g, b, segs, rstd, sqt, *toks):
        n = segs[-1][1]
        t = None
        for k in range(8):
            x = X[:, k, 0:n]
            ta = self.act.do(lambda e, x=x: e.mul(x, x, ALPHA), *toks)
            got = self.proj3(x3, segs, *toks)
            for s, ((bank, ids, t), (lo, hi)) in enumerate(zip(got, segs)):
                x = X[:, k, lo:hi]
                t = self.stt(x, bank[:, 0:hi - lo], m[:, jg + k, s:s + 1], x, ALU.mult, ALU.add, t, ta)
                self.ps.free(ids, t)
        return self.layer_norm(X, g, b, segs, rstd, sqt, t)

    def layer_norm(self, X, g, b, segs, rstd, sqt, t):
        n = segs[-1][1]
        means = []
        for lo, hi in segs:
            bank, ids, rel = self.ps.take()
            u = self.mm(bank[:, 0:hi - lo], [(self.sq["m1024"], X[:, k, lo:hi]) for k in range(8)], t, rel)
            means.append((bank, ids, u))
        for k in range(8):
            for (bank, ids, u), (lo, hi) in zip(means, segs):
                t = self.tt(X[:, k, lo:hi], X[:, k, lo:hi], bank[:, 0:hi - lo], ALU.subtract, u)
        for bank, ids, u in means:
            self.ps.free(ids, t)
        r = self.rms(lambda k: X[:, k, 0:n], 8, rstd, [s[:, 0:n] for s in sqt], self.sq["m1024"], LN_EPS, segs, t)
        for k in range(8):
            x = X[:, k, 0:n]
            t = self.tt(x, x, rstd[:, 0:n], ALU.mult, r)
            t = self.ac(x, x, AF.Identity, t, scale=g[:, k:k + 1], bias=b[:, k:k + 1])
        return t

    def turn(self, x, R, cos, sin, tmp, t, p=128):
        bank, ids, rel = self.ps.take()
        u = self.mm(bank[0:p, :], [(R[0:p, 0:p], x)], t, rel)
        w = self.tt(tmp[0:p, :], bank[0:p, :], sin[0:p, :], ALU.mult, u, self.pool.last())
        self.ps.free(ids, w)
        u = self.tt(x, x, cos[0:p, :], ALU.mult, u, q=self.pool)
        return self.tt(x, x, tmp[0:p, :], ALU.add, u, w, q=self.pool)

    def attend(self, units, P, PT, st, P2=()):
        P, nP = [*P, *P2], len(P)
        P_free, PT_free, st_free = [None] * len(P), [None] * len(PT), [None] * len(st)
        fresh, pend, late, cnt, banks = [], [], [], [0, 0, 0, 0], {}

        def first(u):
            ps = []
            for which, segs in enumerate(u["segs"]):
                n = sum(x[3] for x in segs)
                bank, ids, rel = self.ps.take(2)
                for i, (q, k, c, w) in enumerate(segs):
                    t = self.mm(bank[:, c:c + w], [(q, k)], rel, u["toks"], mark=True)
                for c, mk in u.get("masks", ()):
                    t = self.tt(bank[:, c:c + 128], bank[:, c:c + 128], self.sq[mk], ALU.add, t)
                pi = nP + cnt[3] % 2 if which else cnt[0] % nP
                cnt[3 if which else 0] += 1
                si = cnt[1] % len(st)
                cnt[1] += 1
                p, s = P[pi], st[si]
                t = self.red(s[:, 0:1], bank[:, 0:n], ALU.max, t, st_free[si])
                sc = u["scale"]
                if u.get("sink") is not None:
                    t = self.ts(s[:, 0:1], s[:, 0:1], sc, u["sink"], ALU.mult, ALU.max, t)
                    t = self.ts(s[:, 0:1], s[:, 0:1], -1.0, None, ALU.mult, None, t)
                else:
                    t = self.ts(s[:, 0:1], s[:, 0:1], -sc, None, ALU.mult, None, t)
                t = self.ac(p[:, 0:n], bank[:, 0:n], AF.Exp, t, P_free[pi], scale=sc, bias=s[:, 0:1], accum=s[:, 1:2])
                self.ps.free(ids, t)
                if u.get("sink") is not None:
                    t = self.ac(s[:, 2:3], u["sink"], AF.Exp, t, bias=s[:, 0:1])
                ps.append((p, s, pi, si, n, t))
            return ps

        def weights(u, ps):
            for i, (p, s, pi, si, n, t) in enumerate(ps):
                if u.get("sink") is not None:
                    t = self.tt(s[:, 1:2], s[:, 1:2], s[:, 2:3], ALU.add, t)
                ps[i] = p, s, pi, si, n, self.rec(s[:, 1:2], s[:, 1:2], t)
            p, s, pi, si, n, t = ps[0]
            if len(ps) == 2:
                p2, s2, pi2, si2, _, t2 = ps[1]
                t2 = self.tt(s2[:, 1:2], s2[:, 1:2], self.lam, ALU.mult, t2)
                t2 = self.ts(p2[:, 0:n], p2[:, 0:n], s2[:, 1:2], None, ALU.mult, None, t2)
                t = self.stt(p[:, 0:n], p[:, 0:n], s[:, 1:2], p2[:, 0:n], ALU.mult, ALU.subtract, t, t2)
                P_free[pi2] = st_free[si2] = t
            else:
                t = self.ts(p[:, 0:n], p[:, 0:n], s[:, 1:2], None, ALU.mult, None, t)
            st_free[si] = t
            return p, pi, n, t

        def turned(u, p, pi, n, t):
            xi = cnt[2] % len(PT)
            cnt[2] += 1
            pt = PT[xi]
            bank, ids, rel = self.ps.take(2)
            for c in range(n // 128):
                t2 = self.tr(bank[:, 128 * c:128 * c + 128], p[:, 128 * c:128 * c + 128], t, rel, mark=True)
            P_free[pi] = t2
            h = min(n, 512)
            ta = self.acp(pt[:, 0:h], bank[:, 0:h], t2, PT_free[xi])
            tb = self.cp(pt[:, h:n], bank[:, h:n], t2, PT_free[xi]) if n > h else None
            self.ps.free(ids, [ta, tb])
            return n, pt, xi, ta, tb

        def values(u, n, pt, xi, ta, tb):
            out, p0, M, col, width, key, lastu = u["out"]
            if key not in banks:
                banks[key] = self.ps.take()
            ob, oid, orel = banks[key]
            t = self.mm(ob[p0:p0 + M, col:col + 128],
                        [(v, pt[:, 128 * c:128 * c + 128]) for c, v in enumerate(u["vals"])], ta, tb, orel)
            PT_free[xi] = t
            if lastu and isinstance(out, tuple):
                t = list(self.parts(ob[p0:p0 + M, 0:width], *out, t))
            elif lastu:
                t = self.acp(out, ob[p0:p0 + M, 0:width], t)
            if lastu:
                self.ps.free(oid, t)
                del banks[key]
            return t

        t = None
        for u in [*units, None, None, None, None]:
            if u is not None:
                fresh.append((u, first(u)))
            if len(fresh) > 1 or (u is None and fresh):
                v, a = fresh.pop(0)
                pend.append((v, weights(v, a)))
            if len(pend) > 1 or (u is None and pend):
                v, a = pend.pop(0)
                late.append((v, turned(v, *a)))
            if len(late) > 1 or (not pend and late):
                v, a = late.pop(0)
                t = values(v, *a)
        for v, a in late:
            t = values(v, *a)
        return t

    def feed(self, i, X, m, segs, top, t, V):
        d, ar = self.d, self.ar
        n = segs[-1][1]
        self.fence()
        ar.at = top
        fh, fl = [ar.rounded(n) for _ in range(8)], [ar.rounded(n) for _ in range(8)]
        hh, hl = [ar.rounded(n) for _ in range(4)], [ar.rounded(n) for _ in range(4)]
        raws, accs, hid = [ar.take(776) for _ in range(2)], [ar.take(n) for _ in range(2)], [ar.take(n) for _ in range(2)]
        srcs, NG = [], 11
        for gi in range(NG + 1):
            if gi < NG:
                for j in (2 * gi, 2 * gi + 1):
                    srcs += [(d["wgate"][22 * i + j], 1024), (d["wup"][22 * i + j], 1024)]
            if gi:
                srcs += [(d["wdown"][i, j], 1024) for j in (2 * gi - 2, 2 * gi - 1)]
        self.rings(6, 6, 4, srcs, lambda i: self.pool)
        th, tX = self.affine(X, fh, fl, hid, m, 24, segs)
        tX = [self.ts(X[:, k, 0:n], X[:, k, 0:n], ALPHA, None, ALU.mult, None, u) for k, u in enumerate(tX)]
        tz = [self.zero(r) for r in raws]
        raw_free, acc_free, hid_free, part_free = [tz, tz], [None, None], th[6:8], [None] * 4
        fx = lambda k, a, b: (fh[k][:, a:b], fl[k][:, a:b])
        tH = {}

        def up(gi):
            for j in (2 * gi, 2 * gi + 1):
                r, acc, x = raws[j % 2], accs[j % 2], hid[j % 2]
                tc = []
                for (bank, ids, t), off, (a, b) in zip(self.proj3(fx, segs, th), (2, 518), segs):
                    u = self.acp(r[:, off:off + b - a], bank[:, 0:b - a], t, raw_free[j % 2])
                    self.ps.free(ids, u)
                    tc.append(u)
                w = V["fcw"][:, 66 * i + 3 * j:66 * i + 3 * j + 3]
                last = []
                for base, (a, b) in zip((1, 517), segs):
                    o, w0 = acc[:, a:b], b - a
                    t = self.ts(o, r[:, base:base + w0], w[:, 0:1], V["fcb"][:, 22 * i + j:22 * i + j + 1], ALU.mult, ALU.add,
                                tc, acc_free[j % 2])
                    for k in (1, 2):
                        t = self.stt(o, r[:, base + k:base + k + w0], w[:, k:k + 1], o, ALU.mult, ALU.add, t)
                    last.append(t)
                raw_free[j % 2] = last
                ts = self.ac(acc, acc, AF.Silu, last)
                us = []
                for (bank, ids, t), (a, b) in zip(self.proj3(fx, segs), segs):
                    u = self.tt(x[:, a:b], acc[:, a:b], bank[:, 0:b - a], ALU.mult, t, ts, hid_free[j % 2])
                    self.ps.free(ids, u)
                    us.append(u)
                acc_free[j % 2] = us
                tH[j] = list(self.parts(x, hh[j % 4], hl[j % 4], us, part_free[j % 4]))
                hid_free[j % 2] = tH[j]

        def down(gi, tX):
            js = (2 * gi, 2 * gi + 1)
            ws = [self.stream.next() for _ in js]
            out = []
            for k in range(8):
                ks = slice(128 * k, 128 * k + 128)
                for s, (a, b) in enumerate(segs):
                    bank, ids, rel = self.ps.take()
                    t = self.mm3(bank[:, 0:b - a], [((w[0][:, ks], w[1][:, ks]), (hh[j % 4][:, a:b], hl[j % 4][:, a:b]))
                                                    for w, j in zip(ws, js)], [w[2] for w in ws], [tH[j] for j in js], rel)
                    x = X[:, k, a:b]
                    u = self.stt(x, bank[:, 0:b - a], m[:, 40 + k, s:s + 1], x, ALU.mult, ALU.add, t, tX)
                    self.ps.free(ids, u)
                    out.append(u)
            for j, w in zip(js, ws):
                self.stream.free(w[3], t)
                part_free[j % 4] = t
            return out

        up(0)
        for gi in range(NG):
            if gi + 1 < NG:
                up(gi + 1)
            tX = down(gi, tX)
        self.fence()
        self.rings(13)
        ar.at = top
        rstd, sqt = ar.take(768), [ar.take(768) for _ in range(2)]
        return self.layer_norm(X, V["ln2g"][:, 8 * i:8 * i + 8], V["ln2b"][:, 8 * i:8 * i + 8], segs, rstd, sqt, tX)

    def modulations2(self):
        cb = [self.condition(self.ar.take(1024), 2 + i) for i in range(2)]
        junk = self.ar.take(1024)
        self.mod2, steps = [], []
        for i in range(2):
            m, step, done = self.modulation(1 + i, "wmod2", 48 * i, self.vec["bmod2"][:, 48 * i:48 * i + 48], cb, junk)
            self.mod2.append(m)
            both = 48 if i == 0 else 16
            steps += [lambda j=j, step=step, both=both: step(j, j < both) for j in range(48)]
            if i == 0:
                steps.append(lambda done=done: done(0, 48, True))
            else:
                steps += [lambda done=done: done(0, 16, True), lambda done=done: done(16, 48, False)]
        return steps

    def second(self, alone):
        d, ar, V, S = self.d, self.ar, self.vec, self.sq
        seg2, seg1 = [(0, 512), (512, 768)], [(0, 512)]
        if alone:
            ar.at = self.base + 16384
            for step in self.modulations2():
                step()
        m, m1 = self.mod2
        self.fence()
        ar.at = self.base
        X = v3(ar.take(6144), 768)
        assert ar.at <= self.base + 8192
        if alone:
            tx = self.load(X[:, :, 0:512], d["xT"])
        else:
            tx = self.cp(X[:, :, 0:512], self.h, self.floor)
        tc = self.load(X[:, :, 512:768], d["ctxT2"])
        self.fence()
        self.ones16 = ar.take(16)
        lamb = ar.take(8)
        sub = ar.take(1)
        st = [ar.take(4) for _ in range(6)]
        top = ar.at
        fh, fl = [ar.rounded(768) for _ in range(8)], [ar.rounded(768) for _ in range(8)]
        qa, kva, kr = v3(ar.take(1536), 768), ar.take(768), ar.take(768)
        qs, ks, Vs = v3(ar.take(3072), 768), ar.take(768), v3(ar.take(768), 128)
        Vm1, wkv, rope = ar.take(3072), ar.take(1024), ar.take(2048)
        Vm = v3(Vm1, 512)
        tmp = ar.take(512)
        P = [ar.take(768) for _ in range(3)]
        rstd, sqt = P[0], P[1:3]
        self.rings(4, 4, 2, [(d["abin"][j], 1024) for j in (0, 1, 6, 8, 2, 3, 4, 5, 7, 9)], lambda i: self.pool)
        trp, twk = self.load(rope, d["rope"]), self.load(wkv, d["wkvb"])
        c96, s96, c128, s128 = (rope[:, 512 * i:512 * i + 512] for i in range(4))
        th, _ = self.affine(X, fh, fl, [Vm1[:, 768 * i:768 * i + 768] for i in range(2)], m, 0, seg2, tx, tc)
        fx = lambda k, a, b: (fh[k][:, a:b], fl[k][:, a:b])

        def project(out, p=128):
            ts = []
            for (bank, ids, t), (a, b) in zip(self.proj3(fx, seg2, th), seg2):
                u = self.acp(out[0:p, a:b], bank[0:p, 0:b - a], t)
                self.ps.free(ids, u)
                ts.append(u)
            return ts

        t0 = [project(qa[:, j, :]) for j in range(2)]
        r = self.rms(lambda k: qa[:, k, :], 2, rstd, sqt, S["m256"], EPS, seg2, t0)
        tq = [self.stt(qa[:, k, :], qa[:, k, :], V["qn"][:, k:k + 1], rstd, ALU.mult, ALU.mult, r) for k in range(2)]
        t0 = project(kva)
        r = self.rms(lambda k: kva, 1, rstd, sqt, S["m128"], EPS, seg2, t0, tq)
        tk = self.stt(kva, kva, V["kvn"], rstd, ALU.mult, ALU.mult, r)
        t0 = project(kr, 96)
        tkr = self.turn(kr[0:96, 0:512], S["r96"], c96, s96, tmp, [t0, trp], 96)
        tv = []
        for c in range(6):
            bank, ids, rel = self.ps.take()
            t = self.mm(bank, [(kva[:, 128 * c:128 * c + 128], wkv[:, 512:1024])], tk, twk, rel)
            u = self.acp(Vm[:, c, :], bank, t)
            self.ps.free(ids, u)
            tv.append(u)
        ts_w = []
        for j in range(4):
            t0 = project(qs[:, j, :])
            ts_w.append([t0, self.turn(qs[:, j, 0:512], S["r128"], c128, s128, tmp, t0)])
        t0 = project(ks)
        ts_w.append([t0, self.turn(ks[:, 0:512], S["r128"], c128, s128, tmp, t0)])
        hi, lo, tw, s = self.stream.next()
        for c in range(6):
            bank, ids, rel = self.ps.take()
            cs = slice(128 * c, 128 * c + 128)
            t = self.mm3(bank[:, 0:128], [((fh[k][:, cs], fl[k][:, cs]), tuple(w[:, 128 * k:128 * k + 128] for w in (hi, lo)))
                                          for k in range(8)], tw, rel)
            u = self.acp(Vs[:, c, :], bank[:, 0:128], t)
            self.ps.free(ids, u)
            ts_w.append(u)
        self.stream.free(s, t)
        self.fence()
        self.rings(9)
        PT = [ar.take(768) for _ in range(2)]
        qb, kb = [ar.take(768) for _ in range(2)], [ar.take(768) for _ in range(2)]
        qk_free = [None, None]
        scale = 96 ** -0.5

        def prepare(h):
            q, k = qb[h % 2], kb[h % 2]
            w, tw, s = self.ring.take(d["wqb"][h], 192)
            ts = []
            for a, b in seg2:
                bank, ids, rel = self.ps.take()
                t = self.mm(bank[0:96, 0:b - a], [(w[:, 96 * i:96 * i + 96], qa[:, i, a:b]) for i in range(2)], tw, tq, rel)
                u = self.acp(q[0:96, a:b], bank[0:96, 0:b - a], t, qk_free[h % 2])
                self.ps.free(ids, u)
                ts.append(u)
            self.ring.free(s, t)
            ts.append(self.turn(q[0:96, 0:512], S["r96"], c96, s96, tmp, ts, 96))
            for a, b in seg2:
                bank, ids, rel = self.ps.take()
                t = self.mm(bank[0:64, 0:b - a], [(wkv[:, 64 * h:64 * h + 64], kva[:, a:b])], rel)
                u = self.acp(k[0:64, a:b], bank[0:64, 0:b - a], t, qk_free[h % 2])
                self.ps.free(ids, u)
                ts.append(u)
            ts.append(self.cp(k[64:96, :], kr[64:96, :], tkr, t0, qk_free[h % 2]))
            return ts

        tp = prepare(0)
        for h in range(8):
            tn = prepare(h + 1) if h < 7 else None
            q, k = qb[h % 2], kb[h % 2]
            p0 = 64 * (h % 2)
            units = []
            vals = [Vm[:, c, 64 * h:64 * h + 64] for c in range(6)]
            for qt in range(6):
                ql = q[0:96, 128 * qt:128 * qt + 128]
                lat = qt < 4
                if lat:
                    segs = [(ql, k[0:96, 0:512], 0, 512), (ql, k[0:96, 512:768], 512, 256)]
                else:
                    segs = [(ql, k[0:96, 512:768], 0, 256)]
                o = tuple(x[h // 2][p0:p0 + 64, slice(0, 512) if lat else slice(512, 768)] for x in (fh, fl))
                units.append(dict(segs=[segs], scale=scale, toks=[tp, tv], vals=vals if lat else vals[4:],
                                  out=(o, p0, 64, 128 * (qt % 4), 512 if lat else 256, (h, lat), qt in (3, 5))))
            self.attend(units, P, PT, st)
            qk_free[h % 2] = self.pe.last()
            tp = tn
        units = []
        for i in range(4):
            for kv in range(2):
                p0 = 64 * kv
                ps = slice(p0, p0 + 64)
                sk = self.row["sink"][:, i + 4 * kv:i + 4 * kv + 1]
                for qt in range(6):
                    ql = qs[ps, i, 128 * qt:128 * qt + 128]
                    segs = [(ql, ks[ps, 512:768], 0, 256)]
                    tiles, masks = [4, 5], []
                    if qt < 4:
                        lo, hi = max(qt - 1, 0), min(qt + 1, 3)
                        segs.append((ql, ks[ps, 128 * lo:128 * lo + 256], 256, 256))
                        if hi - lo == 2:
                            segs.append((ql, ks[ps, 128 * hi:128 * hi + 128], 512, 128))
                        tiles += range(lo, hi + 1)
                        if qt > 0:
                            masks.append((256, "bandlo"))
                        if qt < 3:
                            masks.append((256 + 128 * (hi - lo), "bandhi"))
                    o = tuple(x[4 + i][ps, slice(0, 512) if qt < 4 else slice(512, 768)] for x in (fh, fl))
                    units.append(dict(segs=[segs], scale=0.125, toks=[ts_w], masks=masks, sink=sk,
                                      vals=[Vs[:, c, p0:p0 + 64] for c in tiles],
                                      out=(o, p0, 64, 128 * (qt % 4), 512 if qt < 4 else 256, (i, kv, qt < 4), qt in (3, 5))))
        self.attend(units, P, PT, st)
        self.fence()
        self.rings(4, 4, 2, [(d["about"][k], 1024) for k in range(8)], lambda i: self.pool)
        t = self.residual_norm(X, fx, m, 16, V["ln1g"][:, 0:8], V["ln1b"][:, 0:8], seg2, rstd, sqt)
        t = self.feed(0, X, m, seg2, top, t, V)
        self.fence()
        ar.at = top
        ar.at += -ar.at % 8
        low = ar.at
        fh, fl = [ar.rounded(768) for _ in range(8)], [ar.rounded(768) for _ in range(8)]
        q1, k1 = ar.take(4096), ar.take(6144)
        q, k = v3(q1, 512), v3(k1, 768)
        at_v = ar.at
        Vd1 = ar.take(6144)
        Vd = v3(Vd1, 1024)
        rope = ar.take(1024)
        tmp = ar.take(512)
        srcs = [(d["dqk"][j], 1024) for j in range(16)] + [(d["dv"][j], 1024) for j in range(8)]
        self.rings(4, 4, 2, srcs, lambda i: self.pool)
        ar.at = low
        O = v3(ar.take(4096), 512)
        P, P2 = [ar.take(768) for _ in range(3)], [ar.take(768) for _ in range(2)]
        PT = [ar.take(768) for _ in range(2)]
        at_o = ar.at
        trp = self.load(rope, d["rope"][:, 1024:2048])
        c128, s128 = rope[:, 0:512], rope[:, 512:1024]
        self.lam = lamb[:, 0:1]
        pr = tmp[:, 0:64]
        t = self.floor
        for i, (a, b) in enumerate((("lq1", "lk1"), ("lq2", "lk2"))):
            t = self.tt(pr, self.row[a], self.row[b], ALU.mult, t)
            t = self.red(lamb[:, 2 + i:3 + i], pr, ALU.add, t)
            t = self.ac(lamb[:, 2 + i:3 + i], lamb[:, 2 + i:3 + i], AF.Exp, t)
        t = self.tt(lamb[:, 0:1], lamb[:, 2:3], lamb[:, 3:4], ALU.subtract, t)
        t = self.ts(lamb[:, 0:1], lamb[:, 0:1], LAMBDA_INIT, None, ALU.add, None, t)
        t = self.ts(sub, V["subln"], 1.0 - LAMBDA_INIT, None, ALU.mult, None, t)
        th, _ = self.affine(X, fh, fl, [Vd1[:, 768 * i:768 * i + 768] for i in range(2)], m1, 0, seg2)
        fx = lambda k, a, b: (fh[k][:, a:b], fl[k][:, a:b])
        ts = []
        for j in range(16):
            dst, segs = (q[:, j, :], seg1) if j < 8 else (k[:, j - 8, :], seg2)
            t0 = []
            for (bank, ids, t), (a, b) in zip(self.proj3(fx, segs, th), segs):
                u = self.acp(dst[:, a:b], bank[:, 0:b - a], t)
                self.ps.free(ids, u)
                t0.append(u)
            ts += [t0, self.turn(dst[:, 0:512], S["r128"], c128, s128, tmp, [t0, trp])]
        for hf in range(2):
            banks = [self.ps.take() for _ in range(6)]
            for kq in range(4):
                hi, lo, tw, s = self.stream.next()
                for c, (bank, ids, rel) in enumerate(banks):
                    cs = slice(128 * c, 128 * c + 128)
                    t = self.mm3(bank, [((fh[2 * kq + i][:, cs], fl[2 * kq + i][:, cs]),
                                         tuple(w[:, 512 * i:512 * i + 512] for w in (hi, lo))) for i in range(2)],
                                 tw, rel, start=(kq == 0), stop=(kq == 3))
                    if kq == 3:
                        u = self.acp(Vd[:, c, 512 * hf:512 * hf + 512], bank, t)
                        self.ps.free(ids, u)
                        ts.append(u)
                self.stream.free(s, t)
        units = []
        for h in range(8):
            for qt in range(4):
                sg = []
                for s in range(2):
                    ps = slice(64 * s, 64 * s + 64)
                    ql = q[ps, h, 128 * qt:128 * qt + 128]
                    sg.append([(ql, k[ps, h, 0:512], 0, 512), (ql, k[ps, h, 512:768], 512, 256)])
                units.append(dict(segs=sg, scale=0.125, toks=[ts], vals=[Vd[:, c, 128 * h:128 * h + 128] for c in range(6)],
                                  out=(O[:, h, :], 0, 128, 128 * qt, 512, h, qt == 3)))
        t = self.attend(units, P, PT, st, P2)
        self.fence()
        self.rings(4, 4, 2, [(d["dout"][k], 1024) for k in range(8)], lambda i: self.pool)
        ar.at = at_v
        oh = [ar.rounded(512) for _ in range(8)]
        ol = [ar.rounded(512) for _ in range(4)]
        ar.at = at_o
        ol += [ar.rounded(512) for _ in range(4)]

        def finish(h, r, t):
            t = self.stt(O[:, h, :], O[:, h, :], sub, r, ALU.mult, ALU.mult, t)
            return self.parts(O[:, h, :], oh[h], ol[h], t)[1]

        u = self.norms([[O[:, h, :]] for h in range(8)], k1, q1, S["m128"], EPS, finish)
        t = self.residual_norm(X, lambda k, a, b: (oh[k], ol[k]), m1, 16, V["ln1g"][:, 8:16], V["ln1b"][:, 8:16], seg1, P[0],
                               P[1:3], u)
        t = self.feed(1, X, m1, seg1, top, t, V)
        self.h = X[:, :, 0:512]
        return t




def _tiles(w):
    k, n = w.shape
    return np.ascontiguousarray(w.reshape(k // 128, 128, n // 128, 128).transpose(2, 1, 0, 3).reshape(n // 128, 128, k))


def _cols(v):
    return np.ascontiguousarray(np.asarray(v).reshape(-1, 128).T)


def _fm(x):
    t, f = x.shape
    return np.ascontiguousarray(x.T.reshape(f // 128, 128, t).transpose(1, 0, 2))


def _constants():
    f32 = np.float32
    i = np.arange(128)
    j, l = i[:, None], i[None, :]
    sq = {"ident": j == l, "ones": j >= 0 * l, "le": j <= l, "ge": j >= l, "gt": j > l, "lt": j < l}
    sq = {k: (v + 0 * l).astype(f32) for k, v in sq.items()}
    sq["ones"][:] = 1
    sq["m256"] = np.full((128, 128), 1 / 256, f32)
    sq["m1024"] = np.full((128, 128), 1 / 1024, f32)
    sq["m128"] = np.full((128, 128), 1 / 128, f32)
    sq["m64"] = ((j // 64 == l // 64) / 64).astype(f32)
    sq["iota"] = np.broadcast_to(l, (128, 128)).astype(f32)

    def rot(n, blocks, start):
        r = np.zeros((128, 128), f32)
        q = n // 4
        for b in blocks:
            o = start + b * n
            for k in range(q):
                r[o + q + k, o + k] = -1
                r[o + k, o + q + k] = 1
                r[o + 3 * q + k, o + 2 * q + k] = -1
                r[o + 2 * q + k, o + 3 * q + k] = 1
        return r

    sq["r96"] = rot(32, [0], 64)
    sq["r128"] = rot(64, [0, 1], 0)
    sq["bandlo"] = np.where(l >= j, 0, NEG).astype(f32)
    sq["bandhi"] = np.where(l <= j, 0, NEG).astype(f32)
    out = {"squares": np.concatenate([sq[n] for n in SQ], 1)}
    t = np.arange(512)
    ang = 2 * np.pi * ((t[:, None] * t[None, :]) % 1024) / 1024
    c, s = np.cos(ang), np.sin(ang)
    s[0, :] = 0
    s[:, 0] = 0
    tm = lambda a: np.ascontiguousarray(a.reshape(4, 128, -1).transpose(1, 0, 2)).astype(f32)
    out["dftc"], out["dfts"] = tm(c), tm(s)
    is0 = s[0:128].copy()
    is0[0] = (-1.0) ** t
    out["is0"] = is0.astype(f32)
    ny = np.zeros((512, 128))
    ny[:, 0] = (-1.0) ** t
    out["nyq"] = tm(ny)
    tl = np.linspace(0.0, 1.0, 512).astype(f32)
    wa = (f32(2 * np.pi) * t.astype(f32) / f32(512)).astype(f32)
    bands = np.linspace(1e-4, 15, 16).astype(f32)
    an = (wa[:, None] * bands[None, :]).astype(f32)
    out["zpos"] = np.ascontiguousarray(np.concatenate([tl[:, None], np.cos(an), -np.sin(an)], -1).T).astype(f32)
    dl = np.abs(np.linspace(math.log(1e-2) / 1.5, math.log(1e-2) / 0.3, 1024).astype(f32))
    dec = np.exp(-tl[:, None] * dl[None, :]).astype(f32)
    out["dec"] = np.ascontiguousarray(dec.reshape(2, 2, 128, 2, 512).transpose(3, 0, 2, 1, 4).reshape(2, 2, 128, 1024))

    def rope(dim):
        row = np.repeat(np.arange(8), 64).astype(f32)
        col = np.tile(np.arange(64), 8).astype(f32)
        q = dim // 4
        fr = (f32(10000.0) ** (-np.arange(q, dtype=f32) / f32(q))).astype(f32)
        ar, ac = row[:, None] * fr, col[:, None] * fr
        a = np.concatenate([ar, ar, ac, ac], -1)
        return np.cos(a).T.astype(f32), np.sin(a).T.astype(f32)

    c32, s32 = rope(32)
    c64, s64 = rope(64)
    z = np.zeros((32, 512), f32)
    r96c = np.concatenate([np.ones((64, 512), f32), c32, z])
    r96s = np.concatenate([np.zeros((64, 512), f32), s32, z])
    out["rope"] = np.concatenate([r96c, r96s, np.tile(c64, (2, 1)), np.tile(s64, (2, 1))], 1)
    return {k: np.ascontiguousarray(v, dtype=f32) for k, v in out.items()}


def _arrays(p):
    p = {k: np.asarray(v) for k, v in p.items()}
    a = _constants()
    a["xT"], a["ctxT"], a["ctxT2"] = _fm(p["x"][0]), _fm(p["ctx"][0]), _fm(p["ctx_2"][0])
    a["wmod0"] = p["w_mod"][0][:, :2048].reshape(8, 128, 2048)
    a["wmod"] = np.ascontiguousarray(p["w_mod"][0][:, 2048:].T).reshape(32, 128, 1024)
    a["wmod2"] = np.ascontiguousarray(p["w_mod_2"].transpose(0, 2, 1)).reshape(96, 128, 1024)
    a["crow"] = np.tile(np.stack([p["c"][0], p["c_ctx"], p["c_2"][0], p["c_ctx_2"]])[:, None], (1, 128, 1))
    win = p["w_in"][0]
    a["win"] = _tiles(np.concatenate([win[:, :3072], win[:, 3104:]], 1))
    a["wdt"] = np.ascontiguousarray(win[:, 3072:3104].reshape(8, 128, 32).transpose(1, 0, 2).reshape(128, 256))
    w12 = np.zeros((64, 128), np.float32)
    w12[:33, :64] = p["hy_w1"][0]
    w12[:, 64:] = p["hy_w2"][0]
    a["hyw12"] = w12
    w3 = p["hy_w3"][0].reshape(64, 2, 2, 2, 512)
    a["hyw3"] = np.ascontiguousarray(w3.transpose(1, 3, 0, 2, 4).reshape(2, 2, 64, 1024))
    a["wout"] = np.ascontiguousarray(_tiles(p["w_out"][0]).reshape(8, 128, 2, 1024).transpose(0, 2, 1, 3))
    a["wq"] = _tiles(p["peer_wq"][0])
    a["subkeys"] = np.ascontiguousarray(p["peer_subkeys"][0].transpose(2, 0, 1).reshape(128, 256))
    a["peeru"] = np.ascontiguousarray(p["peer_u"][0].reshape(128, 128, 8, 128).transpose(0, 3, 2, 1).reshape(128, 128, 1024))
    a["peerv"] = np.ascontiguousarray(p["peer_v"][0].reshape(128, 128, 1024))

    def pad(v):
        o = np.zeros((128, 1), np.float32)
        o[:v.size, 0] = v.reshape(-1)
        return o

    def taps(w):
        k, n = w.shape
        return np.ascontiguousarray(w.reshape(k, n // 128, 128).transpose(2, 1, 0).reshape(128, -1))

    c2 = lambda x, y: np.ascontiguousarray(np.stack([_cols(x), _cols(y)], 2).reshape(128, 16))
    v = {"norm1": _cols(p["norm1"]), "convw": taps(p["ssd_conv_w"][0]), "convb": _cols(p["ssd_conv_b"]),
         "ssd_norm": _cols(p["ssd_norm"]), "hyw": taps(p["hy_short_w"][0]), "hyb": _cols(p["hy_short_b"]),
         "hbias": _cols(p["hy_filt_bias"]), "hy_norm": _cols(p["hy_norm"]), "norm2": _cols(p["norm2"]),
         "final_norm": _cols(p["final_norm"]), "bmod": _cols(p["b_mod"]), "dtb": pad(p["ssd_dt_bias"]),
         "hyb1": pad(p["hy_b1"]), "hyb2": pad(p["hy_b2"]), "fr0": pad(p["hy_sin_freq"][0, 0]),
         "fr1": pad(p["hy_sin_freq"][0, 1]), "ln1g": _cols(p["ln1_g_2"]), "ln1b": _cols(p["ln1_b_2"]),
         "ln2g": _cols(p["ln2_g_2"]), "ln2b": _cols(p["ln2_b_2"]),
         "fcw": np.concatenate([taps(p["ffn_conv_w_2"][i]) for i in range(2)], 1), "fcb": _cols(p["ffn_conv_b_2"]),
         "bmod2": _cols(p["b_mod_2"]), "qn": _cols(p["mla_q_norm_2"]), "kvn": _cols(p["mla_kv_norm_2"]),
         "subln": _cols(p["diff_subln_g_2"]), "c1": c2(p["c"], p["c_ctx"])}
    a["vecs"] = np.concatenate([v[n] for n, _ in VECS], 1)
    r = {"alog": p["ssd_a_log"], "dskip": p["ssd_d"], "sink": p["swa_sink_2"], "lq1": p["diff_lam_q1_2"],
         "lk1": p["diff_lam_k1_2"], "lq2": p["diff_lam_q2_2"], "lk2": p["diff_lam_k2_2"],
         "i16": np.arange(16, dtype=np.float32)}
    a["rows"] = np.tile(np.concatenate([r[n].reshape(-1) for n, _ in ROWS])[None], (128, 1))
    w = p["ab_w_in_2"][0]
    qs = w[:, 256:768].reshape(1024, 2, 4, 64).transpose(0, 2, 1, 3).reshape(1024, 512)
    kr = np.concatenate([np.zeros((1024, 64), np.float32), w[:, 896:928], np.zeros((1024, 32), np.float32)], 1)
    a["abin"] = _tiles(np.concatenate([w[:, :256], qs, w[:, 768:896], w[:, 928:1056], kr, w[:, 1056:]], 1))
    wq = p["mla_w_qb_2"][0].reshape(2, 128, 8, 96)
    a["wqb"] = np.ascontiguousarray(wq.transpose(2, 1, 0, 3).reshape(8, 128, 192))
    wk = p["mla_w_kvb_2"][0].reshape(128, 8, 128)
    a["wkvb"] = np.ascontiguousarray(np.concatenate([wk[:, :, :64].reshape(128, 512), wk[:, :, 64:].reshape(128, 512)], 1))
    wo = p["ab_w_out_2"][0]
    wos = wo[512:].reshape(2, 4, 64, 1024).transpose(1, 0, 2, 3).reshape(512, 1024)
    a["about"] = _tiles(np.concatenate([wo[:512], wos], 0))
    w = p["diff_w_in_2"][0]
    a["dqk"] = _tiles(w[:, :2048])
    a["dv"] = w[:, 2048:].reshape(4, 2, 128, 2, 512).transpose(3, 0, 2, 1, 4).reshape(8, 128, 1024)
    a["dout"] = _tiles(p["diff_w_out_2"][0])
    a["wgate"] = np.concatenate([_tiles(p["ffn_w_gate_2"][i]) for i in range(2)])
    a["wup"] = np.concatenate([_tiles(p["ffn_w_up_2"][i]) for i in range(2)])
    a["wdown"] = np.ascontiguousarray(p["ffn_w_down_2"].reshape(2, 22, 128, 1024))
    return {k: np.ascontiguousarray(x, dtype=np.float32) for k, x in a.items()}


def build(nc, d, out, part="all", dump=None):
    with ExitStack() as ctx:
        k = Core(nc, d, ctx)
        k.setup()
        if part != "second":
            k.in_projection()
            k.ssd()
            t = k.hyena()
            t = k.out_projection(t)
            t = k.peer(t)
        if part != "first":
            t = k.second(part == "second")
        so = k.dsem()
        t = k.sp.dma(out, k.h, so, t)
        k.sp.wait(t)
        block = ctx.enter_context(nc.Block())
        for deco, q in ((block.tensor, k.pe), (block.vector, k.dve), (block.scalar, k.act), (block.gpsimd, k.pool),
                        (block.sync, k.sp)):
            deco(lambda e, q=q: q.run(e))


def kernel(**inputs):
    import concourse.bacc as bacc
    from concourse.bass_utils import run_bass_kernel_spmd as run

    nc = bacc.Bacc("TRN2", target_bir_lowering=False, num_devices=1)
    arrays = _arrays(inputs)
    d = {n: nc.dram_tensor(n, a.shape, F, kind="ExternalInput").ap() for n, a in arrays.items()}
    d["gates"] = nc.dram_tensor("gates", (16, 128, 4096), F, kind="Internal").ap()
    out = nc.dram_tensor("out", (128, 8, 512), F, kind="ExternalOutput").ap()
    build(nc, d, out)
    r = run(nc, [arrays], core_ids=[0]).results[0]["out"]
    return np.ascontiguousarray(np.asarray(r).transpose(2, 1, 0).reshape(1, 512, 1024))
```
